# Optimizing a Trainium2 kernel written in Bass

```python
import math
import jax, jax.numpy as jnp
from jax import lax
import numpy as np

D_MODEL = 1024
BATCH = 1
SEQ = 256
DEPTH = 1

MOBA_HEAD_DIM = 64
MOBA_HEADS = (D_MODEL // 2) // MOBA_HEAD_DIM
MOBA_WIDTH = MOBA_HEADS * MOBA_HEAD_DIM
MOBA_BLOCK = 256
MOBA_TOPK = 3
Q_BLOCK = 128
GLA_HEADS = 4
GLA_VAL_DIM = (D_MODEL // 2) // GLA_HEADS
GLA_KEY_DIM = GLA_VAL_DIM // 2
GLA_VWIDTH = GLA_HEADS * GLA_VAL_DIM
GLA_KWIDTH = GLA_HEADS * GLA_KEY_DIM
GLA_GATE_RANK = 16
GLA_GATE_TAU = 16.0
GLA_CHUNK = 64
MIX_WIDTH = MOBA_WIDTH + GLA_VWIDTH
IN_COLS = 3 * MOBA_WIDTH + 2 * GLA_KWIDTH + 2 * GLA_VWIDTH + GLA_GATE_RANK
D_FF = 256 * ((8 * D_MODEL // 3 + 255) // 256)
CONV_WIDTH = 3
ROPE_THETA = 10000.0
EPS = 1e-6


def rms_norm(x, g):
    xf = x.astype(jnp.float32)
    y = xf * lax.rsqrt(jnp.mean(xf * xf, axis=-1, keepdims=True) + EPS)
    return (y * g.astype(jnp.float32)).astype(x.dtype)

def rope(t, pos):
    hd = t.shape[-1]
    inv_freq = 1.0 / (ROPE_THETA ** (jnp.arange(0, hd, 2, dtype=jnp.float32) / hd))
    ang = pos.astype(jnp.float32)[:, None] * inv_freq[None, :]
    cos = jnp.cos(ang).astype(t.dtype)
    sin = jnp.sin(ang).astype(t.dtype)
    t1, t2 = t[..., : hd // 2], t[..., hd // 2:]
    return jnp.concatenate([t1 * cos - t2 * sin, t2 * cos + t1 * sin], axis=-1)

def moba_attention(q, k, v):
    B, H, S, hd = q.shape
    nb = -(-S // MOBA_BLOCK)
    n_sel = min(MOBA_TOPK, nb)
    pad = nb * MOBA_BLOCK - S
    padw = ((0, 0), (0, 0), (0, pad), (0, 0))
    kp = jnp.pad(k, padw).reshape(B, H, nb, MOBA_BLOCK, hd)
    vp = jnp.pad(v, padw).reshape(B, H, nb, MOBA_BLOCK, hd)
    k_mean = jnp.mean(kp, axis=3)
    q = q * (hd ** -0.5)
    n_qb = S // Q_BLOCK
    gather = jax.vmap(jax.vmap(lambda blocks, idx: blocks[idx]))
    block_ids = jnp.arange(nb)

    def one_query_block(c):
        q0 = c * Q_BLOCK
        qc = lax.dynamic_slice_in_dim(q, q0, Q_BLOCK, axis=2)
        own = q0 // MOBA_BLOCK
        qpos = q0 + jnp.arange(Q_BLOCK)
        gate = jnp.einsum('bhqd,bhnd->bhqn', qc, k_mean).astype(jnp.float32)
        gate = jnp.where((block_ids < own)[None, None, None, :], gate, -jnp.inf)
        top_s, top_i = lax.top_k(gate, n_sel)
        valid = top_s > -jnp.inf
        kg = gather(kp, top_i)
        vg = gather(vp, top_i)
        s_sel = jnp.einsum('bhqd,bhqnkd->bhqnk', qc, kg).astype(jnp.float32)
        s_sel = jnp.where(valid[..., None], s_sel, -jnp.inf)
        s_sel = s_sel.reshape(B, H, Q_BLOCK, n_sel * MOBA_BLOCK)
        k_own = lax.dynamic_index_in_dim(kp, own, axis=2, keepdims=False)
        v_own = lax.dynamic_index_in_dim(vp, own, axis=2, keepdims=False)
        kpos = own * MOBA_BLOCK + jnp.arange(MOBA_BLOCK)
        s_own = jnp.einsum('bhqd,bhkd->bhqk', qc, k_own).astype(jnp.float32)
        s_own = jnp.where(qpos[:, None] >= kpos[None, :], s_own, -jnp.inf)
        p = jax.nn.softmax(jnp.concatenate([s_sel, s_own], axis=-1), axis=-1).astype(v.dtype)
        p_sel = p[..., : n_sel * MOBA_BLOCK].reshape(B, H, Q_BLOCK, n_sel, MOBA_BLOCK)
        p_own = p[..., n_sel * MOBA_BLOCK:]
        return (jnp.einsum('bhqnk,bhqnkd->bhqd', p_sel, vg)
                + jnp.einsum('bhqk,bhkd->bhqd', p_own, v_own))

    out = lax.map(one_query_block, jnp.arange(n_qb))
    return out.transpose(1, 2, 0, 3, 4).reshape(B, H, S, hd)

def gla_attention(q, k, v, log_a):
    B, H, S, dk = q.shape
    dv = v.shape[-1]
    C = GLA_CHUNK
    nc = S // C
    f32 = jnp.float32

    def to_chunks(t):
        return t.astype(f32).reshape(B, H, nc, C, t.shape[-1]).transpose(2, 0, 1, 3, 4)

    qc = to_chunks(q * (dk ** -0.5))
    kc, vc = to_chunks(k), to_chunks(v)
    G = jnp.cumsum(to_chunks(log_a), axis=3)
    causal = jnp.tril(jnp.ones((C, C), dtype=bool))

    def step(state, inp):
        q_, k_, v_, G_ = inp
        diff = G_[:, :, :, None, :] - G_[:, :, None, :, :]
        decay = jnp.exp(jnp.where(causal[None, None, :, :, None], diff, -jnp.inf))
        A = jnp.einsum('bhtd,bhsd,bhtsd->bhts', q_, k_, decay)
        o = (jnp.einsum('bhts,bhsv->bhtv', A, v_)
             + jnp.einsum('bhtd,bhdv->bhtv', q_ * jnp.exp(G_), state))
        G_last = G_[:, :, -1:, :]
        state = (jnp.exp(G_last)[:, :, 0, :, None] * state
                 + jnp.einsum('bhsd,bhsv->bhdv', k_ * jnp.exp(G_last - G_), v_))
        return state, o

    state0 = jnp.zeros((B, H, dk, dv), f32)
    _, o = lax.scan(step, state0, (qc, kc, vc, G))
    return o.transpose(1, 2, 0, 3, 4).reshape(B, H, S, dv)

def causal_dwconv(h, w, b):
    S = h.shape[1]
    hp = jnp.pad(h, ((0, 0), (CONV_WIDTH - 1, 0), (0, 0)))
    return sum(w[j] * hp[:, j:j + S] for j in range(CONV_WIDTH)) + b

def split_heads(t, n_heads):
    B, S, W = t.shape
    return t.reshape(B, S, n_heads, W // n_heads).transpose(0, 2, 1, 3)

def merge_heads(t):
    B, H, S, d = t.shape
    return t.transpose(0, 2, 1, 3).reshape(B, S, H * d)

def first_inputs(seed: int = 0) -> dict:
    key = jax.random.key(seed)
    ks = jax.random.split(key, 16)
    f32 = jnp.float32
    D, L = D_MODEL, DEPTH
    nrm = lambda k, shape, fan: jax.random.normal(k, shape, f32) * (fan ** -0.5)
    return {
        "x": jax.random.normal(ks[0], (BATCH, SEQ, D), f32),
        "attn_norm_g": 1.0 + 0.02 * jax.random.normal(ks[1], (L, D), f32),
        "w_in": nrm(ks[2], (L, D, IN_COLS), D),
        "w_gate_up": nrm(ks[3], (L, GLA_GATE_RANK, GLA_KWIDTH), GLA_GATE_RANK),
        "b_gate": 0.1 * jax.random.normal(ks[4], (L, GLA_KWIDTH), f32),
        "gla_norm_g": 1.0 + 0.02 * jax.random.normal(ks[5], (L, GLA_HEADS, GLA_VAL_DIM), f32),
        "w_out": nrm(ks[6], (L, MIX_WIDTH, D), MIX_WIDTH),
        "ffn_norm_g": 1.0 + 0.02 * jax.random.normal(ks[7], (L, D), f32),
        "w_ffn_up": nrm(ks[8], (L, D, 2 * D_FF), D),
        "conv_w": nrm(ks[9], (L, CONV_WIDTH, 2 * D_FF), CONV_WIDTH),
        "conv_b": 0.02 * jax.random.normal(ks[10], (L, 2 * D_FF), f32),
        "w_ffn_down": nrm(ks[11], (L, D_FF, D), D_FF),
        "final_norm_g": 1.0 + 0.02 * jax.random.normal(ks[12], (D,), f32),
    }

def first_block(x, attn_norm_g, w_in, w_gate_up, b_gate, gla_norm_g, w_out,
              ffn_norm_g, w_ffn_up, conv_w, conv_b, w_ffn_down, final_norm_g):
    B, S, _ = x.shape
    pos = jnp.arange(S)
    o_mq = 0
    o_mk = o_mq + MOBA_WIDTH
    o_mv = o_mk + MOBA_WIDTH
    o_gq = o_mv + MOBA_WIDTH
    o_gk = o_gq + GLA_KWIDTH
    o_gv = o_gk + GLA_KWIDTH
    o_gr = o_gv + GLA_VWIDTH
    o_gg = o_gr + GLA_VWIDTH
    for l in range(DEPTH):
        xn = rms_norm(x, attn_norm_g[l])
        proj = xn @ w_in[l]
        mq = rope(split_heads(proj[..., o_mq:o_mk], MOBA_HEADS), pos)
        mk = rope(split_heads(proj[..., o_mk:o_mv], MOBA_HEADS), pos)
        mv = split_heads(proj[..., o_mv:o_gq], MOBA_HEADS)
        y_moba = merge_heads(moba_attention(mq, mk, mv))
        gq = split_heads(proj[..., o_gq:o_gk], GLA_HEADS)
        gk = split_heads(proj[..., o_gk:o_gv], GLA_HEADS)
        gv = split_heads(proj[..., o_gv:o_gr], GLA_HEADS)
        gr = proj[..., o_gr:o_gg]
        gate_lr = proj[..., o_gg:]
        log_a = jax.nn.log_sigmoid((gate_lr @ w_gate_up[l] + b_gate[l]).astype(jnp.float32)) / GLA_GATE_TAU
        og = gla_attention(gq, gk, gv, split_heads(log_a, GLA_HEADS))
        og = og * lax.rsqrt(jnp.mean(og * og, axis=-1, keepdims=True) + EPS)
        og = og * gla_norm_g[l].astype(jnp.float32)[None, :, None, :]
        y_gla = merge_heads(og).astype(x.dtype) * jax.nn.silu(gr)
        x = x + jnp.concatenate([y_moba, y_gla], axis=-1) @ w_out[l]
        hn = rms_norm(x, ffn_norm_g[l])
        h = causal_dwconv(hn @ w_ffn_up[l], conv_w[l], conv_b[l])
        h_gate, h_val = h[..., :D_FF], h[..., D_FF:]
        x = x + (jax.nn.silu(h_gate) * h_val) @ w_ffn_down[l]
    return rms_norm(x, final_norm_g)


CHUNK = 64
D_FF_2 = 2816
FFN_RES_WEIGHT = 0.5
ADA_SUBLAYERS = 3
ADA_WIDTH = ADA_SUBLAYERS * 3 * D_MODEL
MLA_HEADS = 8
MLA_Q_RANK = 256
MLA_KV_RANK = 128
MLA_NOPE = 64
MLA_ROPE = 32
MLA_V = 64
CA_HEADS = 8
CA_HEAD_DIM = 64
CA_LEFT_CHUNKS = 8
CA_BAND = CA_LEFT_CHUNKS + 1
MAX_REL_DIST = 256
CA_WIDTH = CA_HEADS * CA_HEAD_DIM
MLA_OUT_WIDTH = MLA_HEADS * MLA_V
W_IN_COLS = MLA_Q_RANK + MLA_KV_RANK + MLA_ROPE + 3 * CA_WIDTH + 2 * D_MODEL
NEG_INF = -1e30


def rmsnorm(x, g):
    xf = x.astype(jnp.float32)
    y = xf * lax.rsqrt(jnp.mean(xf * xf, axis=-1, keepdims=True) + EPS)
    return (y * g.astype(jnp.float32)).astype(x.dtype)

def modulate(h, shift, scale):
    return h * (1 + scale[:, None, :]) + shift[:, None, :]

def swiglu(h, w_in, w_out):
    gu = h @ w_in
    g, u = jnp.split(gu, 2, axis=-1)
    return (jax.nn.silu(g) * u) @ w_out

def rope_2(x, cos, sin):
    half = x.shape[-1] // 2
    x1, x2 = x[..., :half], x[..., half:]
    return jnp.concatenate([x1 * cos - x2 * sin, x1 * sin + x2 * cos], axis=-1).astype(x.dtype)

def mla_attention(q_lat, kv_lat, k_pe_raw, positions, q_norm, w_uq, kv_norm, w_ukv):
    B, S = q_lat.shape[:2]
    cq = rmsnorm(q_lat, q_norm)
    q = (cq @ w_uq).reshape(B, S, MLA_HEADS, MLA_NOPE + MLA_ROPE)
    q_nope, q_pe = q[..., :MLA_NOPE], q[..., MLA_NOPE:]
    ckv = rmsnorm(kv_lat, kv_norm)
    kv = (ckv @ w_ukv).reshape(B, S, MLA_HEADS, MLA_NOPE + MLA_V)
    k_nope, v = kv[..., :MLA_NOPE], kv[..., MLA_NOPE:]

    inv_freq = ROPE_THETA ** (-jnp.arange(0, MLA_ROPE, 2, dtype=jnp.float32) / MLA_ROPE)
    ang = positions.astype(jnp.float32)[..., None] * inv_freq
    cos, sin = jnp.cos(ang), jnp.sin(ang)
    q_pe = rope_2(q_pe, cos[:, :, None, :], sin[:, :, None, :])
    k_pe = rope_2(k_pe_raw, cos, sin)

    scale = (MLA_NOPE + MLA_ROPE) ** -0.5
    key_chunk = jnp.arange(S) // CHUNK

    def block(qi):
        start = qi * Q_BLOCK
        qn = lax.dynamic_slice_in_dim(q_nope, start, Q_BLOCK, axis=1)
        qp = lax.dynamic_slice_in_dim(q_pe, start, Q_BLOCK, axis=1)
        s = (jnp.einsum('bqhd,bkhd->bhqk', qn, k_nope)
             + jnp.einsum('bqhd,bkd->bhqk', qp, k_pe)).astype(jnp.float32) * scale
        q_chunk = (start + jnp.arange(Q_BLOCK)) // CHUNK
        mask = key_chunk[None, :] <= q_chunk[:, None]
        s = jnp.where(mask[None, None], s, NEG_INF)
        p = jax.nn.softmax(s, axis=-1).astype(v.dtype)
        return jnp.einsum('bhqk,bkhd->bqhd', p, v)

    o = lax.map(block, jnp.arange(S // Q_BLOCK))
    return jnp.moveaxis(o, 0, 1).reshape(B, S, MLA_OUT_WIDTH)

def chunk_attention(q, k, v, rel_bias):
    B, S = q.shape[:2]
    NC = S // CHUNK
    KB = CA_BAND * CHUNK
    q = q.reshape(B, NC, CHUNK, CA_HEADS, CA_HEAD_DIM)
    pad = ((0, 0), (CA_LEFT_CHUNKS, 0), (0, 0), (0, 0), (0, 0))
    kpad = jnp.pad(k.reshape(B, NC, CHUNK, CA_HEADS, CA_HEAD_DIM), pad)
    vpad = jnp.pad(v.reshape(B, NC, CHUNK, CA_HEADS, CA_HEAD_DIM), pad)
    idx = jnp.arange(NC)[:, None] + jnp.arange(CA_BAND)[None, :]
    kb = kpad[:, idx].reshape(B, NC, KB, CA_HEADS, CA_HEAD_DIM)
    vb = vpad[:, idx].reshape(B, NC, KB, CA_HEADS, CA_HEAD_DIM)

    s = jnp.einsum('bnqhd,bnkhd->bnhqk', q, kb).astype(jnp.float32) * CA_HEAD_DIM ** -0.5
    rel = CA_LEFT_CHUNKS * CHUNK + jnp.arange(CHUNK)[:, None] - jnp.arange(KB)[None, :]
    rel = jnp.clip(rel, -MAX_REL_DIST, MAX_REL_DIST) + MAX_REL_DIST
    bias = jnp.transpose(rel_bias[rel], (2, 0, 1)).astype(jnp.float32)
    s = s + bias[None, None]
    key_chunk = jnp.arange(NC)[:, None] - CA_LEFT_CHUNKS + jnp.arange(KB)[None, :] // CHUNK
    valid = key_chunk >= 0
    s = jnp.where(valid[None, :, None, None, :], s, NEG_INF)
    p = jax.nn.softmax(s, axis=-1).astype(vb.dtype)
    o = jnp.einsum('bnhqk,bnkhd->bnqhd', p, vb)
    return o.reshape(B, S, CA_WIDTH)

def second_inputs(seed: int = 0) -> dict:
    key = jax.random.key(seed)
    ks = jax.random.split(key, 24)
    L, D = DEPTH, D_MODEL

    def w(k, shape, fan_in, mult=1.0):
        return jax.random.normal(k, shape, jnp.float32) * (mult * fan_in ** -0.5)

    def gain(k, shape):
        return 1.0 + 0.1 * jax.random.normal(k, shape, jnp.float32)

    offsets = jax.random.randint(ks[2], (BATCH, 1), 0, 64, dtype=jnp.int32) * CHUNK
    positions = offsets + jnp.arange(SEQ, dtype=jnp.int32)[None, :]
    return {
        "x": jax.random.normal(ks[0], (BATCH, SEQ, D), jnp.float32),
        "c": jax.random.normal(ks[1], (BATCH, D), jnp.float32),
        "positions": positions,
        "w_ada": w(ks[3], (L, D, ADA_WIDTH), D),
        "b_ada": 0.1 * jax.random.normal(ks[4], (L, ADA_WIDTH), jnp.float32),
        "ffn1_norm": gain(ks[5], (L, D)),
        "ffn1_w_in": w(ks[6], (L, D, 2 * D_FF_2), D),
        "ffn1_w_out": w(ks[7], (L, D_FF_2, D), D_FF_2),
        "mix_norm": gain(ks[8], (L, D)),
        "w_in": w(ks[9], (L, D, W_IN_COLS), D),
        "mla_q_norm": gain(ks[10], (L, MLA_Q_RANK)),
        "mla_w_uq": w(ks[11], (L, MLA_Q_RANK, MLA_HEADS * (MLA_NOPE + MLA_ROPE)), MLA_Q_RANK),
        "mla_kv_norm": gain(ks[12], (L, MLA_KV_RANK)),
        "mla_w_ukv": w(ks[13], (L, MLA_KV_RANK, MLA_HEADS * (MLA_NOPE + MLA_V)), MLA_KV_RANK),
        "rel_bias": 0.5 * jax.random.normal(ks[14], (L, 2 * MAX_REL_DIST + 1, CA_HEADS), jnp.float32),
        "w_branch_a": w(ks[15], (L, MLA_OUT_WIDTH, D), MLA_OUT_WIDTH),
        "w_branch_b": w(ks[16], (L, CA_WIDTH, D), CA_WIDTH),
        "w_out": w(ks[17], (L, D, D), D),
        "ffn2_norm": gain(ks[18], (L, D)),
        "ffn2_w_in": w(ks[19], (L, D, 2 * D_FF_2), D),
        "ffn2_w_out": w(ks[20], (L, D_FF_2, D), D_FF_2),
        "final_norm": gain(ks[21], (D,)),
    }

def second_block(x, c, positions, w_ada, b_ada, ffn1_norm, ffn1_w_in, ffn1_w_out,
              mix_norm, w_in, mla_q_norm, mla_w_uq, mla_kv_norm, mla_w_ukv, rel_bias,
              w_branch_a, w_branch_b, w_out, ffn2_norm, ffn2_w_in, ffn2_w_out, final_norm):
    c_act = jax.nn.silu(c)
    splits = []
    acc = 0
    for width in (MLA_Q_RANK, MLA_KV_RANK, MLA_ROPE, CA_WIDTH, CA_WIDTH, CA_WIDTH, D_MODEL):
        acc += width
        splits.append(acc)

    for l in range(DEPTH):
        ada = c_act @ w_ada[l] + b_ada[l]
        (sh1, sc1, g1, sh2, sc2, g2, sh3, sc3, g3) = jnp.split(ada, 3 * ADA_SUBLAYERS, axis=-1)

        h = modulate(rmsnorm(x, ffn1_norm[l]), sh1, sc1)
        x = x + FFN_RES_WEIGHT * g1[:, None, :] * swiglu(h, ffn1_w_in[l], ffn1_w_out[l])

        h = modulate(rmsnorm(x, mix_norm[l]), sh2, sc2)
        z = h @ w_in[l]
        q_lat, kv_lat, k_pe_raw, ca_q, ca_k, ca_v, gate_a, gate_b = jnp.split(z, splits, axis=-1)
        y_a = mla_attention(q_lat, kv_lat, k_pe_raw, positions, mla_q_norm[l], mla_w_uq[l],
                            mla_kv_norm[l], mla_w_ukv[l]) @ w_branch_a[l]
        B, S = ca_q.shape[:2]
        shp = (B, S, CA_HEADS, CA_HEAD_DIM)
        y_b = chunk_attention(ca_q.reshape(shp), ca_k.reshape(shp), ca_v.reshape(shp),
                              rel_bias[l]) @ w_branch_b[l]
        merged = jax.nn.sigmoid(gate_a) * y_a + jax.nn.sigmoid(gate_b) * y_b
        x = x + g2[:, None, :] * (merged @ w_out[l])

        h = modulate(rmsnorm(x, ffn2_norm[l]), sh3, sc3)
        x = x + FFN_RES_WEIGHT * g3[:, None, :] * swiglu(h, ffn2_w_in[l], ffn2_w_out[l])

    return rmsnorm(x, final_norm)


def setup_inputs(seed=0):
    out = dict(first_inputs(seed))
    for name, value in second_inputs(seed + 1).items():
        if name != "x":
            out[name + "_2"] = value
    return out


def reference(
    x, attn_norm_g, w_in, w_gate_up, b_gate, gla_norm_g, w_out, ffn_norm_g, w_ffn_up, conv_w,
    conv_b, w_ffn_down, final_norm_g, c_2, positions_2, w_ada_2, b_ada_2, ffn1_norm_2,
    ffn1_w_in_2, ffn1_w_out_2, mix_norm_2, w_in_2, mla_q_norm_2, mla_w_uq_2, mla_kv_norm_2,
    mla_w_ukv_2, rel_bias_2, w_branch_a_2, w_branch_b_2, w_out_2, ffn2_norm_2, ffn2_w_in_2,
    ffn2_w_out_2, final_norm_2,
):
    x = first_block(
        x, attn_norm_g, w_in, w_gate_up, b_gate, gla_norm_g, w_out, ffn_norm_g, w_ffn_up,
        conv_w, conv_b, w_ffn_down, final_norm_g,
    )
    return second_block(
        x, c_2, positions_2, w_ada_2, b_ada_2, ffn1_norm_2, ffn1_w_in_2, ffn1_w_out_2,
        mix_norm_2, w_in_2, mla_q_norm_2, mla_w_uq_2, mla_kv_norm_2, mla_w_ukv_2, rel_bias_2,
        w_branch_a_2, w_branch_b_2, w_out_2, ffn2_norm_2, ffn2_w_in_2, ffn2_w_out_2,
        final_norm_2,
    )


_drawn_inputs = setup_inputs


def setup_inputs(seed=0):
    import zlib

    import numpy as np

    out = dict(_drawn_inputs(seed))
    spreads = {}
    factors = {'attn_norm_g': 2.708,
     'b_gate': 3.076,
     'gla_norm_g': 6.217,
     'ffn_norm_g': 3.948,
     'conv_b': 3.994,
     'final_norm_g': 2.769,
     'mla_q_norm_2': 8.0,
     'mla_kv_norm_2': 3.218,
     'rel_bias_2': 4.312,
     'ffn2_norm_2': 3.782}
    for name, (base, spread) in spreads.items():
        noise = np.random.default_rng([zlib.crc32(name.encode()), seed]).standard_normal(out[name].shape)
        drawn = base * np.exp(spread * noise) if base else spread * noise
        out[name] = __import__('jax').numpy.asarray(drawn.astype(out[name].dtype))
    for name, factor in factors.items():
        out[name] = (out[name] * factor).astype(out[name].dtype)
    return out
```

```python
from contextlib import ExitStack

import numpy as np

import concourse.bass as bass
from concourse import mybir

P = 128
D = 1024
S = 256
KC = D // P
DFF = 2816
FT = DFF // P
HALF = 1024
NSLOT = 4
EPS = 1e-6
NEG = -1e30
LEVELS = 7
ADA_Q = 12

C_IN1 = 0
C_OUT1 = C_IN1 + 12
C_UP = [C_OUT1 + 4, 0, 0]
C_DN = [C_UP[0] + FT, 0, 0]
C_UP[1] = C_DN[0] + FT // 2
C_DN[1] = C_UP[1] + FT
C_IN2 = C_DN[1] + FT // 2
C_UQ = C_IN2 + 6
C_UV = C_IN2 + 7
C_CAV = C_IN2 + 8
C_GATE = C_IN2 + 10
C_BR = C_IN2 + 18
C_OUT2 = C_BR + 4
C_UP[2] = C_OUT2 + 4
C_DN[2] = C_UP[2] + FT
NCHUNK = C_DN[2] + FT // 2
NHALF = 2 * NCHUNK

COL = {}
_n = 0
for _name, _w in [("attn_g", 8), ("ffn_g", 8), ("fin1_g", 8), ("gla_g", 4), ("b_gate", 2), ("conv_w", 132),
                  ("conv_b", 44), ("f1_g", 8), ("mix_g", 8), ("f2_g", 8), ("fin2_g", 8), ("q_g", 2),
                  ("kv_g", 1), ("c", 8), ("b_ada", 72), ("freq", 1)]:
    COL[_name] = _n
    _n += _w
NCOL = _n

TAB = {}
_n = 0
for _name, _w in [("cos", S), ("sin", S), ("perm64", P), ("perm32", P), ("causal", S), ("chunked", S)]:
    TAB[_name] = _n
    _n += _w
NTAB = _n


def build(nc, w, ada_w, x_in, cols_in, tab_in, gmask_in, glr_in, gup_in, bias_in, pos_in, out):
    F32 = mybir.dt.float32
    F32R = mybir.dt.float32r
    I32 = mybir.dt.int32
    ALU = mybir.AluOpType
    ACT = mybir.ActivationFunctionType
    AX = mybir.AxisListType
    ds = bass.ds

    with ExitStack() as ctx:
        sb = lambda name, shape, dt=F32: ctx.enter_context(nc.sbuf_tensor(name, shape, dt))
        sem = lambda name: ctx.enter_context(nc.semaphore(name))

        raw = sb("raw", [P, NSLOT, HALF])
        w_hi = sb("w_hi", [P, NSLOT, HALF], F32R)
        w_lo = sb("w_lo", [P, NSLOT, HALF], F32R)
        X = sb("X", [P, KC, S])
        xn = sb("xn", [P, KC, S])
        xh = sb("xh", [P, KC, S], F32R)
        xl = sb("xl", [P, KC, S], F32R)
        sd = sb("sd", [P, S])
        rstd = sb("rstd", [P, S])
        cols = sb("cols", [P, NCOL])
        tab = sb("tab", [P, NTAB])
        ones = sb("ones", [P, P])
        ident = sb("ident", [P, P])
        epsc = sb("epsc", [P, 1])
        cact = sb("cact", [P, KC])
        mod = sb("mod", [P, 3, 24])
        modA = sb("modA", [P, 3, KC])
        ada_raw = sb("ada_raw", [P, 2, HALF])
        cos2 = sb("cos2", [P, S])
        sin2 = sb("sin2", [P, S])

        def phase(names, early=()):
            made = {}

            def place(tensors):
                guards = [nc.sbuf_tensor(n, s, d) for n, s, d in tensors]
                for (n, _, _), g in zip(tensors, guards):
                    made[n] = g.__enter__()
                return reversed(guards)

            kept = place(names[:-1])
            for g in place(early):
                g.__exit__(None, None, None)
            for g in place(names[-1:]):
                g.__exit__(None, None, None)
            for g in kept:
                g.__exit__(None, None, None)
            return made

        ffn = phase([("act_hi", [P, FT, S], F32R), ("act_lo", [P, FT, S], F32R), ("cv", [P, 2, 2, S], F32),
                     ("sg", [P, 2, S], F32), ("av", [P, 2, S], F32), ("acc", [P, 2 * ADA_Q * 256], F32)])
        act_hi, act_lo, cv, sg, av, acc = ffn.values()
        b1 = phase([("qT", [P, 4, S], F32), ("kz", [P, 2, 4, S], F32), ("mv", [P, 2, 512], F32),
                    ("gv", [P, 2, 512], F32), ("gq", [P, 2, S], F32), ("gkz", [P, 2, 2, S], F32),
                    ("gr", [P, 4, S], F32), ("G", [P, 2, S], F32), ("E", [P, 2, 2, S], F32),
                    ("QL", [P, 2, 2, S], F32), ("KL", [P, 2, 2, 2, S], F32), ("AT0", [P, 4, S], F32),
                    ("AT1", [P, 4, P], F32), ("og", [P, 4, S], F32), ("qraw", [P, 2, 2 * S], F32),
                    ("rt", [P, 2, 2 * S], F32), ("glr", [P, S], F32), ("w_glr", [P, 128], F32),
                    ("w_gup", [P, S], F32), ("gmask", [P, 8, P], I32), ("g_sd", [P, 4, S], F32),
                    ("yh1", [P, 8, S], F32R), ("yl1", [P, 8, S], F32R), ("sm1", [P, 2, 768], F32),
                    ("pt1", [P, 2, 768], F32), ("st1", [P, 2, 3, 4], F32), ("trig", [P, 2, S], F32),
                    ("posi", [P, S], I32), ("ones_row", [P, 2], F32)])
        b2 = phase([("qn", [P, 4, S], F32), ("qpe", [P, 2, S], F32), ("nz", [P, 2, 4, S], F32),
                    ("kpz", [P, 4, S], F32), ("v2", [P, 2, 512], F32), ("caq", [P, 4, S], F32),
                    ("caz", [P, 2, 4, S], F32), ("cav", [P, 2, 512], F32), ("l_sd", [P, 2, S], F32), ("kpr", [P, S], F32), ("qpr", [P, 2 * S], F32),
                    ("rt2", [P, 2 * S], F32), ("yh2", [P, 8, S], F32R), ("yl2", [P, 8, S], F32R),
                    ("sm2", [P, 2, 768], F32), ("pt2", [P, 2, 768], F32), ("st2", [P, 2, 3, 4], F32),
                    ("bm", [P, 8, S], F32), ("th", [P, 16, S], F32)],
                   early=[("lat", [P, 3, S], F32), ("latsq", [P, 3, S], F32), ("cqh", [P, 3, S], F32R), ("cql", [P, 3, S], F32R)])

        ps = ctx.enter_context(nc.psum_tensor("ps", [P, 8, 512], F32))

        x_landed, cols_landed, tab_landed, aux_landed, bias_landed = map(sem, ("x_landed", "cols_landed", "tab_landed", "aux_landed", "bias_landed"))
        pos_landed, gmask_landed = sem("pos_landed"), sem("gmask_landed")
        raw_landed = [sem(f"raw_landed{i}") for i in range(NSLOT)]
        ada_landed = [sem(f"ada_landed{i}") for i in range(2)]
        hi_ready, lo_ready, half_used = sem("hi_ready"), sem("lo_ready"), sem("half_used")
        bank_free = [sem("bank0_free"), sem("bank1_free")]
        consts_ready, pool_zero = sem("consts_ready"), sem("pool_zero")
        resid_done, sq_done, ss_done, sd_done, rstd_done = map(sem, ("resid_done", "sq_done", "ss_done", "sd_done", "rstd_done"))
        xt_ready, xh_ready, xl_ready = map(sem, ("xt_ready", "xh_ready", "xl_ready"))
        own_act, own_dve, own_pool = sem("own_act"), sem("own_dve"), sem("own_pool")
        cv_base, cv_gate, cv_own, sg_done, av_done, ah_done, act_ready, down_full = map(
            sem, ("cv_base", "cv_gate", "cv_own", "sg_done", "av_done", "ah_done", "act_ready", "down_full"))
        ada_own, ada_used, ada_cols, mod_ready = map(sem, ("ada_own", "ada_used", "ada_cols", "mod_ready"))
        trig_red, trig_done = sem("trig_red"), sem("trig_done")
        glr_done, glr_sb, gup_done, z_done, ls_done = map(sem, ("glr_done", "glr_sb", "gup_done", "z_done", "ls_done"))
        rot_done, rope_done = map(sem, ("rot_done", "rope_done"))
        lv_d, lv_e, lv_q, lv_k, lv_full, lv_copied = map(sem, ("lv_d", "lv_e", "lv_q", "lv_k", "lv_full", "lv_copied"))
        go_full, go_sq, go_ss, go_sd, gr_silu, go_v, yg_hi, yg_ready = map(
            sem, ("go_full", "go_sq", "go_ss", "go_sd", "gr_silu", "go_v", "yg_hi", "yg_ready"))
        at_s, at_m, at_e, at_n, at_t, at_p0, at_p1, at_o, at_yh, at_y = map(
            sem, ("at_s", "at_m", "at_e", "at_n", "at_t", "at_p0", "at_p1", "at_o", "at_yh", "at_y"))
        lat_ready, lat_sq, lat_ss, lat_sd, lat_v, lat_hi, lat_ready2, uq_full = map(
            sem, ("lat_ready", "lat_sq", "lat_ss", "lat_sd", "lat_v", "lat_hi", "lat_ready2", "uq_full"))
        pe_rot, pe_done, br_done, mh_ready, ml_ready, bm_ready = map(
            sem, ("pe_rot", "pe_done", "br_done", "mh_ready", "ml_ready", "bm_ready"))
        out_written = sem("out_written")

        block = ctx.enter_context(nc.Block())

        def table(name, n):
            return tab[:, TAB[name]:TAB[name] + n]

        def col(name, j=0):
            return cols[:, COL[name] + j:COL[name] + j + 1]

        def over(ap, n):
            return ap.unsqueeze(1).to_broadcast([ap.shape[0], n, ap.shape[1]])

        def slot(h):
            return h % NSLOT

        def pair(a, p):
            return a[:, 2 * p:2 * p + 2, :]

        class Own:
            def __init__(self, eng, s):
                self.eng, self.s, self.n = eng, s, 0

            def mark(self, ins):
                ins.then_inc(self.s, 1)
                self.n += 1

            def wait(self):
                self.eng.wait_ge(self.s, self.n)

        def bank_use(c):
            u = c - sum(FT // 2 for f in range(3) if c > C_DN[f])
            if c <= C_UQ:
                return u
            if c == C_UV:
                return u + 4
            return u + 5 + max(0, min(c, C_OUT2) - C_BR)

        def evacuated(eng, u):
            eng.wait_ge(bank_free[u % 2], u // 2 + 1)

        @block.sync
        def _(sp):
            def load(h, k):
                sp.dma_start(raw[:, k, :], w[h, :, :] if isinstance(h, int) else w[ds(h, 1), :, :].rearrange("a p n -> (a p) n")).then_inc(raw_landed[k], 16)

            for k in range(NSLOT):
                load(k, k)
            with sp.Fori(1, NHALF // NSLOT) as i:
                for k in range(NSLOT):
                    sp.wait_ge(lo_ready, i * NSLOT + (k - NSLOT + 1))
                    load(i * NSLOT + k, k)
            for h in range(NHALF // NSLOT * NSLOT, NHALF):
                sp.wait_ge(lo_ready, h - NSLOT + 1)
                load(h, slot(h))
            for p in range(4):
                sp.wait_ge(resid_done, 17 + p)
                sp.dma_start(out[:, 2 * p:2 * p + 2, :], pair(X, p)).then_inc(out_written, 16)
            sp.wait_ge(out_written, 64)

        @block.gpsimd
        def _(pool):
            own = Own(pool, own_pool)
            pool.memset(ones[:, :], 1.0)
            pool.memset(epsc[:, :], EPS)
            own.mark(pool.memset(ident[:, :], 0.0))
            own.wait()
            pool.affine_select(out=ident[:, :], in_=ident[:, :], compare_op=ALU.not_equal, fill=1.0, base=0,
                               pattern=[[-1, P]], channel_multiplier=1).then_inc(consts_ready, 1)
            pool.memset(b1["glr"][:, :], 0.0).then_inc(pool_zero, 1)
            pool.memset(b1["gkz"][:, :, :, :], 0.0).then_inc(pool_zero, 1)
            pool.memset(b1["kz"][:, :, :, :], 0.0).then_inc(pool_zero, 1)
            pool.memset(b1["AT0"][:, :, :], 0.0).then_inc(pool_zero, 1)
            pool.memset(b1["AT1"][:, :, :], 0.0).then_inc(pool_zero, 1)

            def load_ada(j, k):
                pool.dma_start(ada_raw[:, k, :], ada_w[j, :, :] if isinstance(j, int) else ada_w[ds(j, 1), :, :].rearrange("a p n -> (a p) n")).then_inc(ada_landed[k], 16)

            for k in range(2):
                load_ada(k, k)
            for l in range(LEVELS + 1):
                pool.wait_ge(lv_e, l + 1)
                if l == 0:
                    evacuated(pool, 1)
                if l >= 2:
                    pool.wait_ge(lv_full, 2 * (l - 1))
                for par in range(2):
                    ins = pool.tensor_tensor(b1["KL"][:, l % 2, par, :, :], b1["gkz"][:, par, :, :], b1["E"][:, l % 2, :, :], ALU.mult)
                ins.then_inc(lv_k, 1)
            nq1 = ADA_Q
            with pool.Fori(1, nq1) as q:
                for k in range(2):
                    pool.wait_ge(ada_used, q * 2 + (k - 1))
                    load_ada(q * 2 + k, k)
            with pool.Fori(nq1, 3 * ADA_Q) as q:
                for k in range(2):
                    pool.wait_ge(ada_used, q * 2 + (k - 1))
                    load_ada(q * 2 + k, k)
            pool.wait_ge(ada_cols, 2)
            pool.wait_ge(down_full, 6)
            pool.wait_ge(half_used, 2 * C_IN2)
            pool.dma_start(b2["bm"][:, :, :], bias_in).then_inc(bias_landed, 16)
            pool.memset(b2["nz"][:, :, :, :], 0.0).then_inc(pool_zero, 1)
            pool.memset(b2["kpz"][:, :, :], 0.0).then_inc(pool_zero, 1)
            pool.memset(b2["caz"][:, :, :, :], 0.0).then_inc(pool_zero, 1)
            pool.wait_ge(bias_landed, 16)
            for h in range(8):
                ins = pool.tensor_tensor(b2["bm"][:, h, :], b2["bm"][:, h, :], table("chunked", S), ALU.add)
            ins.then_inc(bm_ready, 1)

        @block.tensor
        def _(pe):
            def three(o, lh, ll, rh, rl, start, stop):
                pe.matmul(o, lh, rh, start=start, stop=False, skip_group_check=True)
                pe.matmul(o, lh, rl, start=False, stop=False, skip_group_check=True)
                return pe.matmul(o, ll, rh, start=False, stop=stop, skip_group_check=True)

            def chunk(c, act=None, i=0, x_wait=None, tokens_out=False):
                ah, al = act or (xh, xl)
                u = bank_use(c)
                b = u % 2
                if not (isinstance(i, int) and u + 2 * i < 2):
                    pe.wait_ge(bank_free[b], u // 2 + i)
                for half in range(2):
                    h = 2 * c + half
                    pe.wait_ge(lo_ready, h + 1 + 4 * i)
                    for k in range(4):
                        kc = 4 * half + k
                        if x_wait is not None and kc % 2 == 0:
                            s, n = x_wait
                            pe.wait_ge(s, n + kc // 2 + 1)
                        for f in range(2):
                            first = half == 0 and k == 0
                            last = half == 1 and k == 3
                            if tokens_out:
                                a = slice(f * P, f * P + P)
                                wcol = slice(k * 256, k * 256 + 256)
                                o = ps[:, b, f * 256:f * 256 + 256]
                                pe.matmul(o, ah[:, kc, a], w_hi[:, slot(h), wcol], start=first and f == 0, stop=False, skip_group_check=True)
                                pe.matmul(o, al[:, kc, a], w_hi[:, slot(h), wcol], start=False, stop=False, skip_group_check=True)
                                m = pe.matmul(o, ah[:, kc, a], w_lo[:, slot(h), wcol], start=False, stop=last, skip_group_check=True)
                            else:
                                wc = slice(k * 256 + f * P, k * 256 + f * P + P)
                                m = three(ps[:, b, f * 256:f * 256 + 256], w_hi[:, slot(h), wc], w_lo[:, slot(h), wc],
                                          ah[:, kc, :], al[:, kc, :], first and f == 0, last)
                    m.then_inc(half_used, 1)

            def norm(n):
                if n == 0:
                    pe.wait_ge(consts_ready, 1)
                for k in range(KC):
                    if k % 2 == 0:
                        pe.wait_ge(sq_done, 4 * n + k // 2 + 1)
                    m = pe.matmul(ps[:, 2, 0:S], ones[:, :], xn[:, k, :], start=k == 0, stop=k == KC - 1)
                m.then_inc(ss_done, 1)

            def att_s(g, q, kz, pe_q=None, pe_k=None):
                a = 4 + 2 * (g % 2)
                if g >= 2:
                    pe.wait_ge(at_y, g - 1)
                t4 = g % 4
                for hh in range(2):
                    h = 2 * t4 + hh
                    for (o, qs, n) in ((ps[:, a, hh * P:hh * P + P], 0, P), (ps[:, a + 1, hh * S:hh * S + S], P, S)):
                        m = pe.matmul(o, q[:, t4, qs:qs + P], kz[:, hh, t4, 0:n], start=True, stop=pe_q is None)
                        if pe_q is not None:
                            m = pe.matmul(o, pe_q[:, h // 4, qs:qs + P], pe_k[:, h % 4, 0:n], start=False, stop=True)
                m.then_inc(at_s, 1)

            def att_t(g, sm):
                a = 4 + 2 * (g % 2)
                r = sm[:, g % 2, :]
                pe.wait_ge(at_n, g + 1)
                for hh in range(2):
                    pe.transpose(ps[:, a + 1, hh * S:hh * S + P], r[:, hh * P:hh * P + P], ident[:, :])
                    pe.transpose(ps[:, a + 1, hh * S + P:hh * S + S], r[:, 256 + hh * S:256 + hh * S + P], ident[:, :])
                    m = pe.transpose(ps[:, a, hh * P:hh * P + P], r[:, 256 + hh * S + P:256 + hh * S + S], ident[:, :])
                m.then_inc(at_t, 1)

            def att_o(g, pt, v):
                a = 4 + 2 * (g % 2)
                pe.wait_ge(at_p0, g + 1)
                pe.wait_ge(at_p1, g + 1)
                for hh in range(2):
                    h = 2 * (g % 4) + hh
                    o = slice(64 * hh, 64 * hh + 64)
                    pe.matmul(ps[o, a, 256:512], v[:, 0, h * 64:h * 64 + 64], pt[:, g % 2, hh * S:hh * S + S],
                              start=True, stop=False, skip_group_check=True)
                    m = pe.matmul(ps[o, a, 384:512], v[:, 1, h * 64:h * 64 + 64], pt[:, g % 2, 512 + hh * P:512 + hh * P + P],
                                  start=False, stop=True, skip_group_check=True)
                m.then_inc(at_o, 1)

            def rot(c):
                evacuated(pe, c)
                if c >= 3:
                    pe.wait_ge(rope_done, c - 2)
                pe.matmul(ps[:, 2, :], table("perm64", P), b1["qraw"][:, c % 2, :], start=True, stop=True).then_inc(rot_done, 1)

            def level(l):
                if l <= LEVELS:
                    pe.wait_ge(lv_q, l + 1)
                    pe.wait_ge(lv_k, l + 1)
                K = (lambda par, ht, a: b1["KL"][:, l % 2, par, ht, a]) if l <= LEVELS else (lambda par, ht, a: b1["gkz"][:, par, ht, a])
                Q = (lambda ht, a: b1["QL"][:, l % 2, ht, a]) if l <= LEVELS else (lambda ht, a: b1["gq"][:, ht, a])
                lo_, hi_ = slice(0, P), slice(P, S)
                for i, (ks, qs) in enumerate([(lo_, hi_)] if l == LEVELS else [(lo_, lo_), (hi_, hi_)]):
                    n = (2 * l + i if l < LEVELS else 2 * LEVELS + (0 if l == LEVELS else 1 + i))
                    bank = 2 + i
                    before = {0: n - 2, 1: n - 2}[i] if l <= LEVELS else (15 - 1 if i == 0 else 13)
                    if before >= 0:
                        pe.wait_ge(lv_copied, before + 1)
                    for h in range(4):
                        m = pe.matmul(ps[:, bank, h * P:h * P + P], K(h % 2, h // 2, ks), Q(h // 2, qs), start=True, stop=True)
                    m.then_inc(lv_full, 1)

            def ffn_up(f, c0, x_wait):
                chunk(c0, x_wait=x_wait)
                chunk(c0 + 1)
                with pe.Fori(0, FT // 2 - 1) as i:
                    for v in range(2):
                        chunk(c0 + 2 + v, i=i)

            def down_half(k, h, kk, start=False, i=0):
                pe.wait_ge(lo_ready, h + 1 + 4 * i)
                for ft in range(KC):
                    wc = slice(ft * P, ft * P + P)
                    m = three(ps[:, 4 + ft // 2, (ft % 2) * S:(ft % 2) * S + S], w_hi[:, slot(h), wc], w_lo[:, slot(h), wc],
                              act_hi[:, kk, :], act_lo[:, kk, :], start and ft % 2 == 0, False)
                m.then_inc(half_used, 1)

            def ffn_down(f, c0):
                h0 = 2 * c0
                pe.wait_ge(act_ready, FT * f + FT - 4)
                down_half(0, h0, 0, start=True)
                down_half(1, h0 + 1, 1)
                pe.wait_ge(act_ready, FT * f + FT)
                with pe.Fori(0, 4) as i:
                    for k in range(4):
                        pe.wait_ge(lo_ready, h0 + 2 + k + 1 + 4 * i)
                        h = h0 + 2 + k
                        for ft in range(KC):
                            wc = slice(ft * P, ft * P + P)
                            o = ps[:, 4 + ft // 2, (ft % 2) * S:(ft % 2) * S + S]
                            rh = act_hi[:, ds(i * 4 + (2 + k), 1), :].rearrange("p a n -> p (a n)")
                            rl = act_lo[:, ds(i * 4 + (2 + k), 1), :].rearrange("p a n -> p (a n)")
                            m = three(o, w_hi[:, slot(h), wc], w_lo[:, slot(h), wc], rh, rl, False, False)
                        m.then_inc(half_used, 1)
                down_half(18, h0 + 18, 18)
                down_half(19, h0 + 19, 19)
                pe.wait_ge(lo_ready, h0 + 22)
                for ft in range(KC):
                    wc = slice(ft * P, ft * P + P)
                    for k in (20, 21):
                        h = h0 + k
                        m = three(ps[:, 4 + ft // 2, (ft % 2) * S:(ft % 2) * S + S], w_hi[:, slot(h), wc], w_lo[:, slot(h), wc],
                                  act_hi[:, k, :], act_lo[:, k, :], False, k == 21)
                    if ft in (1, 3, 5):
                        m.then_inc(down_full, 1)
                m.then_inc(half_used, 2)

            def ada_columns(n, blocks):
                pe.wait_ge(ada_used, 2 * blocks)
                for j in range(n):
                    m = pe.matmul(ps[:, 3, j:j + 1], acc[:, j * P:j * P + P], ones[:, 0:1], start=j == 0, stop=True, skip_group_check=True)
                m.then_inc(ada_cols, 1)

            norm(0)
            pe.wait_ge(aux_landed, 32)
            for kc in range(KC):
                if kc % 2 == 0:
                    pe.wait_ge(xt_ready, kc // 2 + 1)
                m = pe.matmul(ps[0:16, 3, 0:S], b1["w_glr"][:, kc * 16:kc * 16 + 16], xn[:, kc, :], start=kc == 0, stop=kc == KC - 1)
            m.then_inc(glr_done, 1)
            chunk(0, x_wait=(xl_ready, 0))
            chunk(1)
            pe.wait_ge(glr_sb, 1)
            for ht in range(2):
                m = pe.matmul(ps[:, 3, ht * S:ht * S + S], b1["w_gup"][:, ht * P:ht * P + P], b1["glr"][:, :], start=ht == 0, stop=True, skip_group_check=True)
            m.then_inc(gup_done, 1)
            chunk(2)
            chunk(3)
            pe.wait_ge(tab_landed, 16)
            rot(2)
            chunk(4)
            rot(3)
            chunk(5)
            rot(4)
            chunk(6, tokens_out=True)
            rot(5)
            chunk(7, tokens_out=True)
            pe.wait_ge(rope_done, 4)
            att_s(0, b1["qT"], b1["kz"])
            att_s(1, b1["qT"], b1["kz"])
            pe.wait_ge(z_done, 1)
            level(0)
            chunk(8, tokens_out=True)
            level(1)
            att_t(0, b1["sm1"])
            evacuated(pe, 7)
            level(2)
            chunk(9, tokens_out=True)
            att_o(0, b1["pt1"], b1["mv"])
            level(3)
            att_t(1, b1["sm1"])
            att_s(2, b1["qT"], b1["kz"])
            chunk(10)
            att_o(1, b1["pt1"], b1["mv"])
            level(4)
            att_s(3, b1["qT"], b1["kz"])
            att_t(2, b1["sm1"])
            chunk(11)
            level(5)
            att_o(2, b1["pt1"], b1["mv"])
            att_t(3, b1["sm1"])
            level(6)
            att_o(3, b1["pt1"], b1["mv"])
            level(7)
            level(8)
            pe.wait_ge(lv_copied, 17)
            evacuated(pe, 9)
            for h in range(4):
                o = ps[:, 2 + h // 2, (h % 2) * S:(h % 2) * S + S]
                pe.matmul(o, b1["gv"][:, 0, h * P:h * P + P], b1["AT0"][:, h, :], start=h % 2 == 0, stop=False, skip_group_check=True)
                m = pe.matmul(ps[:, 2 + h // 2, (h % 2) * S + P:(h % 2) * S + S], b1["gv"][:, 1, h * P:h * P + P], b1["AT1"][:, h, :],
                              start=False, stop=True, skip_group_check=True)
                if h % 2:
                    m.then_inc(go_full, 1)
            for j in range(2):
                pe.wait_ge(go_sq, j + 1)
                pe.matmul(ps[:, 2 + j, :], ones[:, :], b1["g_sd"][:, 2 * j:2 * j + 2, :].rearrange("p a n -> p (a n)"), start=True, stop=True).then_inc(go_ss, 1)
            pe.wait_ge(at_y, 4)
            pe.wait_ge(yg_ready, 2)
            for c in range(4):
                chunk(C_OUT1 + c, act=(b1["yh1"], b1["yl1"]))
            norm(1)
            ffn_up(0, C_UP[0], (xl_ready, 4))
            ffn_down(0, C_DN[0])
            norm(2)
            ada_columns(24, ADA_Q)
            norm(3)
            ffn_up(1, C_UP[1], (xl_ready, 8))
            ffn_down(1, C_DN[1])
            ada_columns(48, 3 * ADA_Q)
            norm(4)
            chunk(C_IN2, x_wait=(xl_ready, 12))
            chunk(C_IN2 + 1)
            chunk(C_IN2 + 2)
            pe.wait_ge(lat_sq, 1)
            for j in range(3):
                m = pe.matmul(ps[:, 2, (j // 2) * S:(j // 2) * S + S], ones[:, :], b2["latsq"][:, j, :],
                              start=j == 0, stop=j >= 1, skip_group_check=True)
            m.then_inc(lat_ss, 1)
            chunk(C_IN2 + 3)
            evacuated(pe, bank_use(C_IN2 + 1))
            pe.matmul(ps[:, 3, 0:S], table("perm32", P), b2["kpr"][:, :], start=True, stop=True).then_inc(pe_rot, 1)
            chunk(C_IN2 + 4)
            chunk(C_IN2 + 5)
            h = 2 * C_UQ
            pe.wait_ge(lat_ready2, 1)
            pe.wait_ge(lo_ready, h + 2)
            for j in range(5):
                u = bank_use(C_UQ) + j
                pe.wait_ge(bank_free[u % 2], u // 2)
                for f in range(2):
                    o = ps[:, u % 2, f * S:f * S + S]
                    if j < 3:
                        wc = slice((2 * j + f) * P, (2 * j + f) * P + P)
                        three(o, w_hi[:, slot(h), wc], w_lo[:, slot(h), wc], b2["cqh"][:, 0, :], b2["cql"][:, 0, :], f == 0, False)
                        m = three(o, w_hi[:, slot(h + 1), wc], w_lo[:, slot(h + 1), wc], b2["cqh"][:, 1, :], b2["cql"][:, 1, :], False, True)
                    else:
                        s_ = slot(h + j - 3)
                        wc = slice(768 + f * P, 768 + f * P + P)
                        m = three(o, w_hi[:, s_, wc], w_lo[:, s_, wc], b2["cqh"][:, 2, :], b2["cql"][:, 2, :], f == 0, True)
                m.then_inc(*((uq_full, 1) if j < 4 else (half_used, 2)))
            pe.wait_ge(lo_ready, h + 3)
            u = bank_use(C_UV)
            for j in range(2):
                pe.wait_ge(bank_free[(u + j) % 2], (u + j) // 2)
                a = slice(j * P, j * P + P)
                o = ps[:, (u + j) % 2, :]
                s_ = slot(h + 2)
                pe.matmul(o, b2["cqh"][:, 2, a], w_hi[:, s_, 0:512], start=True, stop=False)
                pe.matmul(o, b2["cql"][:, 2, a], w_hi[:, s_, 0:512], start=False, stop=False)
                m = pe.matmul(o, b2["cqh"][:, 2, a], w_lo[:, s_, 0:512], start=False, stop=True)
                m.then_inc(*((uq_full, 1) if j < 1 else (half_used, 2)))
            chunk(C_CAV, tokens_out=True)
            evacuated(pe, bank_use(C_UQ) + 2)
            pe.wait_ge(pe_done, 1)
            pe.matmul(ps[:, 3, :], table("perm32", P), b2["qpr"][:, :], start=True, stop=True).then_inc(pe_rot, 1)
            chunk(C_CAV + 1, tokens_out=True)
            pe.wait_ge(pe_done, 2)
            evacuated(pe, bank_use(C_UQ) + 3)
            evacuated(pe, bank_use(C_UQ) + 4)

            def mla_s(g):
                att_s(g, b2["qn"], b2["nz"], b2["qpe"], b2["kpz"])

            def ca_s(g):
                att_s(g, b2["caq"], b2["caz"])

            def s2(g):
                (mla_s if g < 8 else ca_s)(g)

            def o2(g):
                att_o(g, b2["pt2"], b2["v2"] if g < 8 else b2["cav"])

            s2(4)
            s2(5)
            evacuated(pe, bank_use(C_CAV))
            evacuated(pe, bank_use(C_CAV + 1))
            for c in range(8):
                chunk(C_GATE + c)
                g = 4 + c
                att_t(g, b2["sm2"])
                o2(g)
                if g + 2 < 12:
                    s2(g + 2)
            for br in range(2):
                for cc in range(2):
                    c = C_BR + 2 * br + cc
                    if cc == 0:
                        pe.wait_ge(at_y, 8 + 4 * br)
                    u = bank_use(c)
                    for f2 in range(2):
                        pe.wait_ge(bank_free[(u + f2) % 2], (u + f2) // 2)
                    for half in range(2):
                        h = 2 * c + half
                        pe.wait_ge(lo_ready, h + 1)
                        for k in range(2):
                            for f in range(4):
                                wc = slice(k * 512 + f * P, k * 512 + f * P + P)
                                kk = 4 * br + 2 * half + k
                                m = three(ps[:, (u + f // 2) % 2, (f % 2) * S:(f % 2) * S + S], w_hi[:, slot(h), wc], w_lo[:, slot(h), wc],
                                          b2["yh2"][:, kk, :], b2["yl2"][:, kk, :], half == 0 and k == 0 and f % 2 == 0, half == 1 and k == 1)
                        m.then_inc(half_used, 1)
            chunk(C_OUT2, x_wait=(ml_ready, 0))
            for c in range(1, 4):
                chunk(C_OUT2 + c)
            norm(5)
            ffn_up(2, C_UP[2], (xl_ready, 16))
            ffn_down(2, C_DN[2])
            norm(6)

        @block.scalar
        def _(act):
            own = Own(act, own_act)
            f = nc.scalar.activation

            act.dma_start(cols[:, :], cols_in).then_inc(cols_landed, 16)
            act.dma_start(b1["posi"][:, :], pos_in.to_broadcast([P, S])).then_inc(pos_landed, 16)
            act.dma_start(X[:, :, :], x_in).then_inc(x_landed, 16)
            act.dma_start(b1["w_glr"][:, :], glr_in).then_inc(aux_landed, 16)
            act.dma_start(b1["w_gup"][:, :], gup_in).then_inc(aux_landed, 16)
            act.dma_start(tab[:, :], tab_in).then_inc(tab_landed, 16)
            act.dma_start(b1["gmask"][:, :, :], gmask_in).then_inc(gmask_landed, 16)

            def hi(c, i=0):
                for half in range(2):
                    h = 2 * c + half
                    act.wait_ge(raw_landed[slot(h)], (i + (h // NSLOT + 1)) * 16)
                    if not (isinstance(i, int) and h + 4 * i < NSLOT):
                        act.wait_ge(half_used, h - NSLOT + 1 + 4 * i)
                    f(w_hi[:, slot(h), :], raw[:, slot(h), :], ACT.Copy).then_inc(hi_ready, 1)

            def norm_sums(n, resid=None, c_out=None):
                for p in range(4):
                    if n == 0:
                        act.wait_ge(x_landed, 16)
                    elif c_out is not None:
                        evacuated(act, bank_use(c_out + p))
                    else:
                        act.wait_ge(resid_done, resid + p + 1)
                    f(pair(xn, p), pair(X, p), ACT.Square).then_inc(sq_done, 1)
                act.wait_ge(ss_done, n + 1)
                if n == 0:
                    act.wait_ge(consts_ready, 1)
                f(sd[:, :], ps[:, 2, 0:S], ACT.Sqrt, scale=1.0 / D, bias=epsc[:, 0:1]).then_inc(sd_done, 1)

            def norm_hi(m):
                for p in range(4):
                    act.wait_ge(xt_ready, 4 * m + p + 1)
                    f(pair(xh, p), pair(xn, p), ACT.Copy).then_inc(xh_ready, 1)

            def norm_mod_hi(m, sub):
                act.wait_ge(mod_ready, 1 if sub == 0 else 2)
                for p in range(4):
                    act.wait_ge(xt_ready, 4 * m + p + 1)
                    for k in (2 * p, 2 * p + 1):
                        ins = f(xn[:, k, :], xn[:, k, :], ACT.Identity, scale=modA[:, sub, k:k + 1], bias=mod[:, sub, k:k + 1])
                    own.mark(ins)
                    own.wait()
                    f(pair(xh, p), pair(xn, p), ACT.Copy).then_inc(xh_ready, 1)

            def full(c):
                act.wait_ge(half_used, 2 * c + 2)
                return bank_use(c) % 2

            def bank2(b):
                return ps[:, b, :].rearrange("p (a n) -> p a n", a=2)

            def trig():
                act.wait_ge(trig_red, 1)
                f(sin2[:, :], b1["trig"][:, 0, :], ACT.Sin)
                f(cos2[:, :], b1["trig"][:, 1, :], ACT.Sin).then_inc(trig_done, 1)

            def att_exp(g, sm, st):
                act.wait_ge(at_m, g + 1)
                r = sm[:, g % 2, :]
                for j in range(4):
                    a = slice(j * P, j * P + P) if j < 2 else slice(256 + (j - 2) * S, 256 + (j - 2) * S + S)
                    ins = f(r[:, a], r[:, a], ACT.Exp, bias=st[:, g % 2, 0, j:j + 1], accum_out=st[:, g % 2, 1, j:j + 1])
                ins.then_inc(at_e, 1)

            def att_pt(g, pt):
                act.wait_ge(at_t, g + 1)
                f(pt[:, g % 2, 0:512], ps[:, 5 + 2 * (g % 2), :], ACT.Copy).then_inc(at_p0, 1)

            def att_yh(g, yh, k):
                act.wait_ge(at_o, g + 1)
                f(yh[:, k, :], ps[:, 4 + 2 * (g % 2), 256:512], ACT.Copy).then_inc(at_yh, 1)

            def padded(dst, k, b):
                f(dst[0:64, 0, k:k + 2, :], bank2(b)[0:64, :, :], ACT.Copy)
                return f(dst[64:P, 1, k:k + 2, :], bank2(b)[64:P, :, :], ACT.Copy)

            def level_e(l):
                act.wait_ge(lv_d, l + 1)
                own.mark(f(b1["E"][:, l % 2, :, :], b1["E"][:, l % 2, :, :], ACT.Abs))
                own.wait()
                f(b1["E"][:, l % 2, :, :], b1["E"][:, l % 2, :, :], ACT.Exp, scale=-1.0 / 16).then_inc(lv_e, 1)

            def ffn_up_evac(conv, fi, c, j, i=0):
                u = bank_use(c)
                b = u % 2
                v = j % 2
                act.wait_ge(half_used, 2 * c + 2 + 4 * i)
                n = FT * fi + j + 1 + 2 * i
                if conv:
                    if j >= 2:
                        act.wait_ge(act_ready, n - 2)
                    for t2 in range(2):
                        jj = j + FT * t2
                        wcol = cols[:, ds(i * 2 + (COL["conv_w"] + 2 * 44 + jj), 1)]
                        bcol = cols[:, ds(i * 2 + (COL["conv_b"] + jj), 1)]
                        ins = f(cv[:, v, t2, :], ps[:, b, t2 * S:t2 * S + S], ACT.Identity, scale=wcol, bias=bcol)
                    ins.then_inc(cv_base, 1)
                    act.wait_ge(cv_gate, n)
                    f(sg[:, v, :], cv[:, v, 0, :], ACT.Silu).then_inc(sg_done, 1)
                else:
                    f(sg[:, v, :], ps[:, b, 0:S], ACT.Silu).then_inc(sg_done, 1)

            def ffn_up(fi, c0):
                conv = fi == 0
                hi(c0 + 1)
                ffn_up_evac(conv, fi, c0, 0)
                hi(c0 + 2)
                ffn_up_evac(conv, fi, c0 + 1, 1)
                with act.Fori(0, FT // 2 - 1) as i:
                    for v in range(2):
                        hi(c0 + 3 + v, i=i)
                        ffn_up_evac(conv, fi, c0 + 2 + v, 2 + v, i=i)

            def ffn_down(c0, last=False):
                hi(c0 + 1)
                with act.Fori(0, 4) as i:
                    for v in range(2):
                        hi(c0 + 2 + v, i=i)
                hi(c0 + 10)
                if not last:
                    hi(c0 + 11)

            hi(0)
            norm_sums(0)
            trig()
            norm_hi(0)
            act.wait_ge(glr_done, 1)
            act.wait_ge(pool_zero, 1)
            f(b1["glr"][0:16, :], ps[0:16, 3, 0:S], ACT.Copy).then_inc(glr_sb, 1)
            hi(1)
            f(b1["gq"][:, :, :], bank2(full(0)), ACT.Copy, scale=0.125).then_inc(bank_free[0], 1)
            hi(2)
            act.wait_ge(pool_zero, 2)
            padded(b1["gkz"], 0, full(1)).then_inc(bank_free[1], 1)
            act.wait_ge(cols_landed, 16)
            act.wait_ge(gup_done, 1)
            for ht in range(2):
                ins = f(b1["QL"][:, 0, ht, :], ps[:, 3, ht * S:ht * S + S], ACT.Identity, bias=col("b_gate", ht))
            ins.then_inc(z_done, 1)
            act.wait_ge(z_done, 1)
            own.mark(f(b1["KL"][:, 0, 0, :, :], b1["QL"][:, 0, :, :], ACT.Abs))
            own.wait()
            own.mark(f(b1["KL"][:, 0, 0, :, :], b1["KL"][:, 0, 0, :, :], ACT.Exp, scale=-1.0))
            own.wait()
            f(b1["KL"][:, 0, 1, :, :], b1["KL"][:, 0, 0, :, :], ACT.Ln, bias=1.0).then_inc(ls_done, 1)

            def qraw(c):
                b = full(c)
                if c >= 4:
                    act.wait_ge(rope_done, c - 3)
                f(b1["qraw"][:, c % 2, :], ps[:, b, :], ACT.Copy).then_inc(bank_free[b], 1)

            def vals(dst, c, cc):
                b = full(c)
                f(dst[:, :, cc * 256:cc * 256 + 256], bank2(b), ACT.Copy).then_inc(bank_free[b], 1)

            def gr_evac(c, cc):
                b = full(c)
                f(b1["gr"][:, 2 * cc:2 * cc + 2, :], bank2(b), ACT.Copy).then_inc(bank_free[b], 1)

            sm1, st1, pt1, yh1 = b1["sm1"], b1["st1"], b1["pt1"], b1["yh1"]
            hi(3)
            qraw(2)
            hi(4)
            qraw(3)
            hi(5)
            level_e(0)
            qraw(4)
            hi(6)
            level_e(1)
            qraw(5)
            hi(7)
            vals(b1["mv"], 6, 0)
            level_e(2)
            hi(8)
            vals(b1["mv"], 7, 1)
            att_exp(0, sm1, st1)
            att_exp(1, sm1, st1)
            hi(9)
            level_e(3)
            vals(b1["gv"], 8, 0)
            att_pt(0, pt1)
            hi(10)
            vals(b1["gv"], 9, 1)
            level_e(4)
            hi(11)
            att_yh(0, yh1, 0)
            att_pt(1, pt1)
            att_exp(2, sm1, st1)
            level_e(5)
            gr_evac(10, 0)
            hi(12)
            att_yh(1, yh1, 1)
            att_exp(3, sm1, st1)
            att_pt(2, pt1)
            level_e(6)
            gr_evac(11, 1)
            att_yh(2, yh1, 2)
            att_pt(3, pt1)
            level_e(7)
            att_yh(3, yh1, 3)
            for j in range(2):
                act.wait_ge(go_full, j + 1)
                f(b1["og"][:, 2 * j:2 * j + 2, :], bank2(2 + j), ACT.Copy)
                f(b1["g_sd"][:, 2 * j:2 * j + 2, :], bank2(2 + j), ACT.Square).then_inc(go_sq, 1)
            for j in range(2):
                act.wait_ge(go_ss, j + 1)
                f(b1["g_sd"][:, 2 * j:2 * j + 2, :], bank2(2 + j), ACT.Sqrt, scale=1.0 / P, bias=epsc[:, 0:1]).then_inc(go_sd, 1)
            act.wait_ge(bank_free[1], 6)
            f(b1["gr"][:, :, :], b1["gr"][:, :, :], ACT.Silu)
            act.wait_ge(cols_landed, 16)
            f(cact[:, :], cols[:, COL["c"]:COL["c"] + KC], ACT.Silu).then_inc(gr_silu, 1)
            for j in range(2):
                act.wait_ge(go_v, j + 1)
                f(b1["yh1"][:, 4 + 2 * j:6 + 2 * j, :], b1["og"][:, 2 * j:2 * j + 2, :], ACT.Copy).then_inc(yg_hi, 1)
            for c in range(4):
                hi(C_OUT1 + c + 1)
            norm_sums(1, c_out=C_OUT1)
            norm_hi(1)
            ffn_up(0, C_UP[0])
            ffn_down(C_DN[0])
            norm_sums(2, resid=0)
            norm_sums(3, resid=4)
            norm_mod_hi(2, 0)
            ffn_up(1, C_UP[1])
            ffn_down(C_DN[1])
            norm_sums(4, resid=8)
            norm_mod_hi(3, 1)
            act.wait_ge(ada_cols, 2)
            hi(C_IN2 + 1)
            b = full(C_IN2)
            f(b2["lat"][:, 0:2, :], bank2(b), ACT.Copy)
            f(b2["latsq"][:, 0:2, :], bank2(b), ACT.Square).then_inc(bank_free[b], 1)
            hi(C_IN2 + 2)
            b = full(C_IN2 + 1)
            f(b2["lat"][:, 2, :], ps[:, b, 0:S], ACT.Copy)
            f(b2["latsq"][:, 2, :], ps[:, b, 0:S], ACT.Square).then_inc(lat_sq, 1)
            f(b2["kpr"][:, :], ps[:, b, S:2 * S], ACT.Copy).then_inc(bank_free[b], 1)
            hi(C_IN2 + 3)
            b = full(C_IN2 + 2)
            f(b2["caq"][:, 0:2, :], bank2(b), ACT.Copy).then_inc(bank_free[b], 1)
            act.wait_ge(lat_ss, 1)
            f(b2["l_sd"][:, 0, :], ps[:, 2, 0:S], ACT.Sqrt, scale=1.0 / 256, bias=epsc[:, 0:1])
            f(b2["l_sd"][:, 1, :], ps[:, 2, S:2 * S], ACT.Sqrt, scale=1.0 / 128, bias=epsc[:, 0:1]).then_inc(lat_sd, 1)
            hi(C_IN2 + 4)
            b = full(C_IN2 + 3)
            f(b2["caq"][:, 2:4, :], bank2(b), ACT.Copy).then_inc(bank_free[b], 1)
            act.wait_ge(lat_v, 1)
            f(b2["cqh"][:, :, :], b2["lat"][:, :, :], ACT.Copy).then_inc(lat_hi, 1)
            act.wait_ge(pool_zero, 8)
            for j in range(2):
                hi(C_IN2 + 5 + j)
                b = full(C_IN2 + 4 + j)
                padded(b2["caz"], 2 * j, b).then_inc(bank_free[b], 1)
            hi(C_UV)
            u0 = bank_use(C_UQ)
            for j in range(5):
                b = (u0 + j) % 2
                if j < 4:
                    act.wait_ge(uq_full, j + 1)
                else:
                    full(C_UQ)
                if j < 2:
                    f(b2["qn"][:, 2 * j:2 * j + 2, :], bank2(b), ACT.Copy).then_inc(bank_free[b], 1)
                elif j == 2:
                    f(b2["qpr"][:, :], ps[:, b, :], ACT.Copy).then_inc(bank_free[b], 1)
                else:
                    padded(b2["nz"], 2 * (j - 3), b).then_inc(bank_free[b], 1)
            hi(C_CAV)
            u0 = bank_use(C_UV)
            for j in range(2):
                b = (u0 + j) % 2
                if j == 0:
                    act.wait_ge(uq_full, 5)
                else:
                    full(C_UV)
                f(b2["v2"][:, j, :], ps[:, b, :], ACT.Copy).then_inc(bank_free[b], 1)
            for j in range(2):
                hi(C_CAV + 1 + j)
                vals(b2["cav"], C_CAV + j, j)
            for c in range(8):
                hi(C_GATE + c + 1)
                g = 4 + c
                att_exp(g, b2["sm2"], b2["st2"])
                b = full(C_GATE + c)
                f(b2["th"][:, 2 * c:2 * c + 2, :], bank2(b), ACT.Tanh, scale=0.5).then_inc(bank_free[b], 1)
                att_pt(g, b2["pt2"])
                att_yh(g, b2["yh2"], c)
            for c in range(4):
                hi(C_BR + c + 1)
            for p in range(4):
                act.wait_ge(br_done, p + 1)
                f(pair(xh, p), pair(xn, p), ACT.Copy).then_inc(mh_ready, 1)
            for c in range(4):
                hi(C_OUT2 + c + 1)
            norm_sums(5, c_out=C_OUT2)
            norm_mod_hi(4, 2)
            ffn_up(2, C_UP[2])
            ffn_down(C_DN[2], last=True)
            norm_sums(6, resid=12)

        @block.vector
        def _(dve):
            own = Own(dve, own_dve)
            v = nc.vector

            def lo(c, i=0):
                for half in range(2):
                    h = 2 * c + half
                    dve.wait_ge(hi_ready, h + 1 + 4 * i)
                    v.tensor_tensor(w_lo[:, slot(h), :], raw[:, slot(h), :], w_hi[:, slot(h), :].bitcast(F32), ALU.subtract).then_inc(lo_ready, 1)

            def rstd_of(n):
                dve.wait_ge(sd_done, n + 1)
                v.reciprocal(rstd[:, :], sd[:, :]).then_inc(rstd_done, 1)
                dve.wait_ge(rstd_done, n + 1)

            def norm_plain(n, m, gain):
                rstd_of(n)
                if n == 0:
                    dve.wait_ge(cols_landed, 16)
                for p in range(4):
                    for k in (2 * p, 2 * p + 1):
                        ins = v.scalar_tensor_tensor(out=xn[:, k, :], in0=X[:, k, :], scalar=col(gain, k), in1=rstd[:, :], op0=ALU.mult, op1=ALU.mult)
                    ins.then_inc(xt_ready, 1)
                norm_lo(m)

            def norm_lo(m):
                for p in range(4):
                    dve.wait_ge(xh_ready, 4 * m + p + 1)
                    v.tensor_tensor(pair(xl, p), pair(xn, p), pair(xh, p).bitcast(F32), ALU.subtract).then_inc(xl_ready, 1)

            def norm_in_place(n, gain):
                rstd_of(n)
                for p in range(4):
                    for k in (2 * p, 2 * p + 1):
                        ins = v.scalar_tensor_tensor(out=X[:, k, :], in0=X[:, k, :], scalar=col(gain, k), in1=rstd[:, :], op0=ALU.mult, op1=ALU.mult)
                    ins.then_inc(resid_done, 1)

            def norm_mod(n, m):
                rstd_of(n)
                for p in range(4):
                    v.tensor_tensor(pair(xn, p), pair(X, p), over(rstd[:, :], 2), ALU.mult).then_inc(xt_ready, 1)
                norm_lo(m)

            def full(c):
                dve.wait_ge(half_used, 2 * c + 2)
                return bank_use(c) % 2

            def add_out(c0, gate=None):
                for c in range(4):
                    lo(c0 + c + 1)
                    b = full(c0 + c)
                    ins = add_pair(b, c) if gate is None else gated_pair(b, c, gate)
                    ins.then_inc(bank_free[b], 1)

            def add_pair(b, p):
                return v.tensor_tensor(pair(X, p), ps[:, b, :].rearrange("p (a n) -> p a n", a=2), pair(X, p), ALU.add)

            def gated_pair(b, p, gate):
                for k in (2 * p, 2 * p + 1):
                    ins = v.scalar_tensor_tensor(out=X[:, k, :], in0=ps[:, b, (k % 2) * S:(k % 2) * S + S], scalar=mod[:, gate, 16 + k:17 + k],
                                                 in1=X[:, k, :], op0=ALU.mult, op1=ALU.add)
                return ins

            def rope_trig():
                tr, pos = b1["trig"], b1["posi"]
                magic = 12582912.0
                c1, c2 = 6.28125, 0.0019340515136718750
                c3 = 2 * np.pi - c1 - c2
                dve.wait_ge(pos_landed, 16)
                dve.wait_ge(cols_landed, 16)
                ang, kf = b1["rt"][:, 0, 0:S], b1["rt"][:, 0, S:2 * S]
                own.mark(v.tensor_copy(ang, pos[:, :]))
                own.wait()
                own.mark(v.tensor_scalar(ang, ang, col("freq"), None, ALU.mult))
                own.wait()
                for j, off in enumerate((0.0, 0.25)):
                    own.mark(v.tensor_scalar(kf, ang, float(1 / (2 * np.pi)), off, ALU.mult, ALU.add))
                    own.wait()
                    own.mark(v.tensor_scalar(kf, kf, magic, None, ALU.add))
                    own.wait()
                    own.mark(v.tensor_scalar(kf, kf, magic, None, ALU.subtract))
                    own.wait()
                    r = tr[:, j, :]
                    own.mark(v.scalar_tensor_tensor(out=r, in0=kf, scalar=-c1, in1=ang, op0=ALU.mult, op1=ALU.add))
                    own.wait()
                    own.mark(v.scalar_tensor_tensor(out=r, in0=kf, scalar=-c2, in1=r, op0=ALU.mult, op1=ALU.add))
                    own.wait()
                    own.mark(v.scalar_tensor_tensor(out=r, in0=kf, scalar=-float(c3), in1=r, op0=ALU.mult, op1=ALU.add))
                    own.wait()
                    if j:
                        own.mark(v.tensor_scalar(r, r, float(np.pi / 2), None, ALU.add))
                        own.wait()
                    ins = v.tensor_scalar(r, r, 3.1415925, -3.1415925, ALU.min, ALU.max)
                ins.then_inc(trig_red, 1)

            def rope(c):
                evacuated(dve, c)
                rt = b1["rt"]
                if c == 2:
                    dve.wait_ge(tab_landed, 16)
                else:
                    dve.wait_ge(rope_done, c - 2)
                two = lambda ap: ap.rearrange("p (a n) -> p a n", a=2)
                v.tensor_tensor(two(rt[:, 0, :]), two(b1["qraw"][:, c % 2, :]), over(table("cos", S), 2), ALU.mult)
                dve.wait_ge(rot_done, c - 1)
                own.mark(v.tensor_tensor(two(rt[:, 1, :]), two(ps[:, 2, :]), over(table("sin", S), 2), ALU.mult))
                own.wait()
                if c < 4:
                    v.tensor_tensor(b1["qT"][:, 2 * (c - 2):2 * (c - 1), :], two(rt[:, 0, :]), two(rt[:, 1, :]), ALU.add).then_inc(rope_done, 1)
                else:
                    dve.wait_ge(pool_zero, 3)
                    for par in range(2):
                        a = slice(64 * par, 64 * par + 64)
                        ins = v.tensor_tensor(b1["kz"][a, par, 2 * (c - 4):2 * (c - 3), :], two(rt[a, 0, :]), two(rt[a, 1, :]), ALU.add)
                    ins.then_inc(rope_done, 1)

            def att_mask(g, sm, st, scale, mask):
                a = 4 + 2 * (g % 2)
                r = sm[:, g % 2, :]
                s = st[:, g % 2, 0, :]
                dve.wait_ge(at_s, g + 1)
                s0 = r[:, 0:256].rearrange("p (a n) -> p a n", a=2)
                s1 = r[:, 256:768].rearrange("p (a n) -> p a n", a=2)
                v.scalar_tensor_tensor(out=s0, in0=ps[:, a, 0:256].rearrange("p (a n) -> p a n", a=2), scalar=scale, in1=mask(P, S),
                                       op0=ALU.mult, op1=ALU.add)
                own.mark(v.scalar_tensor_tensor(out=s1, in0=ps[:, a + 1, :].rearrange("p (a n) -> p a n", a=2), scalar=scale, in1=mask(0, S),
                                                op0=ALU.mult, op1=ALU.add))
                own.wait()
                v.tensor_reduce(s[:, 0:2], s0, AX.X, ALU.max, negate=True)
                v.tensor_reduce(s[:, 2:4], s1, AX.X, ALU.max, negate=True).then_inc(at_m, 1)

            def att_norm(g, sm, st):
                r = sm[:, g % 2, :]
                dve.wait_ge(at_e, g + 1)
                own.mark(v.reciprocal(st[:, g % 2, 2, :], st[:, g % 2, 1, :]))
                own.wait()
                for j in range(4):
                    a = slice(j * P, j * P + P) if j < 2 else slice(256 + (j - 2) * S, 256 + (j - 2) * S + S)
                    ins = v.tensor_scalar(r[:, a], r[:, a], st[:, g % 2, 2, j:j + 1], None, ALU.mult)
                ins.then_inc(at_n, 1)

            def att_pt(g, pt):
                dve.wait_ge(at_t, g + 1)
                v.tensor_copy(pt[:, g % 2, 512:768], ps[:, 4 + 2 * (g % 2), 0:256]).then_inc(at_p1, 1)

            def att_y(g, yh, yl, k):
                dve.wait_ge(at_yh, g + 1)
                v.tensor_tensor(yl[:, k, :], ps[:, 4 + 2 * (g % 2), 256:512], yh[:, k, :].bitcast(F32), ALU.subtract).then_inc(at_y, 1)

            causal = lambda a, b: over(table("causal", S)[:, a:b], 2)
            chunked = lambda a, b: over(table("chunked", S)[:, a:b], 2)

            def level_d(l):
                if l >= 2:
                    dve.wait_ge(lv_k, l - 1)
                    dve.wait_ge(lv_q, l - 1)
                p = 1 << l
                G = b1["G"][:, :, :].rearrange("p a (m q) -> p (a m) q", q=2 * p)
                E = b1["E"][:, l % 2, :, :].rearrange("p a (m q) -> p (a m) q", q=2 * p)
                ref = G[:, :, p - 1:p].to_broadcast([P, 2 * S // (2 * p), 2 * p])
                v.tensor_tensor(E, G, ref, ALU.subtract).then_inc(lv_d, 1)

            def level_q(l):
                dve.wait_ge(lv_e, l + 1)
                if l >= 2:
                    dve.wait_ge(lv_full, 2 * (l - 1))
                v.tensor_tensor(b1["QL"][:, l % 2, :, :], b1["gq"][:, :, :], b1["E"][:, l % 2, :, :], ALU.mult).then_inc(lv_q, 1)

            def level_copy(l):
                if l == 0:
                    dve.wait_ge(pool_zero, 5)
                    dve.wait_ge(gmask_landed, 16)
                for i in range(1 if l == LEVELS else 2):
                    n = 2 * l + i if l <= LEVELS else 2 * LEVELS + 1 + i
                    dve.wait_ge(lv_full, n + 1)
                    if n >= 2:
                        dve.wait_ge(lv_copied, n - 1)
                    src = ps[:, 2 + i, :].rearrange("p (h n) -> p h n", h=4)
                    if l == LEVELS:
                        v.tensor_copy(b1["AT0"][:, :, P:S], src).then_inc(lv_copied, 1)
                    else:
                        dst = b1["AT0"][:, :, 0:P] if i == 0 else b1["AT1"][:, :, :]
                        v.copy_predicated(dst, over(b1["gmask"][:, l if l < LEVELS else LEVELS, :], 4), src).then_inc(lv_copied, 1)

            def ada_block(q, aq, i=0, step=0):
                for kc in range(KC):
                    k = kc // 4
                    n = q * 2 + k
                    if kc % 4 == 0:
                        dve.wait_ge(ada_landed[k], (i * step + (q + 1)) * 16)
                    wv = ada_raw[:, k, (kc % 4) * 256:(kc % 4) * 256 + 256]
                    o = acc[:, ds(i * (step * 256) + aq * 256, 256)] if step else acc[:, aq * 256:aq * 256 + 256]
                    if kc == 0:
                        ins = v.tensor_scalar(o, wv, cact[:, 0:1], None, ALU.mult)
                    else:
                        dve.wait_ge(ada_own if (kc - 1) % 4 != 3 else ada_used, (i * (step * 6) + (q * 6 + kc - kc // 4)) if (kc - 1) % 4 != 3 else (i * (step * 2) + (q * 2 + 1)))
                        ins = v.scalar_tensor_tensor(out=o, in0=wv, scalar=cact[:, kc:kc + 1], in1=o, op0=ALU.mult, op1=ALU.add)
                    ins.then_inc(ada_used if kc % 4 == 3 else ada_own, 1)

            def ffn_up_evac(conv, fi, c, j, i=0):
                u = bank_use(c)
                b = u % 2
                vv = j % 2
                n = FT * fi + j + 1 + 2 * i
                if conv:
                    dve.wait_ge(cv_base, n)
                    for t2 in range(2):
                        jj = j + FT * t2
                        w1 = cols[:, ds(i * 2 + (COL["conv_w"] + 44 + jj), 1)]
                        w0 = cols[:, ds(i * 2 + (COL["conv_w"] + jj), 1)]
                        src = ps[:, b, t2 * S:t2 * S + S]
                        y = cv[:, vv, t2, :]
                        v.scalar_tensor_tensor(out=y[:, 1:S], in0=src[:, 0:S - 1], scalar=w1, in1=y[:, 1:S], op0=ALU.mult, op1=ALU.add).then_inc(cv_own, 1)
                        dve.wait_ge(cv_own, 3 * (j + 1) + 6 * i - 2 + t2)
                        ins = v.scalar_tensor_tensor(out=y[:, 2:S], in0=src[:, 0:S - 2], scalar=w0, in1=y[:, 2:S], op0=ALU.mult, op1=ALU.add)
                        ins.then_inc(cv_gate if t2 == 0 else bank_free[b], 1)
                    dve.wait_ge(bank_free[b], u // 2 + 1 + i)
                    dve.wait_ge(sg_done, n)
                    v.tensor_tensor(av[:, vv, :], sg[:, vv, :], cv[:, vv, 1, :], ALU.mult).then_inc(cv_own, 1)
                    dve.wait_ge(cv_own, 3 * (j + 1) + 6 * i)
                else:
                    dve.wait_ge(sg_done, n)
                    if j >= 2:
                        dve.wait_ge(act_ready, n - 2)
                    v.tensor_tensor(av[:, vv, :], sg[:, vv, :], ps[:, b, S:2 * S], ALU.mult).then_inc(bank_free[b], 1)
                    dve.wait_ge(bank_free[b], u // 2 + 1 + i)
                ah = act_hi[:, ds(i * 2 + j, 1), :].rearrange("p a n -> p (a n)")
                al = act_lo[:, ds(i * 2 + j, 1), :].rearrange("p a n -> p (a n)")
                v.tensor_copy(ah, av[:, vv, :]).then_inc(ah_done, 1)
                dve.wait_ge(ah_done, n)
                v.tensor_tensor(al, av[:, vv, :], ah.bitcast(F32), ALU.subtract).then_inc(act_ready, 1)

            def ffn_up(fi, c0, ada=False):
                conv = fi == 0
                for j in range(2):
                    lo(c0 + 1 + j)
                    ffn_up_evac(conv, fi, c0 + j, j)
                    if ada:
                        ada_block(ADA_Q + j, j)
                with dve.Fori(0, FT // 2 - 1) as i:
                    for vv in range(2):
                        lo(c0 + 3 + vv, i=i)
                        ffn_up_evac(conv, fi, c0 + 2 + vv, 2 + vv, i=i)
                    if ada:
                        ada_block(ADA_Q + 2, 2, i=i, step=1)

            def ffn_down(fi, c0, ada=None, gate=None, last=False):
                q, aq, ahead, behind = ada or (0, 0, 0, 0)
                lo(c0 + 1)
                for j in range(ahead):
                    ada_block(q + j, aq + j)
                q, aq = q + ahead, aq + ahead
                with dve.Fori(0, 4) as i:
                    for vv in range(2):
                        lo(c0 + 2 + vv, i=i)
                        if ada:
                            ada_block(q + vv, aq + vv, i=i, step=2)
                q, aq = q + 8, aq + 8
                lo(c0 + 10)
                for j in range(behind):
                    ada_block(q + j, aq + j)
                if not last:
                    lo(c0 + 11)
                for p in range(4):
                    if p < 3:
                        dve.wait_ge(down_full, 3 * fi + p + 1)
                    else:
                        dve.wait_ge(half_used, 2 * (c0 + 11))
                    ins = add_pair(4 + p, p) if gate is None else gated_pair(4 + p, p, gate)
                    ins.then_inc(resid_done, 1)

            def ada_mod(s0, n, gate_scale):
                m = mod[:, s0:s0 + n, :].rearrange("p a b -> p (a b)")
                dve.wait_ge(ada_cols, 1 if s0 == 0 else 2)
                own.mark(v.tensor_tensor(m, ps[:, 3, 0:24 * n], cols[:, COL["b_ada"] + 24 * s0:COL["b_ada"] + 24 * (s0 + n)], ALU.add))
                own.wait()
                for s in range(s0, s0 + n):
                    g = COL[("f1_g", "mix_g", "f2_g")[s]]
                    v.scalar_tensor_tensor(out=modA[:, s, :], in0=mod[:, s, 8:16], scalar=1.0, in1=cols[:, g:g + KC], op0=ALU.add, op1=ALU.mult)
                    ins = v.tensor_scalar(mod[:, s, 16:24], mod[:, s, 16:24], gate_scale, None, ALU.mult)
                ins.then_inc(mod_ready, 1)

            rope_trig()
            lo(0)
            norm_plain(0, 0, "attn_g")
            lo(1)
            lo(2)
            dve.wait_ge(ls_done, 1)
            own.mark(v.scalar_tensor_tensor(out=b1["E"][:, 0, :, :], in0=b1["QL"][:, 0, :, :], scalar=0.0, in1=b1["KL"][:, 0, 1, :, :],
                                            op0=ALU.min, op1=ALU.subtract))
            own.mark(v.memset(b1["E"][:, 1, 0, :], 1.0))
            own.wait()
            for ht in range(2):
                ins = v.tensor_tensor_scan(b1["G"][:, ht, :], b1["E"][:, 1, 0, :], b1["E"][:, 0, ht, :], 0.0, ALU.mult, ALU.add)
            own.mark(ins)
            own.wait()
            sm1, st1, pt1, yh1, yl1 = b1["sm1"], b1["st1"], b1["pt1"], b1["yh1"], b1["yl1"]
            level_d(0)
            level_d(1)
            lo(3)
            lo(4)
            rope(2)
            level_q(0)
            lo(5)
            rope(3)
            level_q(1)
            level_d(2)
            lo(6)
            rope(4)
            lo(7)
            rope(5)
            lo(8)
            att_mask(0, sm1, st1, 0.125, causal)
            att_mask(1, sm1, st1, 0.125, causal)
            level_copy(0)
            level_q(2)
            level_d(3)
            lo(9)
            att_norm(0, sm1, st1)
            level_copy(1)
            att_norm(1, sm1, st1)
            level_q(3)
            level_d(4)
            lo(10)
            att_pt(0, pt1)
            level_copy(2)
            level_q(4)
            level_d(5)
            lo(11)
            att_y(0, yh1, yl1, 0)
            level_copy(3)
            att_pt(1, pt1)
            att_mask(2, sm1, st1, 0.125, causal)
            level_q(5)
            level_d(6)
            lo(12)
            att_y(1, yh1, yl1, 1)
            level_copy(4)
            att_norm(2, sm1, st1)
            att_mask(3, sm1, st1, 0.125, causal)
            att_pt(2, pt1)
            level_q(6)
            level_d(7)
            level_copy(5)
            att_y(2, yh1, yl1, 2)
            att_norm(3, sm1, st1)
            att_pt(3, pt1)
            level_copy(6)
            level_q(7)
            att_y(3, yh1, yl1, 3)
            level_copy(7)
            level_copy(8)
            for j in range(2):
                a = b1["og"][:, 2 * j:2 * j + 2, :]
                r = b1["g_sd"][:, 2 * j:2 * j + 2, :]
                dve.wait_ge(go_sd, j + 1)
                own.mark(v.reciprocal(r, r))
                own.wait()
                for h in (2 * j, 2 * j + 1):
                    ins = v.scalar_tensor_tensor(out=b1["og"][:, h, :], in0=b1["og"][:, h, :], scalar=col("gla_g", h), in1=b1["g_sd"][:, h, :],
                                                 op0=ALU.mult, op1=ALU.mult)
                own.mark(ins)
                own.wait()
                dve.wait_ge(gr_silu, 1)
                v.tensor_tensor(a, a, b1["gr"][:, 2 * j:2 * j + 2, :], ALU.mult).then_inc(go_v, 1)
            for j in range(2):
                dve.wait_ge(yg_hi, j + 1)
                v.tensor_tensor(b1["yl1"][:, 4 + 2 * j:6 + 2 * j, :], b1["og"][:, 2 * j:2 * j + 2, :],
                                b1["yh1"][:, 4 + 2 * j:6 + 2 * j, :].bitcast(F32), ALU.subtract).then_inc(yg_ready, 1)
            add_out(C_OUT1)
            norm_plain(1, 1, "ffn_g")
            ffn_up(0, C_UP[0])
            ffn_down(0, C_DN[0], ada=(0, 0, 2, 2))
            norm_in_place(2, "fin1_g")
            ada_mod(0, 1, 0.5)
            norm_mod(3, 2)
            ffn_up(1, C_UP[1], ada=True)
            ffn_down(1, C_DN[1], ada=(24, 12, 2, 2), gate=0)
            ada_mod(1, 2, 0.5)
            norm_mod(4, 3)
            dve.wait_ge(ada_cols, 2)
            lo(C_IN2 + 1)
            lo(C_IN2 + 2)
            lo(C_IN2 + 3)
            lat, lsd = b2["lat"], b2["l_sd"]
            dve.wait_ge(lat_sd, 1)
            own.mark(v.reciprocal(lsd[:, :, :], lsd[:, :, :]))
            own.wait()
            for j in range(3):
                ins = v.scalar_tensor_tensor(out=lat[:, j, :], in0=lat[:, j, :], scalar=col("q_g", j) if j < 2 else col("kv_g"),
                                             in1=lsd[:, j // 2, :], op0=ALU.mult, op1=ALU.mult)
            ins.then_inc(lat_v, 1)
            lo(C_IN2 + 4)
            dve.wait_ge(lat_hi, 1)
            v.tensor_tensor(b2["cql"][:, :, :], lat[:, :, :], b2["cqh"][:, :, :].bitcast(F32), ALU.subtract).then_inc(lat_ready2, 1)
            dve.wait_ge(pe_rot, 1)
            dve.wait_ge(pool_zero, 8)
            dve.wait_ge(trig_done, 1)
            v.tensor_tensor(b2["rt2"][:, 0:S], b2["kpr"][:, :], cos2[:, :], ALU.mult)
            own.mark(v.tensor_tensor(b2["rt2"][:, S:2 * S], ps[:, 3, 0:S], sin2[:, :], ALU.mult))
            own.wait()
            for j in range(4):
                a = slice(32 * j, 32 * j + 32)
                ins = v.tensor_tensor(b2["kpz"][a, j, :], b2["rt2"][a, 0:S], b2["rt2"][a, S:2 * S], ALU.add)
            ins.then_inc(pe_done, 1)
            lo(C_IN2 + 5)
            lo(C_UQ)
            lo(C_UV)
            lo(C_CAV)
            lo(C_CAV + 1)
            dve.wait_ge(pe_rot, 2)
            dve.wait_ge(pe_done, 1)
            two = lambda ap: ap.rearrange("p (a n) -> p a n", a=2)
            own.mark(v.tensor_tensor(two(b2["rt2"][:, :]), two(ps[:, 3, :]), over(sin2[:, :], 2), ALU.mult))
            own.mark(v.tensor_tensor(two(b2["qpr"][:, :]), two(b2["qpr"][:, :]), over(cos2[:, :], 2), ALU.mult))
            own.wait()
            v.tensor_tensor(b2["qpe"][:, :, :], two(b2["qpr"][:, :]), two(b2["rt2"][:, :]), ALU.add).then_inc(pe_done, 1)
            lo(C_CAV + 2)
            mla = 96.0 ** -0.5
            dve.wait_ge(bm_ready, 1)

            def mask2(g):
                if g < 8:
                    att_mask(g, b2["sm2"], b2["st2"], mla, chunked)
                else:
                    h = 2 * (g - 8)
                    att_mask(g, b2["sm2"], b2["st2"], 0.125, lambda a, b_: b2["bm"][:, h:h + 2, a:b_])

            mask2(4)
            mask2(5)
            for c in range(8):
                lo(C_GATE + c + 1)
                g = 4 + c
                att_norm(g, b2["sm2"], b2["st2"])
                att_pt(g, b2["pt2"])
                att_y(g, b2["yh2"], b2["yl2"], c)
                if g + 2 < 12:
                    mask2(g + 2)
            for br in range(2):
                for cc in range(2):
                    c = C_BR + 2 * br + cc
                    lo(c + 1)
                    dve.wait_ge(half_used, 2 * c + 2)
                    for f2 in range(2):
                        b = (bank_use(c) + f2) % 2
                        k = 4 * cc + 2 * f2
                        th = b2["th"][:, 8 * br + k:8 * br + k + 2, :]
                        dst = xn[:, k:k + 2, :] if br == 0 else b2["caz"][:, cc, 2 * f2:2 * f2 + 2, :]
                        v.scalar_tensor_tensor(out=dst, in0=th, scalar=1.0, in1=two(ps[:, b, :]), op0=ALU.add, op1=ALU.mult).then_inc(bank_free[b], 1)
                        dve.wait_ge(bank_free[b], (bank_use(c) + f2) // 2 + 1)
                        if br == 1:
                            v.tensor_tensor(xn[:, k:k + 2, :], xn[:, k:k + 2, :], dst, ALU.add).then_inc(br_done, 1)
            for p in range(4):
                dve.wait_ge(mh_ready, p + 1)
                v.tensor_tensor(pair(xl, p), pair(xn, p), pair(xh, p).bitcast(F32), ALU.subtract).then_inc(ml_ready, 1)
            add_out(C_OUT2, gate=1)
            norm_mod(5, 4)
            ffn_up(2, C_UP[2])
            ffn_down(2, C_DN[2], gate=2, last=True)
            norm_in_place(6, "fin2_g")



def _tiles(w, k0, kn, c):
    a = w[k0 * P:(k0 + kn) * P][:, c].reshape(kn, P, -1)
    return a.transpose(1, 0, 2).reshape(P, -1)


def _padded(a):
    out = np.zeros((P, HALF), a.dtype)
    out[:, :a.shape[1]] = a
    return out


def _weights(a):
    s = []
    r = np.arange

    def feature_chunk(w, c):
        s.extend([_tiles(w, 0, 4, c), _tiles(w, 4, 4, c)])

    def up(w, width):
        for j in range(FT):
            feature_chunk(w, np.concatenate([r(j * P, j * P + P), width + r(j * P, j * P + P)]))

    w = a["w_in"][0]
    for c0, n in ((1536, 256), (1792, 256), (0, 512), (512, 512), (1024, 512), (2048, 512), (2560, 512)):
        for c in range(c0, c0 + n, 256):
            feature_chunk(w, r(c, c + 256))
    for c in range(0, D, 256):
        feature_chunk(a["w_out"][0], r(c, c + 256))
    up(a["w_ffn_up"][0], DFF)
    s.extend(a["w_ffn_down"][0].reshape(FT, P, D))
    up(a["ffn1_w_in_2"][0], DFF)
    s.extend(a["ffn1_w_out_2"][0].reshape(FT, P, D))
    w = a["w_in_2"][0]
    feature_chunk(w, r(0, 256))
    feature_chunk(w, np.concatenate([r(256, 384)] + 4 * [r(384, 416)]))
    for c in range(416, 416 + 1024, 256):
        feature_chunk(w, r(c, c + 256))
    uq, ukv = a["mla_w_uq_2"][0], a["mla_w_ukv_2"][0]
    head = r(8)[:, None]
    q_cols = np.concatenate([(96 * head + r(64)).ravel(), (96 * head + 64 + r(32)).ravel()])
    k_cols, v_cols = (128 * head + r(64)).ravel(), (128 * head + 64 + r(64)).ravel()
    for j in range(2):
        s.append(np.concatenate([_tiles(uq, j, 1, q_cols), _tiles(ukv, 0, 1, k_cols[256 * j:256 * j + 256])], 1))
    s.append(_padded(_tiles(ukv, 0, 1, v_cols)))
    s.append(_padded(s[-1][:, :0]))
    for c in range(1440, 4000, 256):
        feature_chunk(w, r(c, c + 256))
    for w in (a["w_branch_a_2"][0], a["w_branch_b_2"][0]):
        for c in (0, 512):
            for k in (0, 2):
                s.append(_tiles(w, k, 2, r(c, c + 512)))
    for c in range(0, D, 256):
        feature_chunk(a["w_out_2"][0], r(c, c + 256))
    up(a["ffn2_w_in_2"][0], DFF)
    s.extend(a["ffn2_w_out_2"][0].reshape(FT, P, D))
    return np.stack(s)


def _ada(w):
    a = w.reshape(2, 4, P, 3 * ADA_Q, 256)
    return np.ascontiguousarray(a.transpose(3, 0, 2, 1, 4)).reshape(6 * ADA_Q, P, HALF)


def _columns(a):
    col = lambda v: np.asarray(v).reshape(-1, P).T
    p = np.arange(P)
    freq = np.float32(10000.0) ** (-np.arange(0, 32, 2, dtype=np.float32) / np.float32(32))
    freq = np.where(p % 32 < 16, -freq[p % 16], freq[p % 16]).astype(np.float32)[:, None]
    c = [col(a["attn_norm_g"][0]), col(a["ffn_norm_g"][0]), col(a["final_norm_g"]), col(a["gla_norm_g"][0]), col(a["b_gate"][0]),
         col(a["conv_w"][0, 0]), col(a["conv_w"][0, 1]), col(a["conv_w"][0, 2]), col(a["conv_b"][0]),
         col(a["ffn1_norm_2"][0]), col(a["mix_norm_2"][0]), col(a["ffn2_norm_2"][0]), col(a["final_norm_2"]),
         col(a["mla_q_norm_2"][0]), col(a["mla_kv_norm_2"][0]), col(a["c_2"][0]), col(a["b_ada_2"][0]), freq]
    return np.ascontiguousarray(np.concatenate(c, 1))


def _constants():
    p, n = np.arange(P)[:, None], np.arange(S)[None, :]
    inv = np.float32(1.0) / (np.float32(10000.0) ** (np.arange(0, 64, 2, dtype=np.float32) / np.float32(64)))
    ang = n.astype(np.float32) * inv[p % 32]
    m = np.arange(P)[None, :]
    zero = np.zeros((P, P), np.float32)
    causal = np.where(m <= p, 0, NEG)
    chunked = np.where(m // 64 <= p // 64, 0, NEG)
    tab = [np.cos(ang), np.where(p % 64 < 32, -np.sin(ang), np.sin(ang)), p == (m ^ 32), p == (m ^ 16), zero, causal, zero, chunked]
    tab = np.concatenate([x.astype(np.float32) for x in tab], 1)
    levels = [(p // (2 * q) == m // (2 * q)) & (p % (2 * q) < q) & (m % (2 * q) >= q) for q in (1 << np.arange(LEVELS))]
    return tab, np.stack(levels + [p == m], 1).astype(np.int32)


def _bias(rel):
    i = 256 + np.arange(P)[:, None] + P - np.arange(S)[None, :]
    return np.ascontiguousarray(rel[0][i].transpose(0, 2, 1))


def kernel(**inputs):
    import concourse.bacc as bacc
    from concourse.bass_utils import run_bass_kernel_spmd as run

    a = {k: np.asarray(v) for k, v in inputs.items()}
    tab, gmask = _constants()
    w_in = a["w_in"][0]
    gup = np.zeros((P, S), w_in.dtype)
    gup[:16] = a["w_gate_up"][0]
    arrays = {
        "w": _weights(a), "ada_w": _ada(a["w_ada_2"][0]),
        "x_in": np.ascontiguousarray(a["x"][0].T.reshape(KC, P, S).transpose(1, 0, 2)),
        "cols_in": _columns(a), "tab_in": tab, "gmask_in": gmask,
        "glr_in": np.ascontiguousarray(_tiles(w_in, 0, KC, np.arange(3072, 3088))), "gup_in": gup,
        "bias_in": _bias(a["rel_bias_2"]), "pos_in": a["positions_2"].reshape(1, S).astype(np.int32),
    }
    nc = bacc.Bacc("TRN2", target_bir_lowering=False, num_devices=1)
    aps = {n: nc.dram_tensor(n, v.shape, mybir.dt.from_np(v.dtype), kind="ExternalInput").ap() for n, v in arrays.items()}
    out = nc.dram_tensor("out", (P, KC, S), mybir.dt.float32, kind="ExternalOutput").ap()
    build(nc, out=out, **aps)
    r = run(nc, [arrays], core_ids=[0])
    y = r.results[0]["out"]
    return y.transpose(1, 0, 2).reshape(D, S).T[None]
```

```python
from contextlib import ExitStack

import numpy as np

import concourse.bass as bass
from concourse import mybir

P = 128
D = 1024
S = 256
KC = D // P
DFF = 2816
FT = DFF // P
HALF = 1024
NSLOT = 4
EPS = 1e-6
NEG = -1e30
LEVELS = 7
NADA = 72

C_IN1 = 0
C_OUT1 = C_IN1 + 12
C_UP = [C_OUT1 + 4, 0, 0]
C_DN = [C_UP[0] + FT, 0, 0]
C_UP[1] = C_DN[0] + FT // 2
C_DN[1] = C_UP[1] + FT
C_IN2 = C_DN[1] + FT // 2
C_UQ = C_IN2 + 6
C_UV = C_IN2 + 7
C_CAV = C_IN2 + 8
C_GATE = C_IN2 + 10
C_BR = C_IN2 + 18
C_OUT2 = C_BR + 4
C_UP[2] = C_OUT2 + 4
C_DN[2] = C_UP[2] + FT
NCHUNK = C_DN[2] + FT // 2
NHALF = 2 * NCHUNK
DOWN = [C_OUT1, C_DN[0], C_DN[1], C_OUT2, C_DN[2]]

COL = {}
_n = 0
for _name, _w in [("attn_g", 8), ("ffn_g", 8), ("fin1_g", 8), ("gla_g", 4), ("b_gate", 2), ("conv_w", 132),
                  ("conv_b", 44), ("f1_g", 8), ("mix_g", 8), ("f2_g", 8), ("fin2_g", 8), ("q_g", 2),
                  ("kv_g", 1), ("b_ada", 72), ("freq", 1)]:
    COL[_name] = _n
    _n += _w
NCOL = _n

TAB = {}
_n = 0
for _name, _w in [("cos", S), ("sin", S), ("perm64", P), ("perm32", P), ("causal", S), ("chunked", S)]:
    TAB[_name] = _n
    _n += _w
NTAB = _n


def build(nc, w, ada_w, x_in, cols_in, tab_in, gmask_in, glr_in, gup_in, bias_in, c_in, pos_in, out):
    F32 = mybir.dt.float32
    F32R = mybir.dt.float32r
    I32 = mybir.dt.int32
    ALU = mybir.AluOpType
    ACT = mybir.ActivationFunctionType
    AX = mybir.AxisListType
    ds = bass.ds

    with ExitStack() as ctx:
        sb = lambda name, shape, dt=F32: ctx.enter_context(nc.sbuf_tensor(name, shape, dt))
        sem = lambda name: ctx.enter_context(nc.semaphore(name))

        raw = sb("raw", [P, NSLOT, HALF])
        w_hi = sb("w_hi", [P, NSLOT, HALF], F32R)
        w_lo = sb("w_lo", [P, NSLOT, HALF], F32R)
        X = sb("X", [P, KC, S])
        xn = sb("xn", [P, KC, S])
        xh = sb("xh", [P, KC, S], F32R)
        xl = sb("xl", [P, KC, S], F32R)
        rstd = sb("rstd", [P, S])
        sd = sb("sd", [P, 2, S])
        epsc = sb("epsc", [P, 3])
        cols = sb("cols", [P, NCOL])
        tab = sb("tab", [P, NTAB])
        mean = sb("mean", [P, 3, P])
        ident = sb("ident", [P, P])
        mod = sb("mod", [P, 3, 24])
        modA = sb("modA", [P, 3, KC])
        cos2 = sb("cos2", [P, S])
        sin2 = sb("sin2", [P, S])

        def phase(names, early=()):
            made = {}

            def place(tensors):
                guards = [nc.sbuf_tensor(n, s, d) for n, s, d in tensors]
                for (n, _, _), g in zip(tensors, guards):
                    made[n] = g.__enter__()
                return reversed(guards)

            kept = place(names[:-1])
            for g in place(early):
                g.__exit__(None, None, None)
            for g in place(names[-1:]):
                g.__exit__(None, None, None)
            for g in kept:
                g.__exit__(None, None, None)
            return made

        ffn = phase([("act_hi", [P, FT, S], F32R), ("act_lo", [P, FT, S], F32R), ("cv", [P, 2, 2, S], F32),
                     ("sg", [P, 2, S], F32), ("av", [P, 2, S], F32), ("ada_raw", [P, 4, HALF], F32),
                     ("ada_mul", [P, 2, HALF], F32), ("cact", [P, HALF], F32), ("gmean", [P, KC, P], F32), ("gsq", [P, KC], F32),
                     ("ada_col", [P, 2], F32)])
        act_hi, act_lo, cv, sg, av, ada_raw, ada_mul, cact, gmean, gsq, ada_col = ffn.values()
        b1 = phase([("qT", [P, 4, S], F32), ("kz", [P, 2, 4, S], F32), ("mv", [P, 2, 512], F32),
                    ("gv", [P, 2, 512], F32), ("gq", [P, 2, S], F32), ("gkz", [P, 2, 2, S], F32),
                    ("gr", [P, 4, S], F32), ("G", [P, 2, S], F32), ("E", [P, 2, 2, S], F32),
                    ("QL", [P, 2, 2, S], F32), ("KL", [P, 2, 2, 2, S], F32), ("AT0", [P, 4, S], F32),
                    ("AT1", [P, 4, P], F32), ("og", [P, 4, S], F32), ("qraw", [P, 2, 2 * S], F32),
                    ("rt", [P, 2, 2 * S], F32), ("glr", [P, S], F32), ("w_glr", [P, 128], F32),
                    ("w_gup", [P, S], F32), ("gmask", [P, 8, P], I32), ("g_sd", [P, 4, S], F32),
                    ("yh1", [P, 8, S], F32R), ("yl1", [P, 8, S], F32R), ("sm1", [P, 2, 768], F32),
                    ("pt1", [P, 2, 768], F32), ("st1", [P, 2, 3, 4], F32), ("trig", [P, 2, S], F32),
                    ("posi", [P, S], I32), ("ones_row", [P, 2], F32)])
        b2 = phase([("qn", [P, 4, S], F32), ("qpe", [P, 2, S], F32), ("nz", [P, 2, 4, S], F32),
                    ("kpz", [P, 4, S], F32), ("v2", [P, 2, 512], F32), ("caq", [P, 4, S], F32),
                    ("caz", [P, 2, 4, S], F32), ("cav", [P, 2, 512], F32), ("l_sd", [P, 2, S], F32), ("kpr", [P, S], F32), ("qpr", [P, 2 * S], F32),
                    ("rt2", [P, 2 * S], F32), ("yh2", [P, 8, S], F32R), ("yl2", [P, 8, S], F32R),
                    ("sm2", [P, 2, 768], F32), ("pt2", [P, 2, 768], F32), ("st2", [P, 2, 3, 4], F32),
                    ("bm", [P, 8, S], F32), ("th", [P, 16, S], F32)],
                   early=[("lat", [P, 3, S], F32), ("latsq", [P, 3, S], F32), ("cqh", [P, 3, S], F32R), ("cql", [P, 3, S], F32R)])

        ps = ctx.enter_context(nc.psum_tensor("ps", [P, 8, 512], F32))

        x_landed = [sem(f"x_landed{i}") for i in range(2)]
        cols_landed, tab_landed, aux_landed, bias_landed = map(sem, ("cols_landed", "tab_landed", "aux_landed", "bias_landed"))
        pos_landed, gmask_landed = sem("pos_landed"), sem("gmask_landed")
        raw_landed = [sem(f"raw_landed{i}") for i in range(NSLOT)]
        ada_landed = [sem(f"ada_landed{i}") for i in range(4)]
        hi_ready, lo_ready, half_used = sem("hi_ready"), sem("lo_ready"), sem("half_used")
        bank_free = [sem("bank0_free"), sem("bank1_free")]
        consts_ready, pool_zero = sem("consts_ready"), sem("pool_zero")
        resid_done, sq_done, ss_done, sd_done, rstd_done, eps_mixed = map(
            sem, ("resid_done", "sq_done", "ss_done", "sd_done", "rstd_done", "eps_mixed"))
        xt_ready, xh_ready, xl_ready = map(sem, ("xt_ready", "xh_ready", "xl_ready"))
        own_act, own_dve, own_pool = sem("own_act"), sem("own_dve"), sem("own_pool")
        cv_base, cv_gate, cv_own, sg_done, av_done, ah_done, act_ready, down_full = map(
            sem, ("cv_base", "cv_gate", "cv_own", "sg_done", "av_done", "ah_done", "act_ready", "down_full"))
        c_landed, cact_ready, ada_mult, ada_used, ada_moved, mod_ready, gmean_ready = map(
            sem, ("c_landed", "cact_ready", "ada_mult", "ada_used", "ada_moved", "mod_ready", "gmean_ready"))
        trig_red, trig_done = sem("trig_red"), sem("trig_done")
        glr_done, glr_sb, gup_done, z_done, ls_done = map(sem, ("glr_done", "glr_sb", "gup_done", "z_done", "ls_done"))
        rot_done, rope_done = map(sem, ("rot_done", "rope_done"))
        lv_d, lv_e, lv_q, lv_k, lv_full, lv_copied = map(sem, ("lv_d", "lv_e", "lv_q", "lv_k", "lv_full", "lv_copied"))
        go_full, go_sq, go_ss, go_sd, gr_silu, go_v, yg_hi, yg_ready = map(
            sem, ("go_full", "go_sq", "go_ss", "go_sd", "gr_silu", "go_v", "yg_hi", "yg_ready"))
        at_s, at_m, at_e, at_n, at_t, at_p0, at_p1, at_o, at_yh, at_y = map(
            sem, ("at_s", "at_m", "at_e", "at_n", "at_t", "at_p0", "at_p1", "at_o", "at_yh", "at_y"))
        lat_sq, lat_ss, lat_sd, lat_v, lat_hi, lat_ready2, uq_full = map(
            sem, ("lat_sq", "lat_ss", "lat_sd", "lat_v", "lat_hi", "lat_ready2", "uq_full"))
        pe_rot, pe_done, br_used, br_done, mh_ready, ml_ready, bm_ready = map(
            sem, ("pe_rot", "pe_done", "br_used", "br_done", "mh_ready", "ml_ready", "bm_ready"))
        out_written = sem("out_written")

        block = ctx.enter_context(nc.Block())

        def table(name, n):
            return tab[:, TAB[name]:TAB[name] + n]

        def col(name, j=0):
            return cols[:, COL[name] + j:COL[name] + j + 1]

        def over(ap, n):
            return ap.unsqueeze(1).to_broadcast([ap.shape[0], n, ap.shape[1]])

        def slot(h):
            return h % NSLOT

        def pair(a, p):
            return a[:, 2 * p:2 * p + 2, :]

        class Own:
            def __init__(self, eng, s):
                self.eng, self.s, self.n = eng, s, 0

            def mark(self, ins):
                ins.then_inc(self.s, 1)
                self.n += 1

            def wait(self):
                self.eng.wait_ge(self.s, self.n)

        def bank_use(c):
            other = [(d, 4 if d in (C_OUT1, C_OUT2) else FT // 2) for d in DOWN] + [(C_BR, 4)]
            return c - sum(n for d, n in other if c > d) + 4 * (c > C_UQ) + (c > C_UV)

        def evacuated(eng, u):
            eng.wait_ge(bank_free[u % 2], u // 2 + 1)

        @block.sync
        def _(sp):
            def load(h, k):
                sp.dma_start(raw[:, k, :], w[h, :, :] if isinstance(h, int) else w[ds(h, 1), :, :].rearrange("a p n -> (a p) n")).then_inc(raw_landed[k], 16)

            for j in range(2):
                sp.dma_start(X[:, 4 * j:4 * j + 4, :], x_in[:, 4 * j:4 * j + 4, :]).then_inc(x_landed[j], 16)
            for k in range(NSLOT):
                load(k, k)
            with sp.Fori(1, NHALF // NSLOT) as i:
                for k in range(NSLOT):
                    sp.wait_ge(lo_ready, i * NSLOT + (k - NSLOT + 1))
                    load(i * NSLOT + k, k)
            for h in range(NHALF // NSLOT * NSLOT, NHALF):
                sp.wait_ge(lo_ready, h - NSLOT + 1)
                load(h, slot(h))
            for p in range(4):
                sp.wait_ge(resid_done, 21 + p)
                sp.dma_start(out[:, 2 * p:2 * p + 2, :], pair(X, p)).then_inc(out_written, 16)
            sp.wait_ge(out_written, 64)

        @block.gpsimd
        def _(pool):
            own = Own(pool, own_pool)
            for j, n in enumerate((D, 256, 128)):
                pool.memset(mean[:, j, :], 1.0 / n)
            pool.memset(epsc[:, 0:1], EPS)
            pool.memset(epsc[:, 1:2], EPS * EPS)
            own.mark(pool.memset(ident[:, :], 0.0))
            own.wait()
            pool.affine_select(out=ident[:, :], in_=ident[:, :], compare_op=ALU.not_equal, fill=1.0, base=0,
                               pattern=[[-1, P]], channel_multiplier=1).then_inc(consts_ready, 1)
            pool.memset(b1["glr"][:, :], 0.0).then_inc(pool_zero, 1)
            pool.memset(b1["gkz"][:, :, :, :], 0.0).then_inc(pool_zero, 1)
            pool.memset(b1["kz"][:, :, :, :], 0.0).then_inc(pool_zero, 1)
            pool.memset(b1["AT0"][:, :, :], 0.0).then_inc(pool_zero, 1)
            pool.memset(b1["AT1"][:, :, :], 0.0).then_inc(pool_zero, 1)

            for l in range(LEVELS + 1):
                pool.wait_ge(lv_e, l + 1)
                if l == 0:
                    evacuated(pool, 1)
                if l >= 2:
                    pool.wait_ge(lv_full, 2 * (l - 1))
                for par in range(2):
                    ins = pool.tensor_tensor(b1["KL"][:, l % 2, par, :, :], b1["gkz"][:, par, :, :], b1["E"][:, l % 2, :, :], ALU.mult)
                ins.then_inc(lv_k, 1)
            def load_ada(n, k):
                src = ada_w[n, :, :] if isinstance(n, int) else ada_w[ds(n, 1), :, :].rearrange("a p n -> (a p) n")
                pool.dma_start(ada_raw[:, k, :], src).then_inc(ada_landed[k], 16)

            mod_cols = mod[:, :, :].rearrange("p a b -> p (a b)")

            def move_sum(n, k):
                pool.wait_ge(ada_used, n + 1)
                pool.tensor_copy(mod_cols[:, ds(n, 1)], ada_col[:, k:k + 1]).then_inc(ada_moved, 1)

            def mult_ada(i, k, load=True):
                n = i * 4 + k
                pool.wait_ge(ada_landed[k], (i + 1) * 16)
                if not (isinstance(i, int) and n < 2):
                    move_sum(n - 2, k % 2)
                pool.tensor_tensor(ada_mul[:, k % 2, :], ada_raw[:, k, :], cact[:, :], ALU.mult).then_inc(ada_mult, 1)
                if load:
                    pool.wait_ge(ada_mult, n + 1)
                    load_ada(n + 4, k)

            pool.wait_ge(half_used, 2 * (C_OUT1 + 4))
            pool.wait_ge(trig_done, 1)
            pool.dma_start(cact[:, :], c_in.to_broadcast([P, HALF])).then_inc(c_landed, 16)
            for k in range(4):
                load_ada(k, k)
            pool.wait_ge(cact_ready, 1)
            for k in range(4):
                mult_ada(0, k)
            with pool.Fori(1, NADA // 4 - 1) as i:
                for k in range(4):
                    mult_ada(i, k)
            for k in range(4):
                mult_ada(NADA // 4 - 1, k, load=False)
            for k in range(2):
                move_sum(NADA - 2 + k, k)
            pool.wait_ge(mod_ready, 2)
            pool.wait_ge(half_used, 2 * C_IN2)
            pool.dma_start(b2["bm"][:, :, :], bias_in).then_inc(bias_landed, 16)
            pool.memset(b2["nz"][:, :, :, :], 0.0).then_inc(pool_zero, 1)
            pool.memset(b2["kpz"][:, :, :], 0.0).then_inc(pool_zero, 1)
            pool.memset(b2["caz"][:, :, :, :], 0.0).then_inc(pool_zero, 1)
            pool.wait_ge(bias_landed, 16)
            for h in range(8):
                ins = pool.tensor_tensor(b2["bm"][:, h, :], b2["bm"][:, h, :], table("chunked", S), ALU.add)
            ins.then_inc(bm_ready, 1)

        @block.tensor
        def _(pe):
            def three(o, lh, ll, rh, rl, start, stop):
                pe.matmul(o, lh, rh, start=start, stop=False, skip_group_check=True)
                pe.matmul(o, lh, rl, start=False, stop=False, skip_group_check=True)
                return pe.matmul(o, ll, rh, start=False, stop=stop, skip_group_check=True)

            def chunk(c, i=0, x_wait=None, tokens_out=False, halves=(0, 1)):
                ah, al = xh, xl
                u = bank_use(c)
                b = u % 2
                if halves[0] == 0 and not (isinstance(i, int) and u + 2 * i < 2):
                    pe.wait_ge(bank_free[b], u // 2 + i)
                for half in halves:
                    h = 2 * c + half
                    pe.wait_ge(lo_ready, h + 1 + 4 * i)
                    for k in range(4):
                        kc = 4 * half + k
                        if x_wait is not None and kc % 2 == 0:
                            s, n = x_wait
                            pe.wait_ge(s, n + kc // 2 + 1)
                        for f in range(2):
                            first = half == 0 and k == 0
                            last = half == 1 and k == 3
                            if tokens_out:
                                a = slice(f * P, f * P + P)
                                wcol = slice(k * 256, k * 256 + 256)
                                o = ps[:, b, f * 256:f * 256 + 256]
                                pe.matmul(o, ah[:, kc, a], w_hi[:, slot(h), wcol], start=first and f == 0, stop=False, skip_group_check=True)
                                pe.matmul(o, al[:, kc, a], w_hi[:, slot(h), wcol], start=False, stop=False, skip_group_check=True)
                                m = pe.matmul(o, ah[:, kc, a], w_lo[:, slot(h), wcol], start=False, stop=last, skip_group_check=True)
                            else:
                                wc = slice(k * 256 + f * P, k * 256 + f * P + P)
                                m = three(ps[:, b, f * 256:f * 256 + 256], w_hi[:, slot(h), wc], w_lo[:, slot(h), wc],
                                          ah[:, kc, :], al[:, kc, :], first and f == 0, last)
                    m.then_inc(half_used, 1)

            def norm_pair(n, p, bank=2, gain=False):
                if not gain:
                    pe.wait_ge(sq_done, 4 * (n - (n > 2)) + p + 1)
                for k in (2 * p, 2 * p + 1):
                    m = pe.matmul(ps[:, bank, 0:S], gmean[:, k, :] if gain else mean[:, 0, :], xn[:, k, :],
                                  start=k == 0, stop=k == KC - 1, skip_group_check=True)
                if p == 3:
                    m.then_inc(ss_done, 1)

            def att_s(g, q, kz, pe_q=None, pe_k=None):
                a = 4 + 2 * (g % 2)
                if g >= 2:
                    pe.wait_ge(at_y, g - 1)
                t4 = g % 4
                for hh in range(2):
                    h = 2 * t4 + hh
                    for (o, qs, n) in ((ps[:, a, hh * P:hh * P + P], 0, P), (ps[:, a + 1, hh * S:hh * S + S], P, S)):
                        m = pe.matmul(o, q[:, t4, qs:qs + P], kz[:, hh, t4, 0:n], start=True, stop=pe_q is None)
                        if pe_q is not None:
                            m = pe.matmul(o, pe_q[:, h // 4, qs:qs + P], pe_k[:, h % 4, 0:n], start=False, stop=True)
                m.then_inc(at_s, 1)

            def att_t(g, sm):
                a = 4 + 2 * (g % 2)
                r = sm[:, g % 2, :]
                pe.wait_ge(at_n, g + 1)
                for hh in range(2):
                    pe.transpose(ps[:, a + 1, hh * S:hh * S + P], r[:, hh * P:hh * P + P], ident[:, :])
                    pe.transpose(ps[:, a + 1, hh * S + P:hh * S + S], r[:, 256 + hh * S:256 + hh * S + P], ident[:, :])
                    m = pe.transpose(ps[:, a, hh * P:hh * P + P], r[:, 256 + hh * S + P:256 + hh * S + S], ident[:, :])
                m.then_inc(at_t, 1)

            def att_o(g, pt, v):
                a = 4 + 2 * (g % 2)
                pe.wait_ge(at_p0, g + 1)
                pe.wait_ge(at_p1, g + 1)
                for hh in range(2):
                    h = 2 * (g % 4) + hh
                    o = slice(64 * hh, 64 * hh + 64)
                    pe.matmul(ps[o, a, 256:512], v[:, 0, h * 64:h * 64 + 64], pt[:, g % 2, hh * S:hh * S + S],
                              start=True, stop=False, skip_group_check=True)
                    m = pe.matmul(ps[o, a, 384:512], v[:, 1, h * 64:h * 64 + 64], pt[:, g % 2, 512 + hh * P:512 + hh * P + P],
                                  start=False, stop=True, skip_group_check=True)
                m.then_inc(at_o, 1)

            def rot(c):
                evacuated(pe, c)
                pe.matmul(ps[:, 2 + c, :], table("perm64", P), b1["qraw"][:, c % 2, :], start=True, stop=True).then_inc(rot_done, 1)

            def level(l):
                if l <= LEVELS:
                    pe.wait_ge(lv_q, l + 1)
                    pe.wait_ge(lv_k, l + 1)
                K = (lambda par, ht, a: b1["KL"][:, l % 2, par, ht, a]) if l <= LEVELS else (lambda par, ht, a: b1["gkz"][:, par, ht, a])
                Q = (lambda ht, a: b1["QL"][:, l % 2, ht, a]) if l <= LEVELS else (lambda ht, a: b1["gq"][:, ht, a])
                lo_, hi_ = slice(0, P), slice(P, S)
                for i, (ks, qs) in enumerate([(lo_, hi_)] if l == LEVELS else [(lo_, lo_), (hi_, hi_)]):
                    n = (2 * l + i if l < LEVELS else 2 * LEVELS + (0 if l == LEVELS else 1 + i))
                    bank = 2 + i
                    before = {0: n - 2, 1: n - 2}[i] if l <= LEVELS else (15 - 1 if i == 0 else 13)
                    if before >= 0:
                        pe.wait_ge(lv_copied, before + 1)
                    for h in range(4):
                        m = pe.matmul(ps[:, bank, h * P:h * P + P], K(h % 2, h // 2, ks), Q(h // 2, qs), start=True, stop=True)
                    m.then_inc(lv_full, 1)

            def ffn_up(f, c0, x_wait):
                chunk(c0, x_wait=x_wait)
                chunk(c0 + 1)
                with pe.Fori(0, FT // 2 - 1) as i:
                    for v in range(2):
                        chunk(c0 + 2 + v, i=i)

            def down_half(h, rh, rl, i=0, start=False):
                pe.wait_ge(lo_ready, h + 1 + 4 * i)
                for ft in range(KC):
                    wc = slice(ft * P, ft * P + P)
                    m = three(ps[:, 4 + ft // 2, (ft % 2) * S:(ft % 2) * S + S], w_hi[:, slot(h), wc], w_lo[:, slot(h), wc],
                              rh, rl, start and ft % 2 == 0, False)
                m.then_inc(half_used, 1)

            def down_last(h, ah, al, k0, n):
                pe.wait_ge(lo_ready, h + 2)
                for ft in range(KC):
                    wc = slice(ft * P, ft * P + P)
                    for k in range(2):
                        m = three(ps[:, 4 + ft // 2, (ft % 2) * S:(ft % 2) * S + S], w_hi[:, slot(h + k), wc], w_lo[:, slot(h + k), wc],
                                  ah[:, k0 + k, :], al[:, k0 + k, :], False, k == 1)
                    if ft in (1, 3, 5):
                        m.then_inc(down_full, 1)
                    if ft == KC - 1:
                        m.then_inc(half_used, 2)
                    if ft in (5, 6):
                        norm_pair(n, ft - 5)
                norm_pair(n, 2)
                norm_pair(n, 3)

            def ffn_down(f, c0, n):
                h0 = 2 * c0
                pe.wait_ge(act_ready, FT * f + FT - 4)
                down_half(h0, act_hi[:, 0, :], act_lo[:, 0, :], start=True)
                down_half(h0 + 1, act_hi[:, 1, :], act_lo[:, 1, :])
                pe.wait_ge(act_ready, FT * f + FT)
                with pe.Fori(0, 4) as i:
                    for k in range(4):
                        tile = lambda a: a[:, ds(i * 4 + (2 + k), 1), :].rearrange("p a n -> p (a n)")
                        down_half(h0 + 2 + k, tile(act_hi), tile(act_lo), i=i)
                for k in (18, 19):
                    down_half(h0 + k, act_hi[:, k, :], act_lo[:, k, :])
                down_last(h0 + 20, act_hi, act_lo, 20, n)

            pe.wait_ge(consts_ready, 1)
            for p in range(4):
                norm_pair(0, p)
            chunk(0, x_wait=(xl_ready, 0))
            pe.wait_ge(aux_landed, 32)
            for kc in range(KC):
                m = pe.matmul(ps[0:16, 3, 0:S], b1["w_glr"][:, kc * 16:kc * 16 + 16], xn[:, kc, :], start=kc == 0, stop=kc == KC - 1)
            m.then_inc(glr_done, 1)
            chunk(1)
            pe.wait_ge(glr_sb, 1)
            for ht in range(2):
                m = pe.matmul(ps[:, 3, ht * S:ht * S + S], b1["w_gup"][:, ht * P:ht * P + P], b1["glr"][:, :], start=ht == 0, stop=True, skip_group_check=True)
            m.then_inc(gup_done, 1)
            chunk(2)
            chunk(3)
            pe.wait_ge(tab_landed, 16)
            rot(2)
            chunk(4)
            rot(3)
            pe.wait_ge(z_done, 1)
            level(0)
            chunk(5)
            rot(4)
            level(1)
            chunk(6, tokens_out=True, halves=(0,))
            rot(5)
            level(2)
            chunk(6, tokens_out=True, halves=(1,))
            chunk(7, tokens_out=True, halves=(0,))
            level(3)
            chunk(7, tokens_out=True, halves=(1,))
            pe.wait_ge(rope_done, 4)
            att_s(0, b1["qT"], b1["kz"])
            level(4)
            for g in range(4):
                c = 8 + g
                chunk(c, tokens_out=c < 10, halves=(0,))
                if g < 3:
                    att_s(g + 1, b1["qT"], b1["kz"])
                att_t(g, b1["sm1"])
                if g < 3:
                    level(5 + g)
                else:
                    pe.wait_ge(lv_copied, 17)
                    evacuated(pe, 9)
                    for h in range(4):
                        o = (h % 2) * S
                        pe.matmul(ps[:, 2 + h // 2, o:o + S], b1["gv"][:, 0, h * P:h * P + P], b1["AT0"][:, h, :],
                                  start=h % 2 == 0, stop=False, skip_group_check=True)
                        m = pe.matmul(ps[:, 2 + h // 2, o + P:o + S], b1["gv"][:, 1, h * P:h * P + P], b1["AT1"][:, h, :],
                                      start=False, stop=True, skip_group_check=True)
                        if h % 2:
                            m.then_inc(go_full, 1)
                chunk(c, tokens_out=c < 10, halves=(1,))
                if g == 0:
                    evacuated(pe, 7)
                if g == 3:
                    for j in range(2):
                        pe.wait_ge(go_sq, j + 1)
                        pe.matmul(ps[:, 2 + j, :], mean[:, 2, :], b1["g_sd"][:, 2 * j:2 * j + 2, :].rearrange("p a n -> p (a n)"),
                                  start=True, stop=True).then_inc(go_ss, 1)
                att_o(g, b1["pt1"], b1["mv"])
                if g == 2:
                    level(8)
            pe.wait_ge(at_y, 4)
            for k in range(6):
                if k == 4:
                    pe.wait_ge(yg_ready, 2)
                down_half(2 * C_OUT1 + k, b1["yh1"][:, k, :], b1["yl1"][:, k, :], start=k == 0)
            down_last(2 * C_OUT1 + 6, b1["yh1"], b1["yl1"], 6, 1)
            ffn_up(0, C_UP[0], (xl_ready, 4))
            ffn_down(0, C_DN[0], 2)
            pe.wait_ge(gmean_ready, 1)
            for p in range(4):
                norm_pair(3, p, bank=3, gain=True)
            ffn_up(1, C_UP[1], (xl_ready, 8))
            ffn_down(1, C_DN[1], 4)
            chunk(C_IN2, x_wait=(xl_ready, 12))
            chunk(C_IN2 + 1)
            chunk(C_IN2 + 2)
            pe.wait_ge(lat_sq, 1)
            for j in range(3):
                m = pe.matmul(ps[:, 2, (j // 2) * S:(j // 2) * S + S], mean[:, 1 + j // 2, :], b2["latsq"][:, j, :],
                              start=j == 0, stop=j >= 1, skip_group_check=True)
            m.then_inc(lat_ss, 1)
            chunk(C_IN2 + 3)
            evacuated(pe, bank_use(C_IN2 + 1))
            pe.matmul(ps[:, 3, 0:S], table("perm32", P), b2["kpr"][:, :], start=True, stop=True).then_inc(pe_rot, 1)
            chunk(C_IN2 + 4)
            chunk(C_IN2 + 5)
            h = 2 * C_UQ
            pe.wait_ge(lat_ready2, 1)
            pe.wait_ge(lo_ready, h + 2)
            for j in range(5):
                u = bank_use(C_UQ) + j
                pe.wait_ge(bank_free[u % 2], u // 2)
                for f in range(2):
                    o = ps[:, u % 2, f * S:f * S + S]
                    if j < 3:
                        wc = slice((2 * j + f) * P, (2 * j + f) * P + P)
                        three(o, w_hi[:, slot(h), wc], w_lo[:, slot(h), wc], b2["cqh"][:, 0, :], b2["cql"][:, 0, :], f == 0, False)
                        m = three(o, w_hi[:, slot(h + 1), wc], w_lo[:, slot(h + 1), wc], b2["cqh"][:, 1, :], b2["cql"][:, 1, :], False, True)
                    else:
                        s_ = slot(h + j - 3)
                        wc = slice(768 + f * P, 768 + f * P + P)
                        m = three(o, w_hi[:, s_, wc], w_lo[:, s_, wc], b2["cqh"][:, 2, :], b2["cql"][:, 2, :], f == 0, True)
                m.then_inc(*((uq_full, 1) if j < 4 else (half_used, 2)))
            pe.wait_ge(lo_ready, h + 3)
            u = bank_use(C_UV)
            for j in range(2):
                pe.wait_ge(bank_free[(u + j) % 2], (u + j) // 2)
                a = slice(j * P, j * P + P)
                o = ps[:, (u + j) % 2, :]
                s_ = slot(h + 2)
                pe.matmul(o, b2["cqh"][:, 2, a], w_hi[:, s_, 0:512], start=True, stop=False)
                pe.matmul(o, b2["cql"][:, 2, a], w_hi[:, s_, 0:512], start=False, stop=False)
                m = pe.matmul(o, b2["cqh"][:, 2, a], w_lo[:, s_, 0:512], start=False, stop=True)
                m.then_inc(*((uq_full, 1) if j < 1 else (half_used, 2)))
            def mla_s(g):
                att_s(g, b2["qn"], b2["nz"], b2["qpe"], b2["kpz"])

            def ca_s(g):
                att_s(g, b2["caq"], b2["caz"])

            def s2(g):
                (mla_s if g < 8 else ca_s)(g)

            def o2(g):
                att_o(g, b2["pt2"], b2["v2"] if g < 8 else b2["cav"])

            chunk(C_CAV, tokens_out=True, halves=(0,))
            evacuated(pe, bank_use(C_UQ) + 2)
            pe.wait_ge(pe_done, 1)
            pe.matmul(ps[:, 3, :], table("perm32", P), b2["qpr"][:, :], start=True, stop=True).then_inc(pe_rot, 1)
            chunk(C_CAV, tokens_out=True, halves=(1,))
            chunk(C_CAV + 1, tokens_out=True, halves=(0,))
            pe.wait_ge(pe_done, 2)
            evacuated(pe, bank_use(C_UQ) + 3)
            evacuated(pe, bank_use(C_UQ) + 4)
            s2(4)
            chunk(C_CAV + 1, tokens_out=True, halves=(1,))
            for c in range(8):
                g = 4 + c
                chunk(C_GATE + c, halves=(0,))
                if g < 11:
                    s2(g + 1)
                att_t(g, b2["sm2"])
                chunk(C_GATE + c, halves=(1,))
                if c == 0:
                    evacuated(pe, bank_use(C_CAV))
                    evacuated(pe, bank_use(C_CAV + 1))
                o2(g)
            for n in range(4):
                br, c = n // 2, C_BR + n
                if n % 2 == 0:
                    pe.wait_ge(at_y, 8 + 4 * br)
                if n == 0:
                    evacuated(pe, bank_use(C_GATE + 6))
                    evacuated(pe, bank_use(C_GATE + 7))
                if n >= 2:
                    pe.wait_ge(br_used, 2 * (n - 1))
                for half in range(2):
                    h = 2 * c + half
                    pe.wait_ge(lo_ready, h + 1)
                    for k in range(2):
                        for f in range(4):
                            wc = slice(k * 512 + f * P, k * 512 + f * P + P)
                            kk = 4 * br + 2 * half + k
                            m = three(ps[:, 2 * (n % 2) + f // 2, (f % 2) * S:(f % 2) * S + S], w_hi[:, slot(h), wc], w_lo[:, slot(h), wc],
                                      b2["yh2"][:, kk, :], b2["yl2"][:, kk, :], half == 0 and k == 0 and f % 2 == 0, half == 1 and k == 1)
                    m.then_inc(half_used, 1)
            for k in range(6):
                if k % 2 == 0:
                    pe.wait_ge(ml_ready, k // 2 + 1)
                down_half(2 * C_OUT2 + k, xh[:, k, :], xl[:, k, :], start=k == 0)
            pe.wait_ge(ml_ready, 4)
            down_last(2 * C_OUT2 + 6, xh, xl, 6, 5)
            ffn_up(2, C_UP[2], (xl_ready, 16))
            ffn_down(2, C_DN[2], 6)

        @block.scalar
        def _(act):
            own = Own(act, own_act)
            f = nc.scalar.activation

            act.dma_start(cols[:, :], cols_in).then_inc(cols_landed, 16)
            act.dma_start(b1["posi"][:, :], pos_in.to_broadcast([P, S])).then_inc(pos_landed, 16)
            act.dma_start(b1["w_glr"][:, :], glr_in).then_inc(aux_landed, 16)
            act.dma_start(b1["w_gup"][:, :], gup_in).then_inc(aux_landed, 16)
            act.dma_start(tab[:, :], tab_in).then_inc(tab_landed, 16)
            act.dma_start(b1["gmask"][:, :, :], gmask_in).then_inc(gmask_landed, 16)

            def hi(c, i=0, halves=(0, 1)):
                for half in halves:
                    h = 2 * c + half
                    act.wait_ge(raw_landed[slot(h)], (i + (h // NSLOT + 1)) * 16)
                    if not (isinstance(i, int) and h + 4 * i < NSLOT):
                        act.wait_ge(half_used, h - NSLOT + 1 + 4 * i)
                    f(w_hi[:, slot(h), :], raw[:, slot(h), :], ACT.Copy).then_inc(hi_ready, 1)

            def squares(resid):
                for p in range(4):
                    if resid is None:
                        act.wait_ge(x_landed[p // 2], 16)
                    else:
                        act.wait_ge(resid_done, resid + p + 1)
                    f(pair(xn, p), pair(X, p), ACT.Square).then_inc(sq_done, 1)
                act.wait_ge(consts_ready, 1)
                f(epsc[:, 2:3], epsc[:, 0:1], ACT.Sqrt)

            def root(n):
                act.wait_ge(ss_done, n + 1)
                f(sd[:, 0, :], ps[:, 2, 0:S], ACT.Sqrt, bias=epsc[:, 0:1]).then_inc(sd_done, 1)

            def norm_hi(m):
                for p in range(4):
                    act.wait_ge(xt_ready, 4 * m + p + 1)
                    f(pair(xh, p), pair(xn, p), ACT.Copy).then_inc(xh_ready, 1)

            def norm_mod_hi(m, sub):
                act.wait_ge(mod_ready, 1 if sub == 0 else 2)
                for p in range(4):
                    act.wait_ge(xt_ready, 4 * m + p + 1)
                    if p:
                        for k in (2 * p, 2 * p + 1):
                            ins = f(xn[:, k, :], xn[:, k, :], ACT.Identity, scale=modA[:, sub, k:k + 1], bias=mod[:, sub, k:k + 1])
                        own.mark(ins)
                        own.wait()
                    f(pair(xh, p), pair(xn, p), ACT.Copy).then_inc(xh_ready, 1)

            def full(c):
                act.wait_ge(half_used, 2 * c + 2)
                return bank_use(c) % 2

            def bank2(b):
                return ps[:, b, :].rearrange("p (a n) -> p a n", a=2)

            def trig():
                act.wait_ge(trig_red, 1)
                f(sin2[:, :], b1["trig"][:, 0, :], ACT.Sin)
                f(cos2[:, :], b1["trig"][:, 1, :], ACT.Sin).then_inc(trig_done, 1)

            def att_exp(g, sm, st):
                act.wait_ge(at_m, g + 1)
                r = sm[:, g % 2, :]
                for j in range(4):
                    a = slice(j * P, j * P + P) if j < 2 else slice(256 + (j - 2) * S, 256 + (j - 2) * S + S)
                    ins = f(r[:, a], r[:, a], ACT.Exp, bias=st[:, g % 2, 0, j:j + 1], accum_out=st[:, g % 2, 1, j:j + 1])
                ins.then_inc(at_e, 1)

            def att_pt(g, pt):
                act.wait_ge(at_t, g + 1)
                f(pt[:, g % 2, 0:512], ps[:, 5 + 2 * (g % 2), :], ACT.Copy).then_inc(at_p0, 1)

            def att_yh(g, yh, k):
                act.wait_ge(at_o, g + 1)
                f(yh[:, k, :], ps[:, 4 + 2 * (g % 2), 256:512], ACT.Copy).then_inc(at_yh, 1)

            def padded(dst, k, b):
                f(dst[0:64, 0, k:k + 2, :], bank2(b)[0:64, :, :], ACT.Copy)
                return f(dst[64:P, 1, k:k + 2, :], bank2(b)[64:P, :, :], ACT.Copy)

            def level_e(l):
                act.wait_ge(lv_d, l + 1)
                own.mark(f(b1["E"][:, l % 2, :, :], b1["E"][:, l % 2, :, :], ACT.Abs))
                own.wait()
                f(b1["E"][:, l % 2, :, :], b1["E"][:, l % 2, :, :], ACT.Exp, scale=-1.0 / 16).then_inc(lv_e, 1)

            def up_step(conv, fi, c, j, i=0):
                u = bank_use(c)
                b = u % 2
                v = j % 2
                act.wait_ge(half_used, 2 * c + 2 + 4 * i)
                n = FT * fi + j + 1 + 2 * i
                if conv:
                    if j >= 2:
                        act.wait_ge(act_ready, n - 2)
                    for t2 in range(2):
                        jj = j + FT * t2
                        wcol = cols[:, ds(i * 2 + (COL["conv_w"] + 2 * 44 + jj), 1)]
                        bcol = cols[:, ds(i * 2 + (COL["conv_b"] + jj), 1)]
                        ins = f(cv[:, v, t2, :], ps[:, b, t2 * S:t2 * S + S], ACT.Identity, scale=wcol, bias=bcol)
                    ins.then_inc(cv_base, 1)
                    hi(c + 2, i=i)
                    act.wait_ge(cv_gate, n)
                    f(sg[:, v, :], cv[:, v, 0, :], ACT.Silu).then_inc(sg_done, 1)
                else:
                    f(sg[:, v, :], ps[:, b, 0:S], ACT.Silu).then_inc(sg_done, 1)
                    hi(c + 2, i=i)

            def ada_sum(base, n, i=0):
                n = base + n
                act.wait_ge(ada_mult, i + (n + 1))
                if n >= 2:
                    act.wait_ge(ada_moved, i + (n - 1))
                f(ada_mul[:, n % 2, :], ada_mul[:, n % 2, :], ACT.Copy, accum_out=ada_col[:, n % 2:n % 2 + 1]).then_inc(ada_used, 1)

            def gain_means():
                own.mark(f(gsq[:, :], cols[:, COL["fin1_g"]:COL["fin1_g"] + KC], ACT.Square))
                own.wait()
                for k in range(KC):
                    ins = f(gmean[:, k, :], mean[:, 0, :], ACT.Copy, scale=gsq[:, k:k + 1])
                ins.then_inc(gmean_ready, 1)

            def ffn_up(fi, c0, ada=None):
                conv = fi == 0
                hi(c0 + 1)
                for j in range(2):
                    up_step(conv, fi, c0 + j, j)
                    if fi == 0 and j == 0:
                        gain_means()
                    if ada is not None:
                        ada_sum(ada, j)
                with act.Fori(0, FT // 2 - 1) as i:
                    for v in range(2):
                        up_step(conv, fi, c0 + 2 + v, 2 + v, i=i)
                        if ada is not None:
                            ada_sum(ada, 2 + v, i * 2)

            def ffn_down(c0, last=False, ada=None):
                if ada is not None:
                    ada_sum(ada, FT)
                with act.Fori(0, 2) as i:
                    for v in range(4):
                        hi(c0 + 2 + v, i=i * 2)
                        if ada is not None:
                            for k in ((0, 1), (2,), (3, 4), (5,))[v]:
                                ada_sum(ada, FT + 1 + k, i * 6)
                hi(c0 + 10)
                if ada is not None:
                    ada_sum(ada, FT + 13)
                if not last:
                    hi(c0 + 11)

            squares(None)
            hi(0)
            root(0)
            hi(1)
            norm_hi(0)
            f(b1["gq"][:, :, :], bank2(full(0)), ACT.Copy, scale=0.125).then_inc(bank_free[0], 1)
            hi(2)
            act.wait_ge(pool_zero, 1)
            act.wait_ge(glr_done, 1)
            f(b1["glr"][0:16, :], ps[0:16, 3, 0:S], ACT.Copy).then_inc(glr_sb, 1)
            act.wait_ge(pool_zero, 2)
            padded(b1["gkz"], 0, full(1)).then_inc(bank_free[1], 1)
            act.wait_ge(cols_landed, 16)
            act.wait_ge(gup_done, 1)
            for ht in range(2):
                ins = f(b1["QL"][:, 0, ht, :], ps[:, 3, ht * S:ht * S + S], ACT.Identity, bias=col("b_gate", ht))
            ins.then_inc(z_done, 1)
            act.wait_ge(z_done, 1)
            own.mark(f(b1["KL"][:, 0, 0, :, :], b1["QL"][:, 0, :, :], ACT.Abs))
            own.wait()
            own.mark(f(b1["KL"][:, 0, 0, :, :], b1["KL"][:, 0, 0, :, :], ACT.Exp, scale=-1.0))
            own.wait()
            f(b1["KL"][:, 0, 1, :, :], b1["KL"][:, 0, 0, :, :], ACT.Ln, bias=1.0).then_inc(ls_done, 1)
            hi(3)

            def qraw(c):
                b = full(c)
                if c >= 4:
                    act.wait_ge(rope_done, c - 3)
                f(b1["qraw"][:, c % 2, :], ps[:, b, :], ACT.Copy).then_inc(bank_free[b], 1)

            def vals(dst, c, cc):
                b = full(c)
                f(dst[:, :, cc * 256:cc * 256 + 256], bank2(b), ACT.Copy).then_inc(bank_free[b], 1)

            def gr_evac(c, cc):
                b = full(c)
                f(b1["gr"][:, 2 * cc:2 * cc + 2, :], bank2(b), ACT.Copy).then_inc(bank_free[b], 1)

            sm1, st1, pt1, yh1 = b1["sm1"], b1["st1"], b1["pt1"], b1["yh1"]
            for c in range(2, 6):
                qraw(c)
                hi(c + 2)
                level_e(c - 2)
            vals(b1["mv"], 6, 0)
            hi(8)
            vals(b1["mv"], 7, 1)
            level_e(4)
            att_exp(0, sm1, st1)
            level_e(5)
            for g in range(4):
                c = 8 + g
                hi(c + 1, halves=(0,))
                att_pt(g, pt1)
                hi(c + 1, halves=(1,))
                if g < 3:
                    att_exp(g + 1, sm1, st1)
                if g < 2:
                    level_e(6 + g)
                if g == 3:
                    for j in range(2):
                        act.wait_ge(go_full, j + 1)
                        f(b1["og"][:, 2 * j:2 * j + 2, :], bank2(2 + j), ACT.Copy)
                        f(b1["g_sd"][:, 2 * j:2 * j + 2, :], bank2(2 + j), ACT.Square).then_inc(go_sq, 1)
                    for j in range(2):
                        act.wait_ge(go_ss, j + 1)
                        f(b1["g_sd"][:, 2 * j:2 * j + 2, :], bank2(2 + j), ACT.Sqrt, bias=epsc[:, 0:1]).then_inc(go_sd, 1)
                att_yh(g, yh1, g)
                if g == 3:
                    hi(C_OUT1 + 1, halves=(0,))
                if g < 2:
                    vals(b1["gv"], c, g)
                else:
                    gr_evac(c, g - 2)
            act.wait_ge(bank_free[1], 6)
            f(b1["gr"][:, :, :], b1["gr"][:, :, :], ACT.Silu).then_inc(gr_silu, 1)
            hi(C_OUT1 + 1, halves=(1,))
            for j in range(2):
                act.wait_ge(go_v, j + 1)
                f(b1["yh1"][:, 4 + 2 * j:6 + 2 * j, :], b1["og"][:, 2 * j:2 * j + 2, :], ACT.Copy).then_inc(yg_hi, 1)
            hi(C_OUT1 + 2)
            hi(C_OUT1 + 3)
            trig()
            hi(C_OUT1 + 4)
            squares(0)
            root(1)
            norm_hi(1)
            act.wait_ge(c_landed, 16)
            f(cact[:, :], cact[:, :], ACT.Silu).then_inc(cact_ready, 1)
            ffn_up(0, C_UP[0], ada=0)
            ffn_down(C_DN[0], ada=0)
            squares(4)
            act.wait_ge(eps_mixed, 1)
            f(sd[:, 1, :], sd[:, 1, :], ACT.Sqrt, bias=epsc[:, 1:2]).then_inc(sd_done, 1)
            root(2)
            norm_mod_hi(2, 0)
            ffn_up(1, C_UP[1], ada=NADA // 2)
            ffn_down(C_DN[1], ada=NADA // 2)
            squares(8)
            root(4)
            norm_mod_hi(3, 1)
            hi(C_IN2 + 1)
            b = full(C_IN2)
            f(b2["lat"][:, 0:2, :], bank2(b), ACT.Copy)
            f(b2["latsq"][:, 0:2, :], bank2(b), ACT.Square).then_inc(bank_free[b], 1)
            hi(C_IN2 + 2)
            b = full(C_IN2 + 1)
            f(b2["lat"][:, 2, :], ps[:, b, 0:S], ACT.Copy)
            f(b2["latsq"][:, 2, :], ps[:, b, 0:S], ACT.Square).then_inc(lat_sq, 1)
            f(b2["kpr"][:, :], ps[:, b, S:2 * S], ACT.Copy).then_inc(bank_free[b], 1)
            hi(C_IN2 + 3)
            b = full(C_IN2 + 2)
            f(b2["caq"][:, 0:2, :], bank2(b), ACT.Copy).then_inc(bank_free[b], 1)
            act.wait_ge(lat_ss, 1)
            f(b2["l_sd"][:, :, :], bank2(2), ACT.Sqrt, bias=epsc[:, 0:1]).then_inc(lat_sd, 1)
            hi(C_IN2 + 4)
            b = full(C_IN2 + 3)
            f(b2["caq"][:, 2:4, :], bank2(b), ACT.Copy).then_inc(bank_free[b], 1)
            act.wait_ge(lat_v, 1)
            f(b2["cqh"][:, :, :], b2["lat"][:, :, :], ACT.Copy).then_inc(lat_hi, 1)
            act.wait_ge(pool_zero, 8)
            for j in range(2):
                hi(C_IN2 + 5 + j)
                b = full(C_IN2 + 4 + j)
                padded(b2["caz"], 2 * j, b).then_inc(bank_free[b], 1)
            hi(C_UV)
            u0 = bank_use(C_UQ)
            for j in range(5):
                b = (u0 + j) % 2
                if j < 4:
                    act.wait_ge(uq_full, j + 1)
                else:
                    full(C_UQ)
                if j < 2:
                    f(b2["qn"][:, 2 * j:2 * j + 2, :], bank2(b), ACT.Copy).then_inc(bank_free[b], 1)
                elif j == 2:
                    f(b2["qpr"][:, :], ps[:, b, :], ACT.Copy).then_inc(bank_free[b], 1)
                else:
                    padded(b2["nz"], 2 * (j - 3), b).then_inc(bank_free[b], 1)
            hi(C_CAV)
            u0 = bank_use(C_UV)
            for j in range(2):
                b = (u0 + j) % 2
                if j == 0:
                    act.wait_ge(uq_full, 5)
                else:
                    full(C_UV)
                f(b2["v2"][:, j, :], ps[:, b, :], ACT.Copy).then_inc(bank_free[b], 1)
            hi(C_CAV + 1)
            vals(b2["cav"], C_CAV, 0)
            hi(C_GATE)
            att_exp(4, b2["sm2"], b2["st2"])
            vals(b2["cav"], C_CAV + 1, 1)
            for c in range(8):
                g = 4 + c
                hi(C_GATE + c + 1, halves=(0,))
                att_pt(g, b2["pt2"])
                hi(C_GATE + c + 1, halves=(1,))
                if g < 11:
                    att_exp(g + 1, b2["sm2"], b2["st2"])
                att_yh(g, b2["yh2"], c)
                b = full(C_GATE + c)
                f(b2["th"][:, 2 * c:2 * c + 2, :], bank2(b), ACT.Tanh, scale=0.5).then_inc(bank_free[b], 1)
            for c in range(4):
                hi(C_BR + c + 1)
            for p in range(4):
                act.wait_ge(br_done, p + 1)
                f(pair(xh, p), pair(xn, p), ACT.Copy).then_inc(mh_ready, 1)
                if p == 1:
                    hi(C_OUT2 + 1)
            for c in range(1, 4):
                hi(C_OUT2 + c + 1)
            squares(12)
            root(5)
            norm_mod_hi(4, 2)
            ffn_up(2, C_UP[2])
            ffn_down(C_DN[2], last=True)
            squares(16)
            root(6)

        @block.vector
        def _(dve):
            own = Own(dve, own_dve)
            v = nc.vector

            def lo(c, i=0, halves=(0, 1)):
                for half in halves:
                    h = 2 * c + half
                    dve.wait_ge(hi_ready, h + 1 + 4 * i)
                    v.tensor_tensor(w_lo[:, slot(h), :], raw[:, slot(h), :], w_hi[:, slot(h), :].bitcast(F32), ALU.subtract).then_inc(lo_ready, 1)

            def rstd_of(n, k=0):
                dve.wait_ge(sd_done, n + 1)
                v.reciprocal(rstd[:, :], sd[:, k, :]).then_inc(rstd_done, 1)
                dve.wait_ge(rstd_done, n + 1)

            def norm_plain(n, m, gain):
                rstd_of(n)
                if n == 0:
                    dve.wait_ge(cols_landed, 16)
                for p in range(4):
                    for k in (2 * p, 2 * p + 1):
                        ins = v.scalar_tensor_tensor(out=xn[:, k, :], in0=X[:, k, :], scalar=col(gain, k), in1=rstd[:, :], op0=ALU.mult, op1=ALU.mult)
                    ins.then_inc(xt_ready, 1)
                    if p:
                        norm_lo(m, p - 1)
                norm_lo(m, 3)

            def norm_lo(m, p):
                dve.wait_ge(xh_ready, 4 * m + p + 1)
                v.tensor_tensor(pair(xl, p), pair(xn, p), pair(xh, p).bitcast(F32), ALU.subtract).then_inc(xl_ready, 1)

            def norm_in_place(n, gain):
                rstd_of(n)
                for p in range(4):
                    for k in (2 * p, 2 * p + 1):
                        ins = v.scalar_tensor_tensor(out=X[:, k, :], in0=X[:, k, :], scalar=col(gain, k), in1=rstd[:, :], op0=ALU.mult, op1=ALU.mult)
                    ins.then_inc(resid_done, 1)

            def norm_mod(n, m, sub, twice=False):
                if twice:
                    dve.wait_ge(ss_done, n + 2)
                    own.mark(v.tensor_scalar(sd[:, 1, :], ps[:, 2, 0:S], EPS, None, ALU.mult))
                    own.wait()
                    v.tensor_tensor(sd[:, 1, :], ps[:, 3, 0:S], sd[:, 1, :], ALU.add).then_inc(eps_mixed, 1)
                rstd_of(n, 1 if twice else 0)
                own.mark(v.tensor_tensor(pair(xn, 0), pair(X, 0), over(rstd[:, :], 2), ALU.mult))
                own.wait()
                for k in range(2):
                    ins = v.tensor_scalar(xn[:, k, :], xn[:, k, :], modA[:, sub, k:k + 1], mod[:, sub, k:k + 1], ALU.mult, ALU.add)
                ins.then_inc(xt_ready, 1)
                for p in range(1, 4):
                    v.tensor_tensor(pair(xn, p), pair(X, p), over(rstd[:, :], 2), ALU.mult).then_inc(xt_ready, 1)
                    norm_lo(m, p - 1)
                norm_lo(m, 3)

            def fin1_residual():
                rstd_of(3)
                for k in range(KC):
                    v.scalar_tensor_tensor(out=X[:, k, :], in0=X[:, k, :], scalar=col("fin1_g", k), in1=rstd[:, :], op0=ALU.mult, op1=ALU.mult)

            def full(c):
                dve.wait_ge(half_used, 2 * c + 2)
                return bank_use(c) % 2

            def out_down(n, c0, gate=None, start=1):
                for c in range(start, 4):
                    lo(c0 + c)
                lo(c0 + 4)
                add_down(n, c0 + 4, gate)

            def add_down(n, c_end, gate):
                for p in range(4):
                    if p < 3:
                        dve.wait_ge(down_full, 3 * n + p + 1)
                    else:
                        dve.wait_ge(half_used, 2 * c_end)
                    ins = add_pair(4 + p, p) if gate is None else gated_pair(4 + p, p, gate)
                    ins.then_inc(resid_done, 1)

            def add_pair(b, p):
                return v.tensor_tensor(pair(X, p), ps[:, b, :].rearrange("p (a n) -> p a n", a=2), pair(X, p), ALU.add)

            def gated_pair(b, p, gate):
                for k in (2 * p, 2 * p + 1):
                    ins = v.scalar_tensor_tensor(out=X[:, k, :], in0=ps[:, b, (k % 2) * S:(k % 2) * S + S], scalar=mod[:, gate, 16 + k:17 + k],
                                                 in1=X[:, k, :], op0=ALU.mult, op1=ALU.add)
                return ins

            def rope_trig():
                tr, pos = b1["trig"], b1["posi"]
                magic = 12582912.0
                c1, c2 = 6.28125, 0.0019340515136718750
                c3 = 2 * np.pi - c1 - c2
                dve.wait_ge(pos_landed, 16)
                dve.wait_ge(cols_landed, 16)
                ang, kf = b1["rt"][:, 0, 0:S], b1["rt"][:, 0, S:2 * S]
                own.mark(v.tensor_copy(ang, pos[:, :]))
                own.wait()
                own.mark(v.tensor_scalar(ang, ang, col("freq"), None, ALU.mult))
                own.wait()
                for j, off in enumerate((0.0, 0.25)):
                    own.mark(v.tensor_scalar(kf, ang, float(1 / (2 * np.pi)), off, ALU.mult, ALU.add))
                    own.wait()
                    own.mark(v.tensor_scalar(kf, kf, magic, None, ALU.add))
                    own.wait()
                    own.mark(v.tensor_scalar(kf, kf, magic, None, ALU.subtract))
                    own.wait()
                    r = tr[:, j, :]
                    own.mark(v.scalar_tensor_tensor(out=r, in0=kf, scalar=-c1, in1=ang, op0=ALU.mult, op1=ALU.add))
                    own.wait()
                    own.mark(v.scalar_tensor_tensor(out=r, in0=kf, scalar=-c2, in1=r, op0=ALU.mult, op1=ALU.add))
                    own.wait()
                    own.mark(v.scalar_tensor_tensor(out=r, in0=kf, scalar=-float(c3), in1=r, op0=ALU.mult, op1=ALU.add))
                    own.wait()
                    if j:
                        own.mark(v.tensor_scalar(r, r, float(np.pi / 2), None, ALU.add))
                        own.wait()
                    ins = v.tensor_scalar(r, r, 3.1415925, -3.1415925, ALU.min, ALU.max)
                ins.then_inc(trig_red, 1)

            def rope(c):
                evacuated(dve, c)
                rt = b1["rt"]
                if c == 2:
                    dve.wait_ge(tab_landed, 16)
                else:
                    dve.wait_ge(rope_done, c - 2)
                two = lambda ap: ap.rearrange("p (a n) -> p a n", a=2)
                v.tensor_tensor(two(rt[:, 0, :]), two(b1["qraw"][:, c % 2, :]), over(table("cos", S), 2), ALU.mult)
                dve.wait_ge(rot_done, c - 1)
                own.mark(v.tensor_tensor(two(rt[:, 1, :]), two(ps[:, 2 + c, :]), over(table("sin", S), 2), ALU.mult))
                own.wait()
                if c < 4:
                    v.tensor_tensor(b1["qT"][:, 2 * (c - 2):2 * (c - 1), :], two(rt[:, 0, :]), two(rt[:, 1, :]), ALU.add).then_inc(rope_done, 1)
                else:
                    dve.wait_ge(pool_zero, 3)
                    for par in range(2):
                        a = slice(64 * par, 64 * par + 64)
                        ins = v.tensor_tensor(b1["kz"][a, par, 2 * (c - 4):2 * (c - 3), :], two(rt[a, 0, :]), two(rt[a, 1, :]), ALU.add)
                    ins.then_inc(rope_done, 1)

            def att_mask(g, sm, st, scale, mask):
                a = 4 + 2 * (g % 2)
                r = sm[:, g % 2, :]
                s = st[:, g % 2, 0, :]
                dve.wait_ge(at_s, g + 1)
                s0 = r[:, 0:256].rearrange("p (a n) -> p a n", a=2)
                s1 = r[:, 256:768].rearrange("p (a n) -> p a n", a=2)
                v.scalar_tensor_tensor(out=s0, in0=ps[:, a, 0:256].rearrange("p (a n) -> p a n", a=2), scalar=scale, in1=mask(P, S),
                                       op0=ALU.mult, op1=ALU.add)
                own.mark(v.scalar_tensor_tensor(out=s1, in0=ps[:, a + 1, :].rearrange("p (a n) -> p a n", a=2), scalar=scale, in1=mask(0, S),
                                                op0=ALU.mult, op1=ALU.add))
                own.wait()
                v.tensor_reduce(s[:, 0:2], s0, AX.X, ALU.max, negate=True)
                v.tensor_reduce(s[:, 2:4], s1, AX.X, ALU.max, negate=True).then_inc(at_m, 1)

            def att_norm(g, sm, st):
                r = sm[:, g % 2, :]
                dve.wait_ge(at_e, g + 1)
                own.mark(v.reciprocal(st[:, g % 2, 2, :], st[:, g % 2, 1, :]))
                own.wait()
                for j in range(4):
                    a = slice(j * P, j * P + P) if j < 2 else slice(256 + (j - 2) * S, 256 + (j - 2) * S + S)
                    ins = v.tensor_scalar(r[:, a], r[:, a], st[:, g % 2, 2, j:j + 1], None, ALU.mult)
                ins.then_inc(at_n, 1)

            def att_pt(g, pt):
                dve.wait_ge(at_t, g + 1)
                v.tensor_copy(pt[:, g % 2, 512:768], ps[:, 4 + 2 * (g % 2), 0:256]).then_inc(at_p1, 1)

            def att_y(g, yh, yl, k):
                dve.wait_ge(at_yh, g + 1)
                v.tensor_tensor(yl[:, k, :], ps[:, 4 + 2 * (g % 2), 256:512], yh[:, k, :].bitcast(F32), ALU.subtract).then_inc(at_y, 1)

            causal = lambda a, b: over(table("causal", S)[:, a:b], 2)
            chunked = lambda a, b: over(table("chunked", S)[:, a:b], 2)

            def level_d(l):
                if l >= 2:
                    dve.wait_ge(lv_k, l - 1)
                    dve.wait_ge(lv_q, l - 1)
                p = 1 << l
                G = b1["G"][:, :, :].rearrange("p a (m q) -> p (a m) q", q=2 * p)
                E = b1["E"][:, l % 2, :, :].rearrange("p a (m q) -> p (a m) q", q=2 * p)
                ref = G[:, :, p - 1:p].to_broadcast([P, 2 * S // (2 * p), 2 * p])
                v.tensor_tensor(E, G, ref, ALU.subtract).then_inc(lv_d, 1)

            def level_q(l):
                dve.wait_ge(lv_e, l + 1)
                if l >= 2:
                    dve.wait_ge(lv_full, 2 * (l - 1))
                v.tensor_tensor(b1["QL"][:, l % 2, :, :], b1["gq"][:, :, :], b1["E"][:, l % 2, :, :], ALU.mult).then_inc(lv_q, 1)

            def level_copy(l):
                if l == 0:
                    dve.wait_ge(pool_zero, 5)
                    dve.wait_ge(gmask_landed, 16)
                for i in range(1 if l == LEVELS else 2):
                    n = 2 * l + i if l <= LEVELS else 2 * LEVELS + 1 + i
                    dve.wait_ge(lv_full, n + 1)
                    if n >= 2:
                        dve.wait_ge(lv_copied, n - 1)
                    src = ps[:, 2 + i, :].rearrange("p (h n) -> p h n", h=4)
                    if l == LEVELS:
                        v.tensor_copy(b1["AT0"][:, :, P:S], src).then_inc(lv_copied, 1)
                    else:
                        dst = b1["AT0"][:, :, 0:P] if i == 0 else b1["AT1"][:, :, :]
                        v.copy_predicated(dst, over(b1["gmask"][:, l if l < LEVELS else LEVELS, :], 4), src).then_inc(lv_copied, 1)

            def up_step(conv, fi, c, j, i=0):
                u = bank_use(c)
                b = u % 2
                vv = j % 2
                n = FT * fi + j + 1 + 2 * i
                if conv:
                    dve.wait_ge(cv_base, n)
                    src = lambda t2, k: ps[:, b, t2 * S:t2 * S + S - k]
                    tap = lambda t2, k: cols[:, ds(i * 2 + (COL["conv_w"] + 44 * (2 - k) + j + FT * t2), 1)]
                    y = lambda t2, k: cv[:, vv, t2, k:S]
                    for t2 in range(2):
                        v.scalar_tensor_tensor(out=y(t2, 1), in0=src(t2, 1), scalar=tap(t2, 1), in1=y(t2, 1), op0=ALU.mult, op1=ALU.add).then_inc(cv_own, 1)
                    for t2 in range(2):
                        dve.wait_ge(cv_own, 3 * (j + 1) + 6 * i - 2 + t2)
                        ins = v.scalar_tensor_tensor(out=y(t2, 2), in0=src(t2, 2), scalar=tap(t2, 2), in1=y(t2, 2), op0=ALU.mult, op1=ALU.add)
                        ins.then_inc(cv_gate if t2 == 0 else bank_free[b], 1)
                    lo(c + 2, i=i, halves=(0,))
                    dve.wait_ge(bank_free[b], u // 2 + 1 + i)
                    dve.wait_ge(sg_done, n)
                    v.tensor_tensor(av[:, vv, :], sg[:, vv, :], cv[:, vv, 1, :], ALU.mult).then_inc(cv_own, 1)
                    lo(c + 2, i=i, halves=(1,))
                    dve.wait_ge(cv_own, 3 * (j + 1) + 6 * i)
                else:
                    dve.wait_ge(sg_done, n)
                    if j >= 2:
                        dve.wait_ge(act_ready, n - 2)
                    v.tensor_tensor(av[:, vv, :], sg[:, vv, :], ps[:, b, S:2 * S], ALU.mult).then_inc(bank_free[b], 1)
                    lo(c + 2, i=i)
                    dve.wait_ge(bank_free[b], u // 2 + 1 + i)
                ah = act_hi[:, ds(i * 2 + j, 1), :].rearrange("p a n -> p (a n)")
                al = act_lo[:, ds(i * 2 + j, 1), :].rearrange("p a n -> p (a n)")
                v.tensor_copy(ah, av[:, vv, :]).then_inc(ah_done, 1)
                dve.wait_ge(ah_done, n)
                v.tensor_tensor(al, av[:, vv, :], ah.bitcast(F32), ALU.subtract).then_inc(act_ready, 1)

            def ffn_up(fi, c0, residual=None):
                conv = fi == 0
                lo(c0 + 1)
                for j in range(2):
                    up_step(conv, fi, c0 + j, j)
                    if j == 0 and residual:
                        residual()
                with dve.Fori(0, FT // 2 - 1) as i:
                    for vv in range(2):
                        up_step(conv, fi, c0 + 2 + vv, 2 + vv, i=i)

            def ffn_down(n, c0, mod=None, gate=None, last=False):
                with dve.Fori(0, 4) as i:
                    for vv in range(2):
                        lo(c0 + 2 + vv, i=i)
                lo(c0 + 10)
                if not last:
                    lo(c0 + 11)
                if mod:
                    ada_mod(*mod)
                add_down(n, c0 + 11, gate)

            def ada_mod(s0, n, gate_scale):
                m = mod[:, s0:s0 + n, :].rearrange("p a b -> p (a b)")
                dve.wait_ge(ada_moved, 24 if s0 == 0 else NADA)
                own.mark(v.tensor_tensor(m, m, cols[:, COL["b_ada"] + 24 * s0:COL["b_ada"] + 24 * (s0 + n)], ALU.add))
                own.wait()
                for s in range(s0, s0 + n):
                    g = COL[("f1_g", "mix_g", "f2_g")[s]]
                    own.mark(v.scalar_tensor_tensor(out=modA[:, s, :], in0=mod[:, s, 8:16], scalar=1.0, in1=cols[:, g:g + KC], op0=ALU.add, op1=ALU.mult))
                    if s == 0:
                        own.wait()
                        g = COL["fin1_g"]
                        v.tensor_tensor(modA[:, s, :], modA[:, s, :], cols[:, g:g + KC], ALU.mult)
                    ins = v.tensor_scalar(mod[:, s, 16:24], mod[:, s, 16:24], gate_scale, None, ALU.mult)
                ins.then_inc(mod_ready, 1)

            rope_trig()
            lo(0)
            norm_plain(0, 0, "attn_g")
            lo(1)
            lo(2)
            lo(3)
            dve.wait_ge(ls_done, 1)
            own.mark(v.scalar_tensor_tensor(out=b1["E"][:, 0, :, :], in0=b1["QL"][:, 0, :, :], scalar=0.0, in1=b1["KL"][:, 0, 1, :, :],
                                            op0=ALU.min, op1=ALU.subtract))
            own.mark(v.memset(b1["E"][:, 1, 0, :], 1.0))
            own.wait()
            for ht in range(2):
                ins = v.tensor_tensor_scan(b1["G"][:, ht, :], b1["E"][:, 1, 0, :], b1["E"][:, 0, ht, :], 0.0, ALU.mult, ALU.add)
            own.mark(ins)
            own.wait()
            sm1, st1, pt1, yh1, yl1 = b1["sm1"], b1["st1"], b1["pt1"], b1["yh1"], b1["yl1"]
            level_d(0)
            level_d(1)
            lo(4)
            rope(2)
            lo(5)
            level_q(0)
            rope(3)
            level_q(1)
            level_d(2)
            lo(6)
            level_copy(0)
            rope(4)
            level_q(2)
            level_d(3)
            lo(7)
            level_copy(1)
            level_q(3)
            rope(5)
            level_d(4)
            level_copy(2)
            lo(8)
            level_q(4)
            level_d(5)
            level_copy(3)
            att_mask(0, sm1, st1, 0.125, causal)
            level_q(5)
            level_d(6)
            att_norm(0, sm1, st1)
            for g in range(4):
                c = 8 + g
                lo(c + 1, halves=(0,))
                level_copy(4 + g if g < 3 else 8)
                if g < 3:
                    att_mask(g + 1, sm1, st1, 0.125, causal)
                att_pt(g, pt1)
                if g == 2:
                    level_copy(7)
                lo(c + 1, halves=(1,))
                if g < 3:
                    att_norm(g + 1, sm1, st1)
                if g == 0:
                    level_d(7)
                if g < 2:
                    level_q(6 + g)
                att_y(g, yh1, yl1, g)
            for j in range(2):
                a = b1["og"][:, 2 * j:2 * j + 2, :]
                r = b1["g_sd"][:, 2 * j:2 * j + 2, :]
                dve.wait_ge(go_sd, j + 1)
                own.mark(v.reciprocal(r, r))
                lo(C_OUT1 + 1, halves=(j,))
                own.wait()
                for h in (2 * j, 2 * j + 1):
                    ins = v.scalar_tensor_tensor(out=b1["og"][:, h, :], in0=b1["og"][:, h, :], scalar=col("gla_g", h), in1=b1["g_sd"][:, h, :],
                                                 op0=ALU.mult, op1=ALU.mult)
                own.mark(ins)
                own.wait()
                dve.wait_ge(gr_silu, 1)
                v.tensor_tensor(a, a, b1["gr"][:, 2 * j:2 * j + 2, :], ALU.mult).then_inc(go_v, 1)
            for j in range(2):
                dve.wait_ge(yg_hi, j + 1)
                v.tensor_tensor(b1["yl1"][:, 4 + 2 * j:6 + 2 * j, :], b1["og"][:, 2 * j:2 * j + 2, :],
                                b1["yh1"][:, 4 + 2 * j:6 + 2 * j, :].bitcast(F32), ALU.subtract).then_inc(yg_ready, 1)
            out_down(0, C_OUT1, start=2)
            norm_plain(1, 1, "ffn_g")
            ffn_up(0, C_UP[0])
            ffn_down(1, C_DN[0], mod=(0, 1, 0.5))
            norm_mod(2, 2, 0, twice=True)
            ffn_up(1, C_UP[1], residual=fin1_residual)
            ffn_down(2, C_DN[1], mod=(1, 2, 0.5), gate=0)
            norm_mod(4, 3, 1)
            lo(C_IN2 + 1)
            lo(C_IN2 + 2)
            lo(C_IN2 + 3)
            lat, lsd = b2["lat"], b2["l_sd"]
            dve.wait_ge(lat_sd, 1)
            own.mark(v.reciprocal(lsd[:, :, :], lsd[:, :, :]))
            own.wait()
            for j in range(3):
                ins = v.scalar_tensor_tensor(out=lat[:, j, :], in0=lat[:, j, :], scalar=col("q_g", j) if j < 2 else col("kv_g"),
                                             in1=lsd[:, j // 2, :], op0=ALU.mult, op1=ALU.mult)
            ins.then_inc(lat_v, 1)
            lo(C_IN2 + 4)
            dve.wait_ge(lat_hi, 1)
            v.tensor_tensor(b2["cql"][:, :, :], lat[:, :, :], b2["cqh"][:, :, :].bitcast(F32), ALU.subtract).then_inc(lat_ready2, 1)
            dve.wait_ge(pe_rot, 1)
            dve.wait_ge(pool_zero, 8)
            dve.wait_ge(trig_done, 1)
            v.tensor_tensor(b2["rt2"][:, 0:S], b2["kpr"][:, :], cos2[:, :], ALU.mult)
            own.mark(v.tensor_tensor(b2["rt2"][:, S:2 * S], ps[:, 3, 0:S], sin2[:, :], ALU.mult))
            own.wait()
            for j in range(4):
                a = slice(32 * j, 32 * j + 32)
                ins = v.tensor_tensor(b2["kpz"][a, j, :], b2["rt2"][a, 0:S], b2["rt2"][a, S:2 * S], ALU.add)
            ins.then_inc(pe_done, 1)
            lo(C_IN2 + 5)
            lo(C_UQ)
            lo(C_UV)
            lo(C_CAV)
            lo(C_CAV + 1)
            dve.wait_ge(pe_rot, 2)
            dve.wait_ge(pe_done, 1)
            two = lambda ap: ap.rearrange("p (a n) -> p a n", a=2)
            own.mark(v.tensor_tensor(two(b2["rt2"][:, :]), two(ps[:, 3, :]), over(sin2[:, :], 2), ALU.mult))
            own.mark(v.tensor_tensor(two(b2["qpr"][:, :]), two(b2["qpr"][:, :]), over(cos2[:, :], 2), ALU.mult))
            own.wait()
            v.tensor_tensor(b2["qpe"][:, :, :], two(b2["qpr"][:, :]), two(b2["rt2"][:, :]), ALU.add).then_inc(pe_done, 1)
            lo(C_CAV + 2)
            mla = 96.0 ** -0.5
            dve.wait_ge(bm_ready, 1)

            def mask2(g):
                if g < 8:
                    att_mask(g, b2["sm2"], b2["st2"], mla, chunked)
                else:
                    h = 2 * (g - 8)
                    att_mask(g, b2["sm2"], b2["st2"], 0.125, lambda a, b_: b2["bm"][:, h:h + 2, a:b_])

            mask2(4)
            att_norm(4, b2["sm2"], b2["st2"])
            for c in range(8):
                g = 4 + c
                lo(C_GATE + c + 1, halves=(0,))
                if g < 11:
                    mask2(g + 1)
                att_pt(g, b2["pt2"])
                lo(C_GATE + c + 1, halves=(1,))
                if g < 11:
                    att_norm(g + 1, b2["sm2"], b2["st2"])
                att_y(g, b2["yh2"], b2["yl2"], c)
            def merge_lo(p):
                dve.wait_ge(mh_ready, p + 1)
                v.tensor_tensor(pair(xl, p), pair(xn, p), pair(xh, p).bitcast(F32), ALU.subtract).then_inc(ml_ready, 1)

            for n in range(4):
                c, br, cc = C_BR + n, n // 2, n % 2
                lo(c + 1)
                dve.wait_ge(half_used, 2 * c + 2)
                for f2 in range(2):
                    k = 4 * cc + 2 * f2
                    th = b2["th"][:, 8 * br + k:8 * br + k + 2, :]
                    dst = xn[:, k:k + 2, :] if br == 0 else b2["caz"][:, cc, 2 * f2:2 * f2 + 2, :]
                    v.scalar_tensor_tensor(out=dst, in0=th, scalar=1.0, in1=two(ps[:, 2 * cc + f2, :]), op0=ALU.add, op1=ALU.mult).then_inc(br_used, 1)
                    if br == 1:
                        dve.wait_ge(br_used, 2 * n + f2 + 1)
                        v.tensor_tensor(xn[:, k:k + 2, :], xn[:, k:k + 2, :], dst, ALU.add).then_inc(br_done, 1)
                if n == 2:
                    merge_lo(0)
                    merge_lo(1)
            merge_lo(2)
            merge_lo(3)
            out_down(3, C_OUT2, gate=1)
            norm_mod(5, 4, 2)
            ffn_up(2, C_UP[2])
            ffn_down(4, C_DN[2], gate=2, last=True)
            norm_in_place(6, "fin2_g")



def _tiles(w, k0, kn, c):
    a = w[k0 * P:(k0 + kn) * P][:, c].reshape(kn, P, -1)
    return a.transpose(1, 0, 2).reshape(P, -1)


def _padded(a):
    out = np.zeros((P, HALF), a.dtype)
    out[:, :a.shape[1]] = a
    return out


def _weights(a):
    s = []
    r = np.arange

    def feature_chunk(w, c):
        s.extend([_tiles(w, 0, 4, c), _tiles(w, 4, 4, c)])

    def up(w, width):
        for j in range(FT):
            feature_chunk(w, np.concatenate([r(j * P, j * P + P), width + r(j * P, j * P + P)]))

    w = a["w_in"][0]
    for c0, n in ((1536, 256), (1792, 256), (0, 512), (512, 512), (1024, 512), (2048, 512), (2560, 512)):
        for c in range(c0, c0 + n, 256):
            feature_chunk(w, r(c, c + 256))
    s.extend(a["w_out"][0].reshape(KC, P, D))
    up(a["w_ffn_up"][0], DFF)
    s.extend(a["w_ffn_down"][0].reshape(FT, P, D))
    up(a["ffn1_w_in_2"][0], DFF)
    s.extend(a["ffn1_w_out_2"][0].reshape(FT, P, D))
    w = a["w_in_2"][0]
    feature_chunk(w, r(0, 256))
    feature_chunk(w, np.concatenate([r(256, 384)] + 4 * [r(384, 416)]))
    for c in range(416, 416 + 1024, 256):
        feature_chunk(w, r(c, c + 256))
    uq, ukv = a["mla_w_uq_2"][0], a["mla_w_ukv_2"][0]
    head = r(8)[:, None]
    q_cols = np.concatenate([(96 * head + r(64)).ravel(), (96 * head + 64 + r(32)).ravel()])
    k_cols, v_cols = (128 * head + r(64)).ravel(), (128 * head + 64 + r(64)).ravel()
    for j in range(2):
        s.append(np.concatenate([_tiles(uq, j, 1, q_cols), _tiles(ukv, 0, 1, k_cols[256 * j:256 * j + 256])], 1))
    s.append(_padded(_tiles(ukv, 0, 1, v_cols)))
    s.append(_padded(s[-1][:, :0]))
    for c in range(1440, 4000, 256):
        feature_chunk(w, r(c, c + 256))
    for w in (a["w_branch_a_2"][0], a["w_branch_b_2"][0]):
        for c in (0, 512):
            for k in (0, 2):
                s.append(_tiles(w, k, 2, r(c, c + 512)))
    s.extend(a["w_out_2"][0].reshape(KC, P, D))
    up(a["ffn2_w_in_2"][0], DFF)
    s.extend(a["ffn2_w_out_2"][0].reshape(FT, P, D))
    return np.stack(s)


def _ada(w):
    return np.ascontiguousarray(w.T).reshape(NADA, P, D)


def _columns(a):
    col = lambda v: np.asarray(v).reshape(-1, P).T
    p = np.arange(P)
    freq = np.float32(10000.0) ** (-np.arange(0, 32, 2, dtype=np.float32) / np.float32(32))
    freq = np.where(p % 32 < 16, -freq[p % 16], freq[p % 16]).astype(np.float32)[:, None]
    c = [col(a["attn_norm_g"][0]), col(a["ffn_norm_g"][0]), col(a["final_norm_g"]), col(a["gla_norm_g"][0]), col(a["b_gate"][0]),
         col(a["conv_w"][0, 0]), col(a["conv_w"][0, 1]), col(a["conv_w"][0, 2]), col(a["conv_b"][0]),
         col(a["ffn1_norm_2"][0]), col(a["mix_norm_2"][0]), col(a["ffn2_norm_2"][0]), col(a["final_norm_2"]),
         col(a["mla_q_norm_2"][0]), col(a["mla_kv_norm_2"][0]), col(a["b_ada_2"][0]), freq]
    return np.ascontiguousarray(np.concatenate(c, 1))


def _constants():
    p, n = np.arange(P)[:, None], np.arange(S)[None, :]
    inv = np.float32(1.0) / (np.float32(10000.0) ** (np.arange(0, 64, 2, dtype=np.float32) / np.float32(64)))
    ang = n.astype(np.float32) * inv[p % 32]
    m = np.arange(P)[None, :]
    zero = np.zeros((P, P), np.float32)
    causal = np.where(m <= p, 0, NEG)
    chunked = np.where(m // 64 <= p // 64, 0, NEG)
    tab = [np.cos(ang), np.where(p % 64 < 32, -np.sin(ang), np.sin(ang)), p == (m ^ 32), p == (m ^ 16), zero, causal, zero, chunked]
    tab = np.concatenate([x.astype(np.float32) for x in tab], 1)
    levels = [(p // (2 * q) == m // (2 * q)) & (p % (2 * q) < q) & (m % (2 * q) >= q) for q in (1 << np.arange(LEVELS))]
    return tab, np.stack(levels + [p == m], 1).astype(np.int32)


def _bias(rel):
    i = 256 + np.arange(P)[:, None] + P - np.arange(S)[None, :]
    return np.ascontiguousarray(rel[0][i].transpose(0, 2, 1))


def kernel(**inputs):
    import concourse.bacc as bacc
    from concourse.bass_utils import run_bass_kernel_spmd as run

    a = {k: np.asarray(v) for k, v in inputs.items()}
    tab, gmask = _constants()
    w_in = a["w_in"][0]
    gup = np.zeros((P, S), w_in.dtype)
    gup[:16] = a["w_gate_up"][0]
    arrays = {
        "w": _weights(a), "ada_w": _ada(a["w_ada_2"][0]),
        "x_in": np.ascontiguousarray(a["x"][0].T.reshape(KC, P, S).transpose(1, 0, 2)),
        "cols_in": _columns(a), "tab_in": tab, "gmask_in": gmask,
        "glr_in": np.ascontiguousarray(_tiles(w_in, 0, KC, np.arange(3072, 3088))), "gup_in": gup,
        "c_in": a["c_2"].reshape(1, D), "bias_in": _bias(a["rel_bias_2"]), "pos_in": a["positions_2"].reshape(1, S).astype(np.int32),
    }
    nc = bacc.Bacc("TRN2", target_bir_lowering=False, num_devices=1)
    aps = {n: nc.dram_tensor(n, v.shape, mybir.dt.from_np(v.dtype), kind="ExternalInput").ap() for n, v in arrays.items()}
    out = nc.dram_tensor("out", (P, KC, S), mybir.dt.float32, kind="ExternalOutput").ap()
    build(nc, out=out, **aps)
    r = run(nc, [arrays], core_ids=[0])
    y = r.results[0]["out"]
    return y.transpose(1, 0, 2).reshape(D, S).T[None]
```

```python
from contextlib import ExitStack

import numpy as np

import concourse.bass as bass
from concourse import mybir

P = 128
D = 1024
S = 256
KC = D // P
DFF = 2816
FT = DFF // P
HALF = 1024
NSLOT = 4
EPS = 1e-6
NEG = -1e30
IDLE = 6
DONE = [(0, 2), (2, 2), (4, 2), (6, 1), (7, 1)]
NEXT = [(0, 1), (1, 1), (2, 2), (4, 2), (6, 2)]
LEVELS = 7
NADA = 72

C_IN1 = 0
C_OUT1 = C_IN1 + 12
C_UP = [C_OUT1 + 4, 0, 0]
C_DN = [C_UP[0] + FT, 0, 0]
C_UP[1] = C_DN[0] + FT // 2
C_DN[1] = C_UP[1] + FT
C_IN2 = C_DN[1] + FT // 2
C_UQ = C_IN2 + 6
C_UV = C_IN2 + 7
C_CAV = C_IN2 + 8
C_GATE = C_IN2 + 10
C_BR = C_IN2 + 18
C_OUT2 = C_BR + 4
C_UP[2] = C_OUT2 + 4
C_DN[2] = C_UP[2] + FT
NCHUNK = C_DN[2] + FT // 2
NHALF = 2 * NCHUNK
FIRST = [0, *C_UP, C_IN2]
DOWN = [C_OUT1, C_DN[0], C_DN[1], C_OUT2, C_DN[2]]

COL = {}
_n = 0
for _name, _w in [("attn_g", 8), ("ffn_g", 8), ("fin1_g", 8), ("gla_g", 4), ("b_gate", 2), ("conv_w", 132),
                  ("conv_b", 44), ("f1_g", 8), ("mix_g", 8), ("f2_g", 8), ("fin2_g", 8), ("q_g", 2),
                  ("kv_g", 1), ("b_ada", 72), ("freq", 1)]:
    COL[_name] = _n
    _n += _w
NCOL = _n

TAB = {}
_n = 0
for _name, _w in [("cos", S), ("sin", S), ("perm64", P), ("perm32", P), ("causal", S), ("chunked", S)]:
    TAB[_name] = _n
    _n += _w
NTAB = _n


def build(nc, w, ada_w, x_in, cols_in, tab_in, gmask_in, glr_in, gup_in, bias_in, c_in, pos_in, out):
    F32 = mybir.dt.float32
    F32R = mybir.dt.float32r
    I32 = mybir.dt.int32
    ALU = mybir.AluOpType
    ACT = mybir.ActivationFunctionType
    AX = mybir.AxisListType
    ds = bass.ds

    with ExitStack() as ctx:
        sb = lambda name, shape, dt=F32: ctx.enter_context(nc.sbuf_tensor(name, shape, dt))
        sem = lambda name: ctx.enter_context(nc.semaphore(name))

        raw = sb("raw", [P, NSLOT, HALF])
        w_hi = sb("w_hi", [P, NSLOT, HALF], F32R)
        w_lo = sb("w_lo", [P, NSLOT, HALF], F32R)
        X = sb("X", [P, KC, S])
        xn = sb("xn", [P, KC, S])
        xh = sb("xh", [P, KC, S], F32R)
        xl = sb("xl", [P, KC, S], F32R)
        rstd = sb("rstd", [P, S])
        sd = sb("sd", [P, 2, S])
        epsc = sb("epsc", [P, 3])
        cols = sb("cols", [P, NCOL])
        tab = sb("tab", [P, NTAB])
        mean = sb("mean", [P, 3, P])
        ident = sb("ident", [P, P])
        mod = sb("mod", [P, 3, 24])
        modA = sb("modA", [P, 3, KC])
        cos2 = sb("cos2", [P, S])
        sin2 = sb("sin2", [P, S])

        def phase(names, early=()):
            made = {}

            def place(tensors):
                guards = [nc.sbuf_tensor(n, s, d) for n, s, d in tensors]
                for (n, _, _), g in zip(tensors, guards):
                    made[n] = g.__enter__()
                return reversed(guards)

            kept = place(names[:-1])
            for g in place(early):
                g.__exit__(None, None, None)
            for g in place(names[-1:]):
                g.__exit__(None, None, None)
            for g in kept:
                g.__exit__(None, None, None)
            return made

        ffn = phase([("act_hi", [P, FT, S], F32R), ("act_lo", [P, FT, S], F32R), ("cv", [P, 2, 2, S], F32),
                     ("sg", [P, 2, S], F32), ("av", [P, 2, S], F32), ("ada_raw", [P, 4, HALF], F32),
                     ("ada_mul", [P, 2, HALF], F32), ("cact", [P, HALF], F32), ("gmean", [P, KC, P], F32), ("gsq", [P, KC], F32),
                     ("ada_col", [P, 2], F32), ("posi", [P, S], I32)])
        act_hi, act_lo, cv, sg, av, ada_raw, ada_mul, cact, gmean, gsq, ada_col, posi = ffn.values()
        b1 = phase([("qT", [P, 4, S], F32), ("kz", [P, 2, 4, S], F32), ("mv", [P, 2, 512], F32),
                    ("gv", [P, 2, 512], F32), ("gq", [P, 2, S], F32), ("gkz", [P, 2, 2, S], F32),
                    ("gr", [P, 4, S], F32), ("G", [P, 2, S], F32), ("E", [P, 2, 2, S], F32),
                    ("QL", [P, 2, 2, S], F32), ("KL", [P, 2, 2, 2, S], F32), ("AT0", [P, 4, S], F32),
                    ("AT1", [P, 4, P], F32), ("og", [P, 4, S], F32), ("qraw", [P, 2, 2 * S], F32),
                    ("rt", [P, 2, 2 * S], F32), ("glr", [P, S], F32), ("w_glr", [P, 128], F32),
                    ("w_gup", [P, S], F32), ("gmask", [P, 8, P], I32), ("g_sd", [P, 4, S], F32),
                    ("yh1", [P, 8, S], F32R), ("yl1", [P, 8, S], F32R), ("sm1", [P, 2, 768], F32),
                    ("pt1", [P, 2, 768], F32), ("st1", [P, 2, 3, 4], F32),
                    ("g_rstd", [P, S], F32), ("g_pick", [P, 4, P], F32)])
        b2 = phase([("qn", [P, 4, S], F32), ("qpe", [P, 2, S], F32), ("nz", [P, 2, 4, S], F32),
                    ("kpz", [P, 4, S], F32), ("v2", [P, 2, 512], F32), ("caq", [P, 4, S], F32),
                    ("caz", [P, 2, 4, S], F32), ("cav", [P, 2, 512], F32), ("l_sd", [P, 2, S], F32), ("kpr", [P, S], F32), ("qpr", [P, 2 * S], F32),
                    ("rt2", [P, 2 * S], F32), ("yh2", [P, 8, S], F32R), ("yl2", [P, 8, S], F32R),
                    ("sm2", [P, 2, 768], F32), ("pt2", [P, 2, 768], F32), ("st2", [P, 2, 3, 4], F32),
                    ("bm", [P, 8, S], F32), ("th", [P, 16, S], F32)],
                   early=[("lat", [P, 3, S], F32), ("latsq", [P, 3, S], F32), ("cqh", [P, 3, S], F32R), ("cql", [P, 3, S], F32R)])

        ps = ctx.enter_context(nc.psum_tensor("ps", [P, 8, 512], F32))

        x_landed = [sem(f"x_landed{i}") for i in range(4)]
        cols_landed, tab_landed, aux_landed, bias_landed = map(sem, ("cols_landed", "tab_landed", "aux_landed", "bias_landed"))
        pos_landed, gmask_landed = sem("pos_landed"), sem("gmask_landed")
        raw_landed = [sem(f"raw_landed{i}") for i in range(NSLOT)]
        ada_landed = [sem(f"ada_landed{i}") for i in range(4)]
        hi_ready, lo_ready, half_used = sem("hi_ready"), sem("lo_ready"), sem("half_used")
        bank_free = [sem("bank0_free"), sem("bank1_free")]
        pick_ready, mean_ready, consts_ready, pool_zero = sem("pick_ready"), sem("mean_ready"), sem("consts_ready"), sem("pool_zero")
        resid_done, sq_done, ss_done, sd_done, rstd_done, eps_mixed = map(
            sem, ("resid_done", "sq_done", "ss_done", "sd_done", "rstd_done", "eps_mixed"))
        xt_ready, xh_ready, xl_ready = map(sem, ("xt_ready", "xh_ready", "xl_ready"))
        own_act, own_dve, own_pool = sem("own_act"), sem("own_dve"), sem("own_pool")
        cv_base, cv_gate, cv_own, sg_done, ah_done, act_ready, down_full = map(
            sem, ("cv_base", "cv_gate", "cv_own", "sg_done", "ah_done", "act_ready", "down_full"))
        c_landed, cact_ready, ada_mult, ada_used, ada_moved, mod_ready, gmean_ready = map(
            sem, ("c_landed", "cact_ready", "ada_mult", "ada_used", "ada_moved", "mod_ready", "gmean_ready"))
        trig_red, trig_done = sem("trig_red"), sem("trig_done")
        glr_done, glr_sb, gup_done, z_done, ls_done = map(sem, ("glr_done", "glr_sb", "gup_done", "z_done", "ls_done"))
        rot_done, rope_done = map(sem, ("rot_done", "rope_done"))
        lv_d, lv_e, lv_q, lv_k, lv_full, lv_copied = map(sem, ("lv_d", "lv_e", "lv_q", "lv_k", "lv_full", "lv_copied"))
        go_full, go_sq, go_ss, go_sd, go_rstd, go_spread, gr_silu, go_v, yg_hi, yg_ready = map(
            sem, ("go_full", "go_sq", "go_ss", "go_sd", "go_rstd", "go_spread", "gr_silu", "go_v", "yg_hi", "yg_ready"))
        at_s, at_m, at_e, at_n, at_t, at_p0, at_p1, at_o, at_yh, at_y = map(
            sem, ("at_s", "at_m", "at_e", "at_n", "at_t", "at_p0", "at_p1", "at_o", "at_yh", "at_y"))
        lat_sq, lat_ss, lat_sd, lat_v, lat_hi, lat_ready2, uq_full = map(
            sem, ("lat_sq", "lat_ss", "lat_sd", "lat_v", "lat_hi", "lat_ready2", "uq_full"))
        pe_rot, pe_done, br_used, br_done, mh_ready, ml_ready, bm_ready = map(
            sem, ("pe_rot", "pe_done", "br_used", "br_done", "mh_ready", "ml_ready", "bm_ready"))
        out_written = sem("out_written")

        block = ctx.enter_context(nc.Block())

        def table(name, n):
            return tab[:, TAB[name]:TAB[name] + n]

        def col(name, j=0):
            return cols[:, COL[name] + j:COL[name] + j + 1]

        def over(ap, n):
            return ap.unsqueeze(1).to_broadcast([ap.shape[0], n, ap.shape[1]])

        def slot(h):
            return h % NSLOT

        def pair(a, p):
            return a[:, 2 * p:2 * p + 2, :]

        def tiles(a, k):
            return a[:, k[0]:k[0] + k[1], :]

        def later(a, l):
            if l >= LEVELS:
                return a
            if len(a.shape) == 2:
                return a.rearrange("p (m two q) -> p m two q", two=2, q=1 << l)[:, :, 1, :]
            return a.rearrange("p h (m two q) -> p h m two q", two=2, q=1 << l)[:, :, :, 1, :]

        def down_out(ft):
            return ps[:, 4 + ft // 2, (ft % 2) * S:(ft % 2) * S + S] if ft < KC - 1 else ps[:, 3, 0:S]

        class Own:
            def __init__(self, eng, s):
                self.eng, self.s, self.n = eng, s, 0

            def mark(self, ins):
                ins.then_inc(self.s, 1)
                self.n += 1

            def wait(self):
                self.eng.wait_ge(self.s, self.n)

        def bank_use(c):
            other = [(d, 4 if d in (C_OUT1, C_OUT2) else FT // 2) for d in DOWN] + [(C_BR, 4)]
            return c - sum(n for d, n in other if c > d) + 4 * (c > C_UQ) + (c > C_UV)

        def evacuated(eng, u):
            eng.wait_ge(bank_free[u % 2], u // 2 + 1)

        @block.sync
        def _(sp):
            def load(h, k):
                sp.dma_start(raw[:, k, :], w[h, :, :] if isinstance(h, int) else w[ds(h, 1), :, :].rearrange("a p n -> (a p) n")).then_inc(raw_landed[k], 16)

            for p in range(4):
                sp.dma_start(pair(X, p), x_in[:, 2 * p:2 * p + 2, :]).then_inc(x_landed[p], 16)
            for k in range(NSLOT):
                load(k, k)
            with sp.Fori(1, NHALF // NSLOT) as i:
                for k in range(NSLOT):
                    sp.wait_ge(lo_ready, i * NSLOT + (k - NSLOT + 1))
                    load(i * NSLOT + k, k)
            for h in range(NHALF // NSLOT * NSLOT, NHALF):
                sp.wait_ge(lo_ready, h - NSLOT + 1)
                load(h, slot(h))
            for p in range(4):
                sp.wait_ge(resid_done, 5 * len(DONE) + 1 + p)
                sp.dma_start(out[:, 2 * p:2 * p + 2, :], pair(X, p)).then_inc(out_written, 16)
            sp.wait_ge(out_written, 64)

        @block.gpsimd
        def _(pool):
            own = Own(pool, own_pool)
            for j, n in enumerate((D, 256, 128)):
                ins = pool.memset(mean[:, j, :], 1.0 / n)
            ins.then_inc(mean_ready, 1)
            pool.memset(epsc[:, 0:1], EPS)
            pool.memset(epsc[:, 1:2], EPS * EPS)
            own.mark(pool.memset(ident[:, :], 0.0))
            own.wait()
            pool.affine_select(out=ident[:, :], in_=ident[:, :], compare_op=ALU.not_equal, fill=1.0, base=0,
                               pattern=[[-1, P]], channel_multiplier=1).then_inc(consts_ready, 1)
            pool.memset(b1["glr"][:, :], 0.0).then_inc(pool_zero, 1)
            pool.memset(b1["gkz"][:, :, :, :], 0.0).then_inc(pool_zero, 1)
            pool.memset(b1["kz"][:, :, :, :], 0.0).then_inc(pool_zero, 1)
            pool.memset(b1["AT0"][:, :, :], 0.0).then_inc(pool_zero, 1)
            pool.memset(b1["AT1"][:, :, :], 0.0).then_inc(pool_zero, 1)
            own.mark(pool.memset(b1["g_pick"][:, :, :], 0.0))
            own.wait()
            for h in range(4):
                pool.memset(b1["g_pick"][32 * h:32 * h + 1, h, :], 1.0).then_inc(pick_ready, 1)
            pool.wait_ge(pick_ready, 4)

            for l in range(LEVELS + 1):
                pool.wait_ge(lv_e, l + 1)
                if l == 0:
                    evacuated(pool, 1)
                if l >= 2:
                    pool.wait_ge(lv_full, 2 * (l - 1))
                for par in range(2):
                    ins = pool.tensor_tensor(b1["KL"][:, l % 2, par, :, :], b1["gkz"][:, par, :, :], b1["E"][:, l % 2, :, :], ALU.mult)
                ins.then_inc(lv_k, 1)
            def load_ada(n, k):
                src = ada_w[n, :, :] if isinstance(n, int) else ada_w[ds(n, 1), :, :].rearrange("a p n -> (a p) n")
                pool.dma_start(ada_raw[:, k, :], src).then_inc(ada_landed[k], 16)

            mod_cols = mod[:, :, :].rearrange("p a b -> p (a b)")

            def move_sum(n, k):
                pool.wait_ge(ada_used, n + 1)
                pool.tensor_copy(mod_cols[:, ds(n, 1)], ada_col[:, k:k + 1]).then_inc(ada_moved, 1)

            def mult_ada(i, k, load=True):
                n = i * 4 + k
                pool.wait_ge(ada_landed[k], (i + 1) * 16)
                if not (isinstance(i, int) and n < 2):
                    move_sum(n - 2, k % 2)
                pool.tensor_tensor(ada_mul[:, k % 2, :], ada_raw[:, k, :], cact[:, :], ALU.mult).then_inc(ada_mult, 1)
                if load:
                    pool.wait_ge(ada_mult, n + 1)
                    load_ada(n + 4, k)

            pool.wait_ge(half_used, 2 * (C_OUT1 + 4))
            pool.dma_start(cact[:, :], c_in.to_broadcast([P, HALF])).then_inc(c_landed, 16)
            for k in range(4):
                load_ada(k, k)
            pool.dma_start(posi[:, :], pos_in.to_broadcast([P, S])).then_inc(pos_landed, 16)
            pool.wait_ge(cact_ready, 1)
            for k in range(4):
                mult_ada(0, k)
            with pool.Fori(1, NADA // 4 - 1) as i:
                for k in range(4):
                    mult_ada(i, k)
            for k in range(4):
                mult_ada(NADA // 4 - 1, k, load=False)
            for k in range(2):
                move_sum(NADA - 2 + k, k)
            pool.wait_ge(mod_ready, 2)
            pool.wait_ge(half_used, 2 * C_IN2)
            pool.dma_start(b2["bm"][:, :, :], bias_in).then_inc(bias_landed, 16)
            pool.memset(b2["nz"][:, :, :, :], 0.0).then_inc(pool_zero, 1)
            pool.memset(b2["kpz"][:, :, :], 0.0).then_inc(pool_zero, 1)
            pool.memset(b2["caz"][:, :, :, :], 0.0).then_inc(pool_zero, 1)
            pool.wait_ge(bias_landed, 16)
            for h in range(8):
                ins = pool.tensor_tensor(b2["bm"][:, h, :], b2["bm"][:, h, :], table("chunked", S), ALU.add)
            ins.then_inc(bm_ready, 1)

        @block.tensor
        def _(pe):
            def three(o, lh, ll, rh, rl, start, stop):
                pe.matmul(o, lh, rh, start=start, stop=False, skip_group_check=True)
                pe.matmul(o, lh, rl, start=False, stop=False, skip_group_check=True)
                return pe.matmul(o, ll, rh, start=False, stop=stop, skip_group_check=True)

            def keep_clock(bank, n):
                for _ in range(n):
                    pe.matmul(ps[:, bank, 0:3 * P], mean[:, 0, :], mean[:, :, :].rearrange("p a n -> p (a n)"), start=True, stop=True)

            def feature_tile(u, h, kc, first, last):
                for f in range(2):
                    wc = slice((kc % 4) * 256 + f * P, (kc % 4) * 256 + f * P + P)
                    m = three(ps[:, u % 2, f * 256:f * 256 + 256], w_hi[:, slot(h), wc], w_lo[:, slot(h), wc],
                              xh[:, kc, :], xl[:, kc, :], first and f == 0, last)
                return m

            def first_two(c, x_wait, between=None):
                u, h = bank_use(c), 2 * c
                if c:
                    for j in range(2):
                        pe.wait_ge(bank_free[(u + j) % 2], (u + j) // 2)
                keep_clock(u % 2, IDLE)
                pe.wait_ge(lo_ready, h + 2)
                for kc in range(4):
                    if kc in [k0 for k0, _ in NEXT]:
                        pe.wait_ge(xl_ready, x_wait + 1 + [k0 for k0, _ in NEXT].index(kc))
                    for j in range(2):
                        m = feature_tile(u + j, h + j, kc, kc == 0, False)
                        if kc == 3:
                            m.then_inc(half_used, 1)
                if between:
                    between()
                for j in range(2):
                    pe.wait_ge(lo_ready, h + 3 + j)
                    for kc in range(4, KC):
                        if j == 0 and kc in [k0 for k0, _ in NEXT]:
                            pe.wait_ge(xl_ready, x_wait + 1 + [k0 for k0, _ in NEXT].index(kc))
                        m = feature_tile(u + j, h + 2 + j, kc, False, kc == KC - 1)
                    m.then_inc(half_used, 1)

            def chunk(c, i=0, tokens_out=False, halves=(0, 1)):
                ah, al = xh, xl
                u = bank_use(c)
                b = u % 2
                if halves[0] == 0 and not (isinstance(i, int) and u + 2 * i < 2):
                    pe.wait_ge(bank_free[b], u // 2 + i)
                for half in halves:
                    h = 2 * c + half
                    pe.wait_ge(lo_ready, h + 1 + 4 * i)
                    for k in range(4):
                        kc = 4 * half + k
                        first, last = half == 0 and k == 0, half == 1 and k == 3
                        if not tokens_out:
                            m = feature_tile(u, h, kc, first, last)
                            continue
                        for f in range(2):
                            a = slice(f * P, f * P + P)
                            wcol = slice(k * 256, k * 256 + 256)
                            o = ps[:, b, f * 256:f * 256 + 256]
                            pe.matmul(o, ah[:, kc, a], w_hi[:, slot(h), wcol], start=first and f == 0, stop=False, skip_group_check=True)
                            pe.matmul(o, al[:, kc, a], w_hi[:, slot(h), wcol], start=False, stop=False, skip_group_check=True)
                            m = pe.matmul(o, ah[:, kc, a], w_lo[:, slot(h), wcol], start=False, stop=last, skip_group_check=True)
                    m.then_inc(half_used, 1)

            def norm_part(n, j, bank=2, gain=False):
                if not gain:
                    pe.wait_ge(sq_done, len(DONE) * (n - (n > 2)) + j + 1)
                for k in range(DONE[j][0], sum(DONE[j])):
                    m = pe.matmul(ps[:, bank, 0:S], gmean[:, k, :] if gain else mean[:, 0, :], xn[:, k, :],
                                  start=k == 0, stop=k == KC - 1, skip_group_check=True)
                if j == len(DONE) - 1:
                    m.then_inc(ss_done, 1)

            def att_s(g, q, kz, pe_q=None, pe_k=None):
                a = 4 + 2 * (g % 2)
                if g >= 2:
                    pe.wait_ge(at_y, g - 1)
                t4 = g % 4
                for hh in range(2):
                    h = 2 * t4 + hh
                    for (o, qs, n) in ((ps[:, a, hh * P:hh * P + P], 0, P), (ps[:, a + 1, hh * S:hh * S + S], P, S)):
                        m = pe.matmul(o, q[:, t4, qs:qs + P], kz[:, hh, t4, 0:n], start=True, stop=pe_q is None)
                        if pe_q is not None:
                            m = pe.matmul(o, pe_q[:, h // 4, qs:qs + P], pe_k[:, h % 4, 0:n], start=False, stop=True)
                m.then_inc(at_s, 1)

            def att_t(g, sm):
                a = 4 + 2 * (g % 2)
                r = sm[:, g % 2, :]
                pe.wait_ge(at_n, g + 1)
                for hh in range(2):
                    pe.transpose(ps[:, a + 1, hh * S:hh * S + P], r[:, hh * P:hh * P + P], ident[:, :])
                    pe.transpose(ps[:, a + 1, hh * S + P:hh * S + S], r[:, 256 + hh * S:256 + hh * S + P], ident[:, :])
                    m = pe.transpose(ps[:, a, hh * P:hh * P + P], r[:, 256 + hh * S + P:256 + hh * S + S], ident[:, :])
                m.then_inc(at_t, 1)

            def att_o(g, pt, v):
                a = 4 + 2 * (g % 2)
                pe.wait_ge(at_p0, g + 1)
                pe.wait_ge(at_p1, g + 1)
                for hh in range(2):
                    h = 2 * (g % 4) + hh
                    o = slice(64 * hh, 64 * hh + 64)
                    pe.matmul(ps[o, a, 256:512], v[:, 0, h * 64:h * 64 + 64], pt[:, g % 2, hh * S:hh * S + S],
                              start=True, stop=False, skip_group_check=True)
                    m = pe.matmul(ps[o, a, 384:512], v[:, 1, h * 64:h * 64 + 64], pt[:, g % 2, 512 + hh * P:512 + hh * P + P],
                                  start=False, stop=True, skip_group_check=True)
                m.then_inc(at_o, 1)

            def rot(c):
                evacuated(pe, c)
                pe.matmul(ps[:, 2 + c, :], table("perm64", P), b1["qraw"][:, c % 2, :], start=True, stop=True).then_inc(rot_done, 1)

            def level(l):
                if l <= LEVELS:
                    pe.wait_ge(lv_q, l + 1)
                    pe.wait_ge(lv_k, l + 1)
                K = (lambda par, ht, a: b1["KL"][:, l % 2, par, ht, a]) if l <= LEVELS else (lambda par, ht, a: b1["gkz"][:, par, ht, a])
                Q = (lambda ht, a: later(b1["QL"][:, l % 2, ht, a], l)) if l <= LEVELS else (lambda ht, a: b1["gq"][:, ht, a])
                w = P // 2 if l < LEVELS else P
                lo_, hi_ = slice(0, P), slice(P, S)
                for i, (ks, qs) in enumerate([(lo_, hi_)] if l == LEVELS else [(lo_, lo_), (hi_, hi_)]):
                    n = (2 * l + i if l < LEVELS else 2 * LEVELS + (0 if l == LEVELS else 1 + i))
                    bank = 2 + i
                    before = {0: n - 2, 1: n - 2}[i] if l <= LEVELS else (15 - 1 if i == 0 else 13)
                    if before >= 0:
                        pe.wait_ge(lv_copied, before + 1)
                    for h in range(4):
                        m = pe.matmul(ps[:, bank, h * w:h * w + w], K(h % 2, h // 2, ks), Q(h // 2, qs), start=True, stop=True)
                    m.then_inc(lv_full, 1)

            def ffn_up(f, c0, x_wait):
                first_two(c0, x_wait)
                with pe.Fori(0, FT // 2 - 1) as i:
                    for v in range(2):
                        chunk(c0 + 2 + v, i=i)

            def down_half(h, rh, rl, i=0, start=False, ends_att=False):
                pe.wait_ge(lo_ready, h + 1 + 4 * i)
                for ft in range(KC):
                    wc = slice(ft * P, ft * P + P)
                    if ends_att and ft == 4:
                        pe.wait_ge(at_y, 4)
                    m = three(down_out(ft), w_hi[:, slot(h), wc], w_lo[:, slot(h), wc],
                              rh, rl, start and (ft % 2 == 0 or ft == KC - 1), False)
                m.then_inc(half_used, 1)

            def down_last(h, ah, al, k0, n):
                def part(j):
                    norm_part(n, j)
                    if n == 2:
                        norm_part(3, j, bank=1, gain=True)

                if n == 2:
                    pe.wait_ge(gmean_ready, 1)
                pe.wait_ge(lo_ready, h + 2)
                for ft in range(KC):
                    wc = slice(ft * P, ft * P + P)
                    for k in range(2):
                        m = three(down_out(ft), w_hi[:, slot(h + k), wc], w_lo[:, slot(h + k), wc],
                                  ah[:, k0 + k, :], al[:, k0 + k, :], False, k == 1)
                    if ft in (1, 3, 5, 6):
                        m.then_inc(down_full, 1)
                    if ft == KC - 1:
                        m.then_inc(half_used, 2)
                    if ft in (5, 6):
                        part(ft - 5)
                for j in (2, 3, 4):
                    part(j)

            def ffn_down(f, c0, n):
                h0 = 2 * c0
                pe.wait_ge(act_ready, FT * f + FT - 4)
                down_half(h0, act_hi[:, 0, :], act_lo[:, 0, :], start=True)
                down_half(h0 + 1, act_hi[:, 1, :], act_lo[:, 1, :])
                with pe.Fori(0, 4) as i:
                    for k in range(4):
                        tile = lambda a: a[:, ds(i * 4 + (2 + k), 1), :].rearrange("p a n -> p (a n)")
                        down_half(h0 + 2 + k, tile(act_hi), tile(act_lo), i=i)
                pe.wait_ge(act_ready, FT * f + FT)
                for k in (18, 19):
                    down_half(h0 + k, act_hi[:, k, :], act_lo[:, k, :])
                down_last(h0 + 20, act_hi, act_lo, 20, n)

            pe.wait_ge(mean_ready, 1)
            keep_clock(0, IDLE)
            for j in range(len(DONE)):
                norm_part(0, j)

            def gate_low_rank():
                pe.wait_ge(aux_landed, 32)
                pe.wait_ge(xt_ready, len(NEXT))
                for kc in range(KC):
                    m = pe.matmul(ps[0:16, 3, 0:S], b1["w_glr"][:, kc * 16:kc * 16 + 16], xn[:, kc, :], start=kc == 0, stop=kc == KC - 1)
                m.then_inc(glr_done, 1)

            first_two(0, 0, between=gate_low_rank)
            pe.wait_ge(glr_sb, 1)
            for ht in range(2):
                m = pe.matmul(ps[:, 3, ht * S:ht * S + S], b1["w_gup"][:, ht * P:ht * P + P], b1["glr"][:, :], start=ht == 0, stop=True, skip_group_check=True)
            m.then_inc(gup_done, 1)
            chunk(2)
            chunk(3)
            pe.wait_ge(tab_landed, 16)
            pe.wait_ge(consts_ready, 1)
            rot(2)
            chunk(4)
            rot(3)
            pe.wait_ge(z_done, 1)
            level(0)
            chunk(5)
            rot(4)
            level(1)
            chunk(6, tokens_out=True, halves=(0,))
            rot(5)
            level(2)
            chunk(6, tokens_out=True, halves=(1,))
            chunk(7, tokens_out=True, halves=(0,))
            level(3)
            chunk(7, tokens_out=True, halves=(1,))
            pe.wait_ge(rope_done, 4)
            att_s(0, b1["qT"], b1["kz"])
            level(4)
            for g in range(4):
                c = 8 + g
                chunk(c, tokens_out=c < 10, halves=(0,))
                if g < 3:
                    att_s(g + 1, b1["qT"], b1["kz"])
                att_t(g, b1["sm1"])
                if g < 3:
                    level(5 + g)
                else:
                    pe.wait_ge(lv_copied, 17)
                    evacuated(pe, 9)
                    for h in range(4):
                        o = (h % 2) * S
                        pe.matmul(ps[:, 2 + h // 2, o:o + S], b1["gv"][:, 0, h * P:h * P + P], b1["AT0"][:, h, :],
                                  start=h % 2 == 0, stop=False, skip_group_check=True)
                        m = pe.matmul(ps[:, 2 + h // 2, o + P:o + S], b1["gv"][:, 1, h * P:h * P + P], b1["AT1"][:, h, :],
                                      start=False, stop=True, skip_group_check=True)
                        if h % 2:
                            m.then_inc(go_full, 1)
                chunk(c, tokens_out=c < 10, halves=(1,))
                if g == 0:
                    evacuated(pe, 7)
                if g == 3:
                    for h in range(4):
                        pe.wait_ge(go_sq, h // 2 + 1)
                        m = pe.matmul(ps[32 * h:32 * h + 32, 2, 0:S], mean[:, 2, 0:32], b1["g_sd"][:, h, :], start=True, stop=True,
                                      skip_group_check=True)
                    m.then_inc(go_ss, 1)
                att_o(g, b1["pt1"], b1["mv"])
                if g == 2:
                    level(8)
            pe.wait_ge(at_y, 3)
            for k in range(6):
                if k == 4:
                    pe.wait_ge(yg_ready, 1)
                down_half(2 * C_OUT1 + k, b1["yh1"][:, k, :], b1["yl1"][:, k, :], start=k == 0, ends_att=k == 0)
                if k == 0:
                    pe.wait_ge(pick_ready, 4)
                    pe.wait_ge(go_rstd, 1)
                    evacuated(pe, bank_use(10))
                    for h in range(4):
                        m = pe.matmul(ps[:, 2 - 2 * (h // 2), (h % 2) * S:(h % 2) * S + S], b1["g_pick"][:, h, :], b1["g_rstd"][:, :],
                                      start=h % 2 == 0, stop=True, skip_group_check=True)
                        if h % 2:
                            m.then_inc(go_spread, 1)
            pe.wait_ge(yg_ready, 2)
            down_last(2 * C_OUT1 + 6, b1["yh1"], b1["yl1"], 6, 1)
            ffn_up(0, C_UP[0], 1 * len(NEXT))
            ffn_down(0, C_DN[0], 2)
            ffn_up(1, C_UP[1], 2 * len(NEXT))
            ffn_down(1, C_DN[1], 4)
            first_two(C_IN2, 3 * len(NEXT))
            chunk(C_IN2 + 2)
            pe.wait_ge(lat_sq, 1)
            for j in range(3):
                m = pe.matmul(ps[:, 2, (j // 2) * S:(j // 2) * S + S], mean[:, 1 + j // 2, :], b2["latsq"][:, j, :],
                              start=j == 0, stop=j >= 1, skip_group_check=True)
            m.then_inc(lat_ss, 1)
            chunk(C_IN2 + 3)
            evacuated(pe, bank_use(C_IN2 + 1))
            pe.matmul(ps[:, 3, 0:S], table("perm32", P), b2["kpr"][:, :], start=True, stop=True).then_inc(pe_rot, 1)
            chunk(C_IN2 + 4)
            chunk(C_IN2 + 5)
            h = 2 * C_UQ
            pe.wait_ge(lat_ready2, 1)
            pe.wait_ge(lo_ready, h + 2)
            for j in range(5):
                u = bank_use(C_UQ) + j
                pe.wait_ge(bank_free[u % 2], u // 2)
                for f in range(2):
                    o = ps[:, u % 2, f * S:f * S + S]
                    if j < 3:
                        wc = slice((2 * j + f) * P, (2 * j + f) * P + P)
                        three(o, w_hi[:, slot(h), wc], w_lo[:, slot(h), wc], b2["cqh"][:, 0, :], b2["cql"][:, 0, :], f == 0, False)
                        m = three(o, w_hi[:, slot(h + 1), wc], w_lo[:, slot(h + 1), wc], b2["cqh"][:, 1, :], b2["cql"][:, 1, :], False, True)
                    else:
                        s_ = slot(h + j - 3)
                        wc = slice(768 + f * P, 768 + f * P + P)
                        m = three(o, w_hi[:, s_, wc], w_lo[:, s_, wc], b2["cqh"][:, 2, :], b2["cql"][:, 2, :], f == 0, True)
                m.then_inc(*((uq_full, 1) if j < 4 else (half_used, 2)))
            pe.wait_ge(lo_ready, h + 3)
            u = bank_use(C_UV)
            for j in range(2):
                pe.wait_ge(bank_free[(u + j) % 2], (u + j) // 2)
                a = slice(j * P, j * P + P)
                o = ps[:, (u + j) % 2, :]
                s_ = slot(h + 2)
                pe.matmul(o, b2["cqh"][:, 2, a], w_hi[:, s_, 0:512], start=True, stop=False)
                pe.matmul(o, b2["cql"][:, 2, a], w_hi[:, s_, 0:512], start=False, stop=False)
                m = pe.matmul(o, b2["cqh"][:, 2, a], w_lo[:, s_, 0:512], start=False, stop=True)
                m.then_inc(*((uq_full, 1) if j < 1 else (half_used, 2)))
            def mla_s(g):
                att_s(g, b2["qn"], b2["nz"], b2["qpe"], b2["kpz"])

            def ca_s(g):
                att_s(g, b2["caq"], b2["caz"])

            def s2(g):
                (mla_s if g < 8 else ca_s)(g)

            def o2(g):
                att_o(g, b2["pt2"], b2["v2"] if g < 8 else b2["cav"])

            chunk(C_CAV, tokens_out=True, halves=(0,))
            evacuated(pe, bank_use(C_UQ) + 2)
            pe.wait_ge(pe_done, 1)
            pe.matmul(ps[:, 3, :], table("perm32", P), b2["qpr"][:, :], start=True, stop=True).then_inc(pe_rot, 1)
            chunk(C_CAV, tokens_out=True, halves=(1,))
            chunk(C_CAV + 1, tokens_out=True, halves=(0,))
            pe.wait_ge(pe_done, 2)
            evacuated(pe, bank_use(C_UQ) + 3)
            evacuated(pe, bank_use(C_UQ) + 4)
            s2(4)
            chunk(C_CAV + 1, tokens_out=True, halves=(1,))
            for c in range(8):
                g = 4 + c
                chunk(C_GATE + c, halves=(0,))
                if g < 11:
                    s2(g + 1)
                att_t(g, b2["sm2"])
                chunk(C_GATE + c, halves=(1,))
                if c == 0:
                    evacuated(pe, bank_use(C_CAV))
                    evacuated(pe, bank_use(C_CAV + 1))
                o2(g)
            for n in range(4):
                br, c = n // 2, C_BR + n
                if n % 2 == 0:
                    pe.wait_ge(at_y, 8 + 4 * br)
                if n == 1:
                    evacuated(pe, bank_use(C_GATE + 6))
                    evacuated(pe, bank_use(C_GATE + 7))
                if n >= 2:
                    pe.wait_ge(br_used, 2 * (n - 1))
                for half in range(2):
                    h = 2 * c + half
                    pe.wait_ge(lo_ready, h + 1)
                    for k in range(2):
                        for f in range(4):
                            wc = slice(k * 512 + f * P, k * 512 + f * P + P)
                            kk = 4 * br + 2 * half + k
                            m = three(ps[:, 2 * ((n + 1) % 2) + f // 2, (f % 2) * S:(f % 2) * S + S], w_hi[:, slot(h), wc], w_lo[:, slot(h), wc],
                                      b2["yh2"][:, kk, :], b2["yl2"][:, kk, :], half == 0 and k == 0 and f % 2 == 0, half == 1 and k == 1)
                    m.then_inc(half_used, 1)
            for k in range(6):
                if k % 2 == 0:
                    pe.wait_ge(ml_ready, k // 2 + 1)
                down_half(2 * C_OUT2 + k, xh[:, k, :], xl[:, k, :], start=k == 0)
            pe.wait_ge(ml_ready, 4)
            down_last(2 * C_OUT2 + 6, xh, xl, 6, 5)
            ffn_up(2, C_UP[2], 4 * len(NEXT))
            ffn_down(2, C_DN[2], 6)

        @block.scalar
        def _(act):
            own = Own(act, own_act)
            f = nc.scalar.activation

            act.dma_start(cols[:, :], cols_in).then_inc(cols_landed, 16)
            act.dma_start(b1["w_glr"][:, :], glr_in).then_inc(aux_landed, 16)
            act.dma_start(b1["w_gup"][:, :], gup_in).then_inc(aux_landed, 16)
            act.dma_start(tab[:, :], tab_in).then_inc(tab_landed, 16)
            act.dma_start(b1["gmask"][:, :, :], gmask_in).then_inc(gmask_landed, 16)

            def hi(c, i=0, halves=(0, 1)):
                for half in halves:
                    h = 2 * c + half
                    act.wait_ge(raw_landed[slot(h)], (i + (h // NSLOT + 1)) * 16)
                    if not (isinstance(i, int) and h + 4 * i < NSLOT):
                        act.wait_ge(half_used, h - NSLOT + 1 + 4 * i)
                    f(w_hi[:, slot(h), :], raw[:, slot(h), :], ACT.Copy).then_inc(hi_ready, 1)

            def squares(resid):
                for j, k in enumerate(DONE):
                    if resid is None:
                        act.wait_ge(x_landed[k[0] // 2], 16)
                    else:
                        act.wait_ge(resid_done, resid * len(DONE) + j + 1)
                    f(tiles(xn, k), tiles(X, k), ACT.Square).then_inc(sq_done, 1)
                act.wait_ge(consts_ready, 1)
                f(epsc[:, 2:3], epsc[:, 0:1], ACT.Sqrt)

            def root(n):
                act.wait_ge(ss_done, n + 1)
                f(sd[:, 0, :], ps[:, 2, 0:S], ACT.Sqrt, bias=epsc[:, 0:1]).then_inc(sd_done, 1)

            def norm_hi(m):
                for j, k in enumerate(NEXT):
                    act.wait_ge(xt_ready, len(NEXT) * m + j + 1)
                    f(tiles(xh, k), tiles(xn, k), ACT.Copy).then_inc(xh_ready, 1)

            def norm_mod_hi(m, sub):
                act.wait_ge(mod_ready, 1 if sub == 0 else 2)
                for j, k in enumerate(NEXT):
                    act.wait_ge(xt_ready, len(NEXT) * m + j + 1)
                    if j > 1:
                        for kk in range(k[0], sum(k)):
                            ins = f(xn[:, kk, :], xn[:, kk, :], ACT.Identity, scale=modA[:, sub, kk:kk + 1], bias=mod[:, sub, kk:kk + 1])
                        own.mark(ins)
                        own.wait()
                    f(tiles(xh, k), tiles(xn, k), ACT.Copy).then_inc(xh_ready, 1)

            def full(c):
                act.wait_ge(half_used, 2 * c + 2 + (c in FIRST))
                return bank_use(c) % 2

            def bank2(b):
                return ps[:, b, :].rearrange("p (a n) -> p a n", a=2)

            def trig():
                act.wait_ge(trig_red, 2)
                f(sin2[:, :], sin2[:, :], ACT.Sin)
                f(cos2[:, :], cos2[:, :], ACT.Sin).then_inc(trig_done, 1)

            def att_exp(g, sm, st):
                act.wait_ge(at_m, g + 1)
                r = sm[:, g % 2, :]
                for j in range(4):
                    a = slice(j * P, j * P + P) if j < 2 else slice(256 + (j - 2) * S, 256 + (j - 2) * S + S)
                    ins = f(r[:, a], r[:, a], ACT.Exp, bias=st[:, g % 2, 0, j:j + 1], accum_out=st[:, g % 2, 1, j:j + 1])
                ins.then_inc(at_e, 1)

            def att_pt(g, pt):
                act.wait_ge(at_t, g + 1)
                f(pt[:, g % 2, 0:512], ps[:, 5 + 2 * (g % 2), :], ACT.Copy).then_inc(at_p0, 1)

            def att_yh(g, yh, k):
                act.wait_ge(at_o, g + 1)
                f(yh[:, k, :], ps[:, 4 + 2 * (g % 2), 256:512], ACT.Copy).then_inc(at_yh, 1)

            def padded(dst, k, b):
                f(dst[0:64, 0, k:k + 2, :], bank2(b)[0:64, :, :], ACT.Copy)
                return f(dst[64:P, 1, k:k + 2, :], bank2(b)[64:P, :, :], ACT.Copy)

            def level_e(l):
                act.wait_ge(lv_d, l + 1)
                own.mark(f(b1["E"][:, l % 2, :, :], b1["E"][:, l % 2, :, :], ACT.Abs))
                own.wait()
                f(b1["E"][:, l % 2, :, :], b1["E"][:, l % 2, :, :], ACT.Exp, scale=-1.0 / 16).then_inc(lv_e, 1)

            def up_step(conv, fi, c, j, i=0):
                u = bank_use(c)
                b = u % 2
                v = j % 2
                act.wait_ge(half_used, 2 * c + 2 + (c in FIRST) + 4 * i)
                n = FT * fi + j + 1 + 2 * i
                if conv:
                    if j >= 2:
                        act.wait_ge(act_ready, n - 2)
                    for t2 in range(2):
                        jj = j + FT * t2
                        wcol = cols[:, ds(i * 2 + (COL["conv_w"] + 2 * 44 + jj), 1)]
                        bcol = cols[:, ds(i * 2 + (COL["conv_b"] + jj), 1)]
                        ins = f(cv[:, v, t2, :], ps[:, b, t2 * S:t2 * S + S], ACT.Identity, scale=wcol, bias=bcol)
                    ins.then_inc(cv_base, 1)
                    hi(c + 2, i=i)
                    act.wait_ge(cv_gate, n)
                    f(sg[:, v, :], cv[:, v, 0, :], ACT.Silu).then_inc(sg_done, 1)
                else:
                    f(sg[:, v, :], ps[:, b, 0:S], ACT.Silu).then_inc(sg_done, 1)
                    hi(c + 2, i=i)

            def ada_sum(base, n, i=0):
                n = base + n
                act.wait_ge(ada_mult, i + (n + 1))
                if n >= 2:
                    act.wait_ge(ada_moved, i + (n - 1))
                f(ada_mul[:, n % 2, :], ada_mul[:, n % 2, :], ACT.Copy, accum_out=ada_col[:, n % 2:n % 2 + 1]).then_inc(ada_used, 1)

            def gain_means():
                own.mark(f(gsq[:, :], cols[:, COL["fin1_g"]:COL["fin1_g"] + KC], ACT.Square))
                own.wait()
                for k in range(KC):
                    ins = f(gmean[:, k, :], mean[:, 0, :], ACT.Copy, scale=gsq[:, k:k + 1])
                ins.then_inc(gmean_ready, 1)

            def ffn_up(fi, c0, ada=None):
                conv = fi == 0
                for j in range(2):
                    up_step(conv, fi, c0 + j, j)
                    if fi == 0 and j == 0:
                        gain_means()
                    if ada is not None:
                        ada_sum(ada, j)
                with act.Fori(0, FT // 2 - 1) as i:
                    for v in range(2):
                        up_step(conv, fi, c0 + 2 + v, 2 + v, i=i)
                        if ada is not None:
                            ada_sum(ada, 2 + v, i * 2)

            def ffn_down(c0, last=False, ada=None):
                if ada is not None:
                    ada_sum(ada, FT)
                with act.Fori(0, 2) as i:
                    for v in range(4):
                        hi(c0 + 2 + v, i=i * 2)
                        if ada is not None:
                            for k in ((0, 1), (2,), (3, 4), (5,))[v]:
                                ada_sum(ada, FT + 1 + k, i * 6)
                if ada:
                    trig()
                hi(c0 + 10)
                if ada is not None:
                    ada_sum(ada, FT + 13)
                if not last:
                    hi(c0 + 11)

            squares(None)
            hi(0, halves=(0,))
            root(0)
            hi(0, halves=(1,))
            norm_hi(0)
            hi(1)
            act.wait_ge(pool_zero, 1)
            act.wait_ge(glr_done, 1)
            f(b1["glr"][0:16, :], ps[0:16, 3, 0:S], ACT.Copy).then_inc(glr_sb, 1)
            hi(2)
            f(b1["gq"][:, :, :], bank2(full(0)), ACT.Copy, scale=0.125).then_inc(bank_free[0], 1)
            hi(3, halves=(0,))
            act.wait_ge(pool_zero, 2)
            padded(b1["gkz"], 0, full(1)).then_inc(bank_free[1], 1)
            hi(3, halves=(1,))
            act.wait_ge(cols_landed, 16)
            act.wait_ge(gup_done, 1)
            for ht in range(2):
                ins = f(b1["QL"][:, 0, ht, :], ps[:, 3, ht * S:ht * S + S], ACT.Identity, bias=col("b_gate", ht))
            ins.then_inc(z_done, 1)
            act.wait_ge(z_done, 1)
            own.mark(f(b1["KL"][:, 0, 0, :, :], b1["QL"][:, 0, :, :], ACT.Abs))
            own.wait()
            own.mark(f(b1["KL"][:, 0, 0, :, :], b1["KL"][:, 0, 0, :, :], ACT.Exp, scale=-1.0))
            own.wait()
            f(b1["KL"][:, 0, 1, :, :], b1["KL"][:, 0, 0, :, :], ACT.Ln, bias=1.0).then_inc(ls_done, 1)

            def qraw(c):
                b = full(c)
                if c >= 4:
                    act.wait_ge(rope_done, c - 3)
                f(b1["qraw"][:, c % 2, :], ps[:, b, :], ACT.Copy).then_inc(bank_free[b], 1)

            def vals(dst, c, cc):
                b = full(c)
                f(dst[:, :, cc * 256:cc * 256 + 256], bank2(b), ACT.Copy).then_inc(bank_free[b], 1)

            def gr_evac(c, cc):
                b = full(c)
                f(b1["gr"][:, 2 * cc:2 * cc + 2, :], bank2(b), ACT.Copy).then_inc(bank_free[b], 1)

            sm1, st1, pt1, yh1 = b1["sm1"], b1["st1"], b1["pt1"], b1["yh1"]
            for c in range(2, 6):
                qraw(c)
                hi(c + 2)
                level_e(c - 2)
            vals(b1["mv"], 6, 0)
            hi(8)
            level_e(4)
            vals(b1["mv"], 7, 1)
            level_e(5)
            att_exp(0, sm1, st1)
            for g in range(4):
                c = 8 + g
                hi(c + 1, halves=(0,))
                att_pt(g, pt1)
                hi(c + 1, halves=(1,))
                if g < 3:
                    att_exp(g + 1, sm1, st1)
                if g < 2:
                    level_e(6 + g)
                if g == 3:
                    for j in range(2):
                        act.wait_ge(go_full, j + 1)
                        f(b1["og"][:, 2 * j:2 * j + 2, :], bank2(2 + j), ACT.Copy)
                        f(b1["g_sd"][:, 2 * j:2 * j + 2, :], bank2(2 + j), ACT.Square).then_inc(go_sq, 1)
                    act.wait_ge(go_ss, 1)
                    f(b1["g_rstd"][:, :], ps[:, 2, 0:S], ACT.Sqrt, bias=epsc[:, 0:1]).then_inc(go_sd, 1)
                att_yh(g, yh1, g)
                if g == 3:
                    hi(C_OUT1 + 1, halves=(0,))
                if g < 2:
                    vals(b1["gv"], c, g)
                else:
                    gr_evac(c, g - 2)
            act.wait_ge(bank_free[1], 6)
            f(b1["gr"][:, :, :], b1["gr"][:, :, :], ACT.Silu).then_inc(gr_silu, 1)
            hi(C_OUT1 + 1, halves=(1,))
            for j in range(2):
                act.wait_ge(go_v, j + 1)
                f(b1["yh1"][:, 4 + 2 * j:6 + 2 * j, :], b1["og"][:, 2 * j:2 * j + 2, :], ACT.Copy).then_inc(yg_hi, 1)
            hi(C_OUT1 + 2)
            hi(C_OUT1 + 3)
            hi(C_OUT1 + 4)
            squares(0)
            root(1)
            hi(C_UP[0] + 1)
            norm_hi(1)
            act.wait_ge(c_landed, 16)
            f(cact[:, :], cact[:, :], ACT.Silu).then_inc(cact_ready, 1)
            ffn_up(0, C_UP[0], ada=0)
            ffn_down(C_DN[0], ada=0)
            squares(1)
            act.wait_ge(eps_mixed, 1)
            f(sd[:, 1, :], sd[:, 1, :], ACT.Sqrt, bias=epsc[:, 1:2]).then_inc(sd_done, 1)
            root(2)
            hi(C_UP[1] + 1)
            norm_mod_hi(2, 0)
            ffn_up(1, C_UP[1], ada=NADA // 2)
            ffn_down(C_DN[1], ada=NADA // 2)
            squares(2)
            root(4)
            hi(C_IN2 + 1)
            norm_mod_hi(3, 1)
            hi(C_IN2 + 2)
            b = full(C_IN2)
            f(b2["lat"][:, 0:2, :], bank2(b), ACT.Copy)
            f(b2["latsq"][:, 0:2, :], bank2(b), ACT.Square).then_inc(bank_free[b], 1)
            b = full(C_IN2 + 1)
            f(b2["lat"][:, 2, :], ps[:, b, 0:S], ACT.Copy)
            f(b2["latsq"][:, 2, :], ps[:, b, 0:S], ACT.Square).then_inc(lat_sq, 1)
            f(b2["kpr"][:, :], ps[:, b, S:2 * S], ACT.Copy).then_inc(bank_free[b], 1)
            hi(C_IN2 + 3)
            b = full(C_IN2 + 2)
            f(b2["caq"][:, 0:2, :], bank2(b), ACT.Copy).then_inc(bank_free[b], 1)
            hi(C_IN2 + 4)
            act.wait_ge(lat_ss, 1)
            f(b2["l_sd"][:, :, :], bank2(2), ACT.Sqrt, bias=epsc[:, 0:1]).then_inc(lat_sd, 1)
            b = full(C_IN2 + 3)
            f(b2["caq"][:, 2:4, :], bank2(b), ACT.Copy).then_inc(bank_free[b], 1)
            hi(C_IN2 + 5)
            act.wait_ge(lat_v, 1)
            f(b2["cqh"][:, :, :], b2["lat"][:, :, :], ACT.Copy).then_inc(lat_hi, 1)
            act.wait_ge(pool_zero, 8)
            b = full(C_IN2 + 4)
            padded(b2["caz"], 0, b).then_inc(bank_free[b], 1)
            hi(C_UQ)
            b = full(C_IN2 + 5)
            padded(b2["caz"], 2, b).then_inc(bank_free[b], 1)
            hi(C_UV, halves=(0,))
            u0 = bank_use(C_UQ)
            for j in (0, 2, 4):
                b = (u0 + j) % 2
                if j < 4:
                    act.wait_ge(uq_full, j + 1)
                else:
                    full(C_UQ)
                if j == 0:
                    f(b2["qn"][:, 0:2, :], bank2(b), ACT.Copy).then_inc(bank_free[b], 1)
                    hi(C_UV, halves=(1,))
                elif j == 2:
                    f(b2["qpr"][:, :], ps[:, b, :], ACT.Copy).then_inc(bank_free[b], 1)
                else:
                    padded(b2["nz"], 2, b).then_inc(bank_free[b], 1)
            u0 = bank_use(C_UV)
            for j in range(2):
                hi(C_CAV, halves=(j,))
                b = (u0 + j) % 2
                if j == 0:
                    act.wait_ge(uq_full, 5)
                else:
                    full(C_UV)
                f(b2["v2"][:, j, :], ps[:, b, :], ACT.Copy).then_inc(bank_free[b], 1)
            hi(C_CAV + 1)
            vals(b2["cav"], C_CAV, 0)
            hi(C_GATE)
            att_exp(4, b2["sm2"], b2["st2"])
            vals(b2["cav"], C_CAV + 1, 1)
            for c in range(8):
                g = 4 + c
                hi(C_GATE + c + 1, halves=(0,))
                att_pt(g, b2["pt2"])
                hi(C_GATE + c + 1, halves=(1,))
                if g < 11:
                    att_exp(g + 1, b2["sm2"], b2["st2"])
                att_yh(g, b2["yh2"], c)
                b = full(C_GATE + c)
                f(b2["th"][:, 2 * c:2 * c + 2, :], bank2(b), ACT.Tanh, scale=0.5).then_inc(bank_free[b], 1)
            for c in range(4):
                hi(C_BR + c + 1)
            for p in range(4):
                act.wait_ge(br_done, p + 1)
                f(pair(xh, p), pair(xn, p), ACT.Copy).then_inc(mh_ready, 1)
                if p == 1:
                    hi(C_OUT2 + 1)
            for c in range(1, 4):
                hi(C_OUT2 + c + 1)
            squares(3)
            root(5)
            hi(C_UP[2] + 1)
            norm_mod_hi(4, 2)
            ffn_up(2, C_UP[2])
            ffn_down(C_DN[2], last=True)
            squares(4)
            root(6)

        @block.vector
        def _(dve):
            own = Own(dve, own_dve)
            v = nc.vector

            def lo(c, i=0, halves=(0, 1)):
                for half in halves:
                    h = 2 * c + half
                    dve.wait_ge(hi_ready, h + 1 + 4 * i)
                    v.tensor_tensor(w_lo[:, slot(h), :], raw[:, slot(h), :], w_hi[:, slot(h), :].bitcast(F32), ALU.subtract).then_inc(lo_ready, 1)

            def rstd_of(n, k=0):
                dve.wait_ge(sd_done, n + 1)
                v.reciprocal(rstd[:, :], sd[:, k, :]).then_inc(rstd_done, 1)
                dve.wait_ge(rstd_done, n + 1)

            def norm_plain(n, m, gain, nxt):
                rstd_of(n)
                if n == 0:
                    dve.wait_ge(cols_landed, 16)
                for j, (k0, n_) in enumerate(NEXT):
                    for k in range(k0, k0 + n_):
                        ins = v.scalar_tensor_tensor(out=xn[:, k, :], in0=X[:, k, :], scalar=col(gain, k), in1=rstd[:, :], op0=ALU.mult, op1=ALU.mult)
                    ins.then_inc(xt_ready, 1)
                    if n + j == 0:
                        lo(0)
                    if j:
                        norm_lo(m, j - 1)
                lo(nxt, halves=(0,))
                norm_lo(m, len(NEXT) - 1)
                lo(nxt, halves=(1,))

            def norm_lo(m, j):
                dve.wait_ge(xh_ready, len(NEXT) * m + j + 1)
                k = NEXT[j]
                v.tensor_tensor(tiles(xl, k), tiles(xn, k), tiles(xh, k).bitcast(F32), ALU.subtract).then_inc(xl_ready, 1)

            def norm_in_place(n, gain):
                rstd_of(n)
                for p in range(4):
                    for k in (2 * p, 2 * p + 1):
                        ins = v.scalar_tensor_tensor(out=X[:, k, :], in0=X[:, k, :], scalar=col(gain, k), in1=rstd[:, :], op0=ALU.mult, op1=ALU.mult)
                    ins.then_inc(resid_done, 1)

            def norm_mod(n, m, sub, nxt, twice=False):
                if twice:
                    dve.wait_ge(ss_done, n + 2)
                    own.mark(v.tensor_scalar(sd[:, 1, :], ps[:, 2, 0:S], EPS, None, ALU.mult))
                    own.wait()
                    v.tensor_tensor(sd[:, 1, :], ps[:, 1, 0:S], sd[:, 1, :], ALU.add).then_inc(eps_mixed, 1)
                rstd_of(n, 1 if twice else 0)
                for k in range(2):
                    own.mark(v.tensor_tensor(xn[:, k, :], X[:, k, :], rstd[:, :], ALU.mult))
                    own.wait()
                    v.tensor_scalar(xn[:, k, :], xn[:, k, :], modA[:, sub, k:k + 1], mod[:, sub, k:k + 1], ALU.mult, ALU.add).then_inc(xt_ready, 1)
                norm_lo(m, 0)
                for j in range(2, len(NEXT)):
                    v.tensor_tensor(tiles(xn, NEXT[j]), tiles(X, NEXT[j]), over(rstd[:, :], 2), ALU.mult).then_inc(xt_ready, 1)
                    norm_lo(m, j - 1)
                lo(nxt, halves=(0,))
                norm_lo(m, len(NEXT) - 1)
                lo(nxt, halves=(1,))

            def fin1_residual(part):
                if part == 0:
                    rstd_of(3)
                for k in range(4 * part, 4 * part + 4):
                    v.scalar_tensor_tensor(out=X[:, k, :], in0=X[:, k, :], scalar=col("fin1_g", k), in1=rstd[:, :], op0=ALU.mult, op1=ALU.mult)

            def full(c):
                dve.wait_ge(half_used, 2 * c + 2)
                return bank_use(c) % 2

            def out_down(n, c0, gate=None, start=1):
                for c in range(start, 4):
                    lo(c0 + c)
                lo(c0 + 4)
                add_down(n, c0 + 4, gate)

            def add_down(n, c_end, gate):
                for j, (k0, n_) in enumerate(DONE):
                    if j < len(DONE) - 1:
                        dve.wait_ge(down_full, (len(DONE) - 1) * n + j + 1)
                    else:
                        dve.wait_ge(half_used, 2 * c_end)
                    for k in range(k0, k0 + n_):
                        src = down_out(k)
                        if gate is not None:
                            ins = v.scalar_tensor_tensor(out=X[:, k, :], in0=src, scalar=mod[:, gate, 16 + k:17 + k], in1=X[:, k, :],
                                                         op0=ALU.mult, op1=ALU.add)
                        elif n_ == 1:
                            ins = v.tensor_tensor(X[:, k, :], src, X[:, k, :], ALU.add)
                    if gate is None and n_ == 2:
                        ins = v.tensor_tensor(tiles(X, (k0, 2)), ps[:, 4 + k0 // 2, :].rearrange("p (a n) -> p a n", a=2), tiles(X, (k0, 2)), ALU.add)
                    ins.then_inc(resid_done, 1)

            def rope_trig(j):
                magic = 12582912.0
                c1, c2 = 6.28125, 0.0019340515136718750
                c3 = 2 * np.pi - c1 - c2
                dve.wait_ge(pos_landed, 16)
                dve.wait_ge(act_ready, FT * (j + 1))
                ang, kf = av[:, 0, :], av[:, 1, :]
                own.mark(v.tensor_copy(ang, posi[:, :]))
                own.wait()
                own.mark(v.tensor_scalar(ang, ang, col("freq"), None, ALU.mult))
                own.wait()
                own.mark(v.tensor_scalar(kf, ang, float(1 / (2 * np.pi)), (0.0, 0.25)[j], ALU.mult, ALU.add))
                own.wait()
                own.mark(v.tensor_scalar(kf, kf, magic, None, ALU.add))
                own.wait()
                own.mark(v.tensor_scalar(kf, kf, magic, None, ALU.subtract))
                own.wait()
                r = (sin2, cos2)[j][:, :]
                own.mark(v.scalar_tensor_tensor(out=r, in0=kf, scalar=-c1, in1=ang, op0=ALU.mult, op1=ALU.add))
                own.wait()
                own.mark(v.scalar_tensor_tensor(out=r, in0=kf, scalar=-c2, in1=r, op0=ALU.mult, op1=ALU.add))
                own.wait()
                own.mark(v.scalar_tensor_tensor(out=r, in0=kf, scalar=-float(c3), in1=r, op0=ALU.mult, op1=ALU.add))
                own.wait()
                if j:
                    own.mark(v.tensor_scalar(r, r, float(np.pi / 2), None, ALU.add))
                    own.wait()
                v.tensor_scalar(r, r, 3.1415925, -3.1415925, ALU.min, ALU.max).then_inc(trig_red, 1)

            def rope(c):
                evacuated(dve, c)
                rt = b1["rt"]
                if c == 2:
                    dve.wait_ge(tab_landed, 16)
                else:
                    dve.wait_ge(rope_done, c - 2)
                two = lambda ap: ap.rearrange("p (a n) -> p a n", a=2)
                v.tensor_tensor(two(rt[:, 0, :]), two(b1["qraw"][:, c % 2, :]), over(table("cos", S), 2), ALU.mult)
                dve.wait_ge(rot_done, c - 1)
                own.mark(v.tensor_tensor(two(rt[:, 1, :]), two(ps[:, 2 + c, :]), over(table("sin", S), 2), ALU.mult))
                own.wait()
                if c < 4:
                    v.tensor_tensor(b1["qT"][:, 2 * (c - 2):2 * (c - 1), :], two(rt[:, 0, :]), two(rt[:, 1, :]), ALU.add).then_inc(rope_done, 1)
                else:
                    dve.wait_ge(pool_zero, 3)
                    for par in range(2):
                        a = slice(64 * par, 64 * par + 64)
                        ins = v.tensor_tensor(b1["kz"][a, par, 2 * (c - 4):2 * (c - 3), :], two(rt[a, 0, :]), two(rt[a, 1, :]), ALU.add)
                    ins.then_inc(rope_done, 1)

            def att_mask(g, sm, st, scale, mask):
                a = 4 + 2 * (g % 2)
                r = sm[:, g % 2, :]
                s = st[:, g % 2, 0, :]
                dve.wait_ge(at_s, g + 1)
                s0 = r[:, 0:256].rearrange("p (a n) -> p a n", a=2)
                s1 = r[:, 256:768].rearrange("p (a n) -> p a n", a=2)
                v.scalar_tensor_tensor(out=s0, in0=ps[:, a, 0:256].rearrange("p (a n) -> p a n", a=2), scalar=scale, in1=mask(P, S),
                                       op0=ALU.mult, op1=ALU.add)
                own.mark(v.scalar_tensor_tensor(out=s1, in0=ps[:, a + 1, :].rearrange("p (a n) -> p a n", a=2), scalar=scale, in1=mask(0, S),
                                                op0=ALU.mult, op1=ALU.add))
                own.wait()
                v.tensor_reduce(s[:, 0:2], s0, AX.X, ALU.max, negate=True)
                v.tensor_reduce(s[:, 2:4], s1, AX.X, ALU.max, negate=True).then_inc(at_m, 1)

            def att_norm(g, sm, st):
                r = sm[:, g % 2, :]
                dve.wait_ge(at_e, g + 1)
                own.mark(v.reciprocal(st[:, g % 2, 2, :], st[:, g % 2, 1, :]))
                own.wait()
                for j in range(4):
                    a = slice(j * P, j * P + P) if j < 2 else slice(256 + (j - 2) * S, 256 + (j - 2) * S + S)
                    ins = v.tensor_scalar(r[:, a], r[:, a], st[:, g % 2, 2, j:j + 1], None, ALU.mult)
                ins.then_inc(at_n, 1)

            def att_pt(g, pt):
                dve.wait_ge(at_t, g + 1)
                v.tensor_copy(pt[:, g % 2, 512:768], ps[:, 4 + 2 * (g % 2), 0:256]).then_inc(at_p1, 1)

            def att_y(g, yh, yl, k):
                dve.wait_ge(at_yh, g + 1)
                v.tensor_tensor(yl[:, k, :], ps[:, 4 + 2 * (g % 2), 256:512], yh[:, k, :].bitcast(F32), ALU.subtract).then_inc(at_y, 1)

            causal = lambda a, b: over(table("causal", S)[:, a:b], 2)
            chunked = lambda a, b: over(table("chunked", S)[:, a:b], 2)

            def level_d(l):
                if l >= 2:
                    dve.wait_ge(lv_k, l - 1)
                    dve.wait_ge(lv_q, l - 1)
                p = 1 << l
                G = b1["G"][:, :, :].rearrange("p a (m q) -> p (a m) q", q=2 * p)
                E = b1["E"][:, l % 2, :, :].rearrange("p a (m q) -> p (a m) q", q=2 * p)
                ref = G[:, :, p - 1:p].to_broadcast([P, 2 * S // (2 * p), 2 * p])
                v.tensor_tensor(E, G, ref, ALU.subtract).then_inc(lv_d, 1)

            def level_q(l):
                dve.wait_ge(lv_e, l + 1)
                if l >= 2:
                    dve.wait_ge(lv_full, 2 * (l - 1))
                v.tensor_tensor(later(b1["QL"][:, l % 2, :, :], l), later(b1["gq"][:, :, :], l), later(b1["E"][:, l % 2, :, :], l),
                                ALU.mult).then_inc(lv_q, 1)

            def level_copy(l):
                if l == 0:
                    dve.wait_ge(pool_zero, 5)
                    dve.wait_ge(gmask_landed, 16)
                for i in range(1 if l == LEVELS else 2):
                    n = 2 * l + i if l <= LEVELS else 2 * LEVELS + 1 + i
                    dve.wait_ge(lv_full, n + 1)
                    if n >= 2:
                        dve.wait_ge(lv_copied, n - 1)
                    w = P // 2 if l < LEVELS else P
                    src = ps[:, 2 + i, 0:4 * w].rearrange("p (h n) -> p h n", h=4)
                    if l == LEVELS:
                        v.tensor_copy(b1["AT0"][:, :, P:S], src).then_inc(lv_copied, 1)
                    else:
                        dst = b1["AT0"][:, :, 0:P] if i == 0 else b1["AT1"][:, :, :]
                        mask = over(b1["gmask"][:, min(l, LEVELS), :], 4)
                        if l < LEVELS:
                            dst, mask = later(dst, l), later(mask, l)
                            src = src.rearrange("p h (m q) -> p h m q", q=1 << l)
                        v.copy_predicated(dst, mask, src).then_inc(lv_copied, 1)

            def up_step(conv, fi, c, j, i=0):
                u = bank_use(c)
                b = u % 2
                vv = j % 2
                n = FT * fi + j + 1 + 2 * i
                if conv:
                    dve.wait_ge(cv_base, n)
                    src = lambda t2, k: ps[:, b, t2 * S:t2 * S + S - k]
                    tap = lambda t2, k: cols[:, ds(i * 2 + (COL["conv_w"] + 44 * (2 - k) + j + FT * t2), 1)]
                    y = lambda t2, k: cv[:, vv, t2, k:S]
                    for t2 in range(2):
                        v.scalar_tensor_tensor(out=y(t2, 1), in0=src(t2, 1), scalar=tap(t2, 1), in1=y(t2, 1), op0=ALU.mult, op1=ALU.add).then_inc(cv_own, 1)
                    for t2 in range(2):
                        dve.wait_ge(cv_own, 3 * (j + 1) + 6 * i - 2 + t2)
                        ins = v.scalar_tensor_tensor(out=y(t2, 2), in0=src(t2, 2), scalar=tap(t2, 2), in1=y(t2, 2), op0=ALU.mult, op1=ALU.add)
                        ins.then_inc(cv_gate if t2 == 0 else bank_free[b], 1)
                    lo(c + 2, i=i, halves=(0,))
                    dve.wait_ge(bank_free[b], u // 2 + 1 + i)
                    dve.wait_ge(sg_done, n)
                    v.tensor_tensor(av[:, vv, :], sg[:, vv, :], cv[:, vv, 1, :], ALU.mult).then_inc(cv_own, 1)
                    lo(c + 2, i=i, halves=(1,))
                    dve.wait_ge(cv_own, 3 * (j + 1) + 6 * i)
                else:
                    dve.wait_ge(sg_done, n)
                    if j >= 2:
                        dve.wait_ge(act_ready, n - 2)
                    v.tensor_tensor(av[:, vv, :], sg[:, vv, :], ps[:, b, S:2 * S], ALU.mult).then_inc(bank_free[b], 1)
                    lo(c + 2, i=i)
                    dve.wait_ge(bank_free[b], u // 2 + 1 + i)
                ah = act_hi[:, ds(i * 2 + j, 1), :].rearrange("p a n -> p (a n)")
                al = act_lo[:, ds(i * 2 + j, 1), :].rearrange("p a n -> p (a n)")
                v.tensor_copy(ah, av[:, vv, :]).then_inc(ah_done, 1)
                dve.wait_ge(ah_done, n)
                v.tensor_tensor(al, av[:, vv, :], ah.bitcast(F32), ALU.subtract).then_inc(act_ready, 1)

            def ffn_up(fi, c0):
                conv = fi == 0
                for j in range(2):
                    up_step(conv, fi, c0 + j, j)
                with dve.Fori(0, FT // 2 - 1) as i:
                    for vv in range(2):
                        up_step(conv, fi, c0 + 2 + vv, 2 + vv, i=i)

            def ffn_down(n, c0, mod=None, gate=None, last=False, residual=None, trig=None):
                if residual:
                    residual(0)
                    residual(1)
                with dve.Fori(0, 4) as i:
                    for vv in range(2):
                        lo(c0 + 2 + vv, i=i)
                if trig is not None:
                    rope_trig(trig)
                lo(c0 + 10)
                if not last:
                    lo(c0 + 11)
                if mod:
                    ada_mod(*mod)
                add_down(n, c0 + 11, gate)

            def ada_mod(s0, n, gate_scale):
                m = mod[:, s0:s0 + n, :].rearrange("p a b -> p (a b)")
                dve.wait_ge(ada_moved, 24 if s0 == 0 else NADA)
                own.mark(v.tensor_tensor(m, m, cols[:, COL["b_ada"] + 24 * s0:COL["b_ada"] + 24 * (s0 + n)], ALU.add))
                own.wait()
                for s in range(s0, s0 + n):
                    g = COL[("f1_g", "mix_g", "f2_g")[s]]
                    own.mark(v.scalar_tensor_tensor(out=modA[:, s, :], in0=mod[:, s, 8:16], scalar=1.0, in1=cols[:, g:g + KC], op0=ALU.add, op1=ALU.mult))
                    if s == 0:
                        own.wait()
                        g = COL["fin1_g"]
                        v.tensor_tensor(modA[:, s, :], modA[:, s, :], cols[:, g:g + KC], ALU.mult)
                    ins = v.tensor_scalar(mod[:, s, 16:24], mod[:, s, 16:24], gate_scale, None, ALU.mult)
                ins.then_inc(mod_ready, 1)

            norm_plain(0, 0, "attn_g", 1)
            lo(2)
            lo(3)
            dve.wait_ge(ls_done, 1)
            own.mark(v.scalar_tensor_tensor(out=b1["E"][:, 0, :, :], in0=b1["QL"][:, 0, :, :], scalar=0.0, in1=b1["KL"][:, 0, 1, :, :],
                                            op0=ALU.min, op1=ALU.subtract))
            own.mark(v.memset(b1["E"][:, 1, 0, :], 1.0))
            own.wait()
            for ht in range(2):
                ins = v.tensor_tensor_scan(b1["G"][:, ht, :], b1["E"][:, 1, 0, :], b1["E"][:, 0, ht, :], 0.0, ALU.mult, ALU.add)
            own.mark(ins)
            own.wait()
            sm1, st1, pt1, yh1, yl1 = b1["sm1"], b1["st1"], b1["pt1"], b1["yh1"], b1["yl1"]
            level_d(0)
            level_d(1)
            lo(4)
            rope(2)
            lo(5)
            level_q(0)
            rope(3)
            level_q(1)
            level_d(2)
            lo(6)
            level_copy(0)
            rope(4)
            level_copy(1)
            level_q(2)
            level_d(3)
            lo(7)
            level_q(3)
            rope(5)
            level_d(4)
            level_copy(2)
            lo(8)
            level_q(4)
            level_d(5)
            level_copy(3)
            att_mask(0, sm1, st1, 0.125, causal)
            level_q(5)
            level_d(6)
            att_norm(0, sm1, st1)
            for g in range(4):
                c = 8 + g
                level_copy(4 + g if g < 3 else 8)
                lo(c + 1, halves=(0,))
                if g < 3:
                    att_mask(g + 1, sm1, st1, 0.125, causal)
                att_pt(g, pt1)
                if g == 2:
                    level_copy(7)
                lo(c + 1, halves=(1,))
                if g < 3:
                    att_norm(g + 1, sm1, st1)
                if g == 0:
                    level_d(7)
                if g < 2:
                    level_q(6 + g)
                if g == 3:
                    dve.wait_ge(go_sd, 1)
                    v.reciprocal(b1["g_rstd"][:, :], b1["g_rstd"][:, :]).then_inc(go_rstd, 1)
                att_y(g, yh1, yl1, g)
            def gla_lo(j):
                dve.wait_ge(yg_hi, j + 1)
                v.tensor_tensor(b1["yl1"][:, 4 + 2 * j:6 + 2 * j, :], b1["og"][:, 2 * j:2 * j + 2, :],
                                b1["yh1"][:, 4 + 2 * j:6 + 2 * j, :].bitcast(F32), ALU.subtract).then_inc(yg_ready, 1)

            lo(C_OUT1 + 1)
            for j in range(2):
                a = b1["og"][:, 2 * j:2 * j + 2, :]
                dve.wait_ge(go_spread, j + 1)
                for h in (2 * j, 2 * j + 1):
                    ins = v.scalar_tensor_tensor(out=b1["og"][:, h, :], in0=b1["og"][:, h, :], scalar=col("gla_g", h),
                                                 in1=ps[:, 2 - 2 * j, (h % 2) * S:(h % 2) * S + S], op0=ALU.mult, op1=ALU.mult)
                own.mark(ins)
                own.wait()
                dve.wait_ge(gr_silu, 1)
                v.tensor_tensor(a, a, b1["gr"][:, 2 * j:2 * j + 2, :], ALU.mult).then_inc(go_v, 1)
            gla_lo(0)
            gla_lo(1)
            out_down(0, C_OUT1, start=2)
            norm_plain(1, 1, "ffn_g", C_UP[0] + 1)
            ffn_up(0, C_UP[0])
            ffn_down(1, C_DN[0], mod=(0, 1, 0.5), trig=0)
            norm_mod(2, 2, 0, C_UP[1] + 1, twice=True)
            ffn_up(1, C_UP[1])
            ffn_down(2, C_DN[1], mod=(1, 2, 0.5), gate=0, residual=fin1_residual, trig=1)
            norm_mod(4, 3, 1, C_IN2 + 1)
            lo(C_IN2 + 2)
            lo(C_IN2 + 3)
            lo(C_IN2 + 4)
            lat, lsd = b2["lat"], b2["l_sd"]
            dve.wait_ge(lat_sd, 1)
            own.mark(v.reciprocal(lsd[:, :, :], lsd[:, :, :]))
            own.wait()
            for j in range(3):
                ins = v.scalar_tensor_tensor(out=lat[:, j, :], in0=lat[:, j, :], scalar=col("q_g", j) if j < 2 else col("kv_g"),
                                             in1=lsd[:, j // 2, :], op0=ALU.mult, op1=ALU.mult)
            ins.then_inc(lat_v, 1)
            lo(C_IN2 + 5)
            dve.wait_ge(lat_hi, 1)
            v.tensor_tensor(b2["cql"][:, :, :], lat[:, :, :], b2["cqh"][:, :, :].bitcast(F32), ALU.subtract).then_inc(lat_ready2, 1)
            dve.wait_ge(pe_rot, 1)
            dve.wait_ge(pool_zero, 8)
            dve.wait_ge(trig_done, 1)
            v.tensor_tensor(b2["rt2"][:, 0:S], b2["kpr"][:, :], cos2[:, :], ALU.mult)
            own.mark(v.tensor_tensor(b2["rt2"][:, S:2 * S], ps[:, 3, 0:S], sin2[:, :], ALU.mult))
            own.wait()
            for j in range(4):
                a = slice(32 * j, 32 * j + 32)
                ins = v.tensor_tensor(b2["kpz"][a, j, :], b2["rt2"][a, 0:S], b2["rt2"][a, S:2 * S], ALU.add)
            ins.then_inc(pe_done, 1)
            lo(C_UQ)
            lo(C_UV, halves=(0,))
            b = (bank_use(C_UQ) + 1) % 2
            dve.wait_ge(uq_full, 2)
            v.tensor_copy(b2["qn"][:, 2:4, :], ps[:, b, :].rearrange("p (a n) -> p a n", a=2)).then_inc(bank_free[b], 1)
            dve.wait_ge(uq_full, 4)
            for par in range(2):
                a = slice(64 * par, 64 * par + 64)
                ins = v.tensor_copy(b2["nz"][a, par, 0:2, :], ps[a, b, :].rearrange("p (a n) -> p a n", a=2))
            ins.then_inc(bank_free[b], 1)
            lo(C_UV, halves=(1,))
            lo(C_CAV)
            lo(C_CAV + 1)
            dve.wait_ge(pe_rot, 2)
            dve.wait_ge(pe_done, 1)
            two = lambda ap: ap.rearrange("p (a n) -> p a n", a=2)
            own.mark(v.tensor_tensor(two(b2["rt2"][:, :]), two(ps[:, 3, :]), over(sin2[:, :], 2), ALU.mult))
            own.mark(v.tensor_tensor(two(b2["qpr"][:, :]), two(b2["qpr"][:, :]), over(cos2[:, :], 2), ALU.mult))
            own.wait()
            v.tensor_tensor(b2["qpe"][:, :, :], two(b2["qpr"][:, :]), two(b2["rt2"][:, :]), ALU.add).then_inc(pe_done, 1)
            lo(C_CAV + 2)
            mla = 96.0 ** -0.5
            dve.wait_ge(bm_ready, 1)

            def mask2(g):
                if g < 8:
                    att_mask(g, b2["sm2"], b2["st2"], mla, chunked)
                else:
                    h = 2 * (g - 8)
                    att_mask(g, b2["sm2"], b2["st2"], 0.125, lambda a, b_: b2["bm"][:, h:h + 2, a:b_])

            mask2(4)
            att_norm(4, b2["sm2"], b2["st2"])
            for c in range(8):
                g = 4 + c
                lo(C_GATE + c + 1, halves=(0,))
                if g < 11:
                    mask2(g + 1)
                att_pt(g, b2["pt2"])
                lo(C_GATE + c + 1, halves=(1,))
                if g < 11:
                    att_norm(g + 1, b2["sm2"], b2["st2"])
                att_y(g, b2["yh2"], b2["yl2"], c)
            def merge_lo(p):
                dve.wait_ge(mh_ready, p + 1)
                v.tensor_tensor(pair(xl, p), pair(xn, p), pair(xh, p).bitcast(F32), ALU.subtract).then_inc(ml_ready, 1)

            for n in range(4):
                c, br, cc = C_BR + n, n // 2, n % 2
                lo(c + 1)
                dve.wait_ge(half_used, 2 * c + 2)
                for f2 in range(2):
                    k = 4 * cc + 2 * f2
                    th = b2["th"][:, 8 * br + k:8 * br + k + 2, :]
                    dst = xn[:, k:k + 2, :] if br == 0 else b2["caz"][:, cc, 2 * f2:2 * f2 + 2, :]
                    v.scalar_tensor_tensor(out=dst, in0=th, scalar=1.0, in1=two(ps[:, 2 * (1 - cc) + f2, :]), op0=ALU.add, op1=ALU.mult).then_inc(br_used, 1)
                    if br == 1:
                        dve.wait_ge(br_used, 2 * n + f2 + 1)
                        v.tensor_tensor(xn[:, k:k + 2, :], xn[:, k:k + 2, :], dst, ALU.add).then_inc(br_done, 1)
                if n == 2:
                    merge_lo(0)
                    merge_lo(1)
            merge_lo(2)
            merge_lo(3)
            out_down(3, C_OUT2, gate=1)
            norm_mod(5, 4, 2, C_UP[2] + 1)
            ffn_up(2, C_UP[2])
            ffn_down(4, C_DN[2], gate=2, last=True)
            norm_in_place(6, "fin2_g")



def _tiles(w, k0, kn, c):
    a = w[k0 * P:(k0 + kn) * P][:, c].reshape(kn, P, -1)
    return a.transpose(1, 0, 2).reshape(P, -1)


def _padded(a):
    out = np.zeros((P, HALF), a.dtype)
    out[:, :a.shape[1]] = a
    return out


def _weights(a):
    s = []
    r = np.arange

    def feature_chunk(w, c):
        s.extend([_tiles(w, 0, 4, c), _tiles(w, 4, 4, c)])

    def up(w, width):
        for j in range(FT):
            feature_chunk(w, np.concatenate([r(j * P, j * P + P), width + r(j * P, j * P + P)]))

    w = a["w_in"][0]
    for c0, n in ((1536, 256), (1792, 256), (0, 512), (512, 512), (1024, 512), (2048, 512), (2560, 512)):
        for c in range(c0, c0 + n, 256):
            feature_chunk(w, r(c, c + 256))
    s.extend(a["w_out"][0].reshape(KC, P, D))
    up(a["w_ffn_up"][0], DFF)
    s.extend(a["w_ffn_down"][0].reshape(FT, P, D))
    up(a["ffn1_w_in_2"][0], DFF)
    s.extend(a["ffn1_w_out_2"][0].reshape(FT, P, D))
    w = a["w_in_2"][0]
    feature_chunk(w, r(0, 256))
    feature_chunk(w, np.concatenate([r(256, 384)] + 4 * [r(384, 416)]))
    for c in range(416, 416 + 1024, 256):
        feature_chunk(w, r(c, c + 256))
    uq, ukv = a["mla_w_uq_2"][0], a["mla_w_ukv_2"][0]
    head = r(8)[:, None]
    q_cols = np.concatenate([(96 * head + r(64)).ravel(), (96 * head + 64 + r(32)).ravel()])
    k_cols, v_cols = (128 * head + r(64)).ravel(), (128 * head + 64 + r(64)).ravel()
    for j in range(2):
        s.append(np.concatenate([_tiles(uq, j, 1, q_cols), _tiles(ukv, 0, 1, k_cols[256 * j:256 * j + 256])], 1))
    s.append(_padded(_tiles(ukv, 0, 1, v_cols)))
    s.append(_padded(s[-1][:, :0]))
    for c in range(1440, 4000, 256):
        feature_chunk(w, r(c, c + 256))
    for w in (a["w_branch_a_2"][0], a["w_branch_b_2"][0]):
        for c in (0, 512):
            for k in (0, 2):
                s.append(_tiles(w, k, 2, r(c, c + 512)))
    s.extend(a["w_out_2"][0].reshape(KC, P, D))
    up(a["ffn2_w_in_2"][0], DFF)
    s.extend(a["ffn2_w_out_2"][0].reshape(FT, P, D))
    for c in FIRST:
        s[2 * c + 1], s[2 * c + 2] = s[2 * c + 2], s[2 * c + 1]
    return np.stack(s)


def _ada(w):
    return np.ascontiguousarray(w.T).reshape(NADA, P, D)


def _columns(a):
    col = lambda v: np.asarray(v).reshape(-1, P).T
    p = np.arange(P)
    freq = np.float32(10000.0) ** (-np.arange(0, 32, 2, dtype=np.float32) / np.float32(32))
    freq = np.where(p % 32 < 16, -freq[p % 16], freq[p % 16]).astype(np.float32)[:, None]
    c = [col(a["attn_norm_g"][0]), col(a["ffn_norm_g"][0]), col(a["final_norm_g"]), col(a["gla_norm_g"][0]), col(a["b_gate"][0]),
         col(a["conv_w"][0, 0]), col(a["conv_w"][0, 1]), col(a["conv_w"][0, 2]), col(a["conv_b"][0]),
         col(a["ffn1_norm_2"][0]), col(a["mix_norm_2"][0]), col(a["ffn2_norm_2"][0]), col(a["final_norm_2"]),
         col(a["mla_q_norm_2"][0]), col(a["mla_kv_norm_2"][0]), col(a["b_ada_2"][0]), freq]
    return np.ascontiguousarray(np.concatenate(c, 1))


def _constants():
    p, n = np.arange(P)[:, None], np.arange(S)[None, :]
    inv = np.float32(1.0) / (np.float32(10000.0) ** (np.arange(0, 64, 2, dtype=np.float32) / np.float32(64)))
    ang = n.astype(np.float32) * inv[p % 32]
    m = np.arange(P)[None, :]
    zero = np.zeros((P, P), np.float32)
    causal = np.where(m <= p, 0, NEG)
    chunked = np.where(m // 64 <= p // 64, 0, NEG)
    tab = [np.cos(ang), np.where(p % 64 < 32, -np.sin(ang), np.sin(ang)), p == (m ^ 32), p == (m ^ 16), zero, causal, zero, chunked]
    tab = np.concatenate([x.astype(np.float32) for x in tab], 1)
    levels = [(p // (2 * q) == m // (2 * q)) & (p % (2 * q) < q) & (m % (2 * q) >= q) for q in (1 << np.arange(LEVELS))]
    return tab, np.stack(levels + [p == m], 1).astype(np.int32)


def _bias(rel):
    i = 256 + np.arange(P)[:, None] + P - np.arange(S)[None, :]
    return np.ascontiguousarray(rel[0][i].transpose(0, 2, 1))


def kernel(**inputs):
    import concourse.bacc as bacc
    from concourse.bass_utils import run_bass_kernel_spmd as run

    a = {k: np.asarray(v) for k, v in inputs.items()}
    tab, gmask = _constants()
    w_in = a["w_in"][0]
    gup = np.zeros((P, S), w_in.dtype)
    gup[:16] = a["w_gate_up"][0]
    arrays = {
        "w": _weights(a), "ada_w": _ada(a["w_ada_2"][0]),
        "x_in": np.ascontiguousarray(a["x"][0].T.reshape(KC, P, S).transpose(1, 0, 2)),
        "cols_in": _columns(a), "tab_in": tab, "gmask_in": gmask,
        "glr_in": np.ascontiguousarray(_tiles(w_in, 0, KC, np.arange(3072, 3088))), "gup_in": gup,
        "c_in": a["c_2"].reshape(1, D), "bias_in": _bias(a["rel_bias_2"]), "pos_in": a["positions_2"].reshape(1, S).astype(np.int32),
    }
    nc = bacc.Bacc("TRN2", target_bir_lowering=False, num_devices=1)
    aps = {n: nc.dram_tensor(n, v.shape, mybir.dt.from_np(v.dtype), kind="ExternalInput").ap() for n, v in arrays.items()}
    out = nc.dram_tensor("out", (P, KC, S), mybir.dt.float32, kind="ExternalOutput").ap()
    build(nc, out=out, **aps)
    r = run(nc, [arrays], core_ids=[0])
    y = r.results[0]["out"]
    return y.transpose(1, 0, 2).reshape(D, S).T[None]
```
